# Optimizing a Trainium2 kernel written in Bass

```python
import math
import jax, jax.numpy as jnp
from jax import lax
import numpy as np

D_MODEL = 1024
BATCH = 1
SEQ = 512
DEPTH = 2

EPS = 1e-6
MLA_HEADS = 4
MLA_NOPE = 128
MLA_ROPE = 64
MLA_V = 128
MLA_Q_RANK = 384
MLA_KV_RANK = 256
MLA_ROPE_BASE = 10000.0
Q_BLOCK = 128
GLA_HEADS = 4
GLA_DK = 32
GLA_DV = 64
GLA_GATE_RANK = 16
GLA_GATE_NORM = 16.0
GLA_CHUNK = 64
RET_HEADS = 4
RET_DK = 32
RET_DV = 64
RET_CHUNK = 64
RET_ROPE_BASE = 10000.0
D_MIX = MLA_HEADS * MLA_V + GLA_HEADS * GLA_DV + RET_HEADS * RET_DV
IN_SIZES = (MLA_Q_RANK, MLA_KV_RANK, MLA_ROPE,
            GLA_HEADS * GLA_DK, GLA_HEADS * GLA_DK, GLA_HEADS * GLA_DV, GLA_GATE_RANK, GLA_HEADS * GLA_DV,
            RET_HEADS * RET_DK, RET_HEADS * RET_DK, RET_HEADS * RET_DV, RET_HEADS * RET_DV)
D_IN = sum(IN_SIZES)
D_FF = 2816
CONV_W = 3


def rmsnorm(x, gain):
    xf = x.astype(jnp.float32)
    y = xf * lax.rsqrt(jnp.mean(xf * xf, axis=-1, keepdims=True) + EPS)
    return (y * gain.astype(jnp.float32)).astype(x.dtype)

def head_rmsnorm(x, gain):
    H, d = x.shape[-2], x.shape[-1]
    return rmsnorm(x, gain.reshape(H, d))

def rope_tables(S, dim, base):
    inv = base ** (-(jnp.arange(0, dim, 2, dtype=jnp.float32) / dim))
    ang = jnp.arange(S, dtype=jnp.float32)[:, None] * inv[None, :]
    return jnp.cos(ang), jnp.sin(ang)

def apply_rope(x, cos, sin):
    half = x.shape[-1] // 2
    c = cos[None, :, None, :].astype(x.dtype)
    s = sin[None, :, None, :].astype(x.dtype)
    x1, x2 = x[..., :half], x[..., half:]
    return jnp.concatenate([x1 * c - x2 * s, x2 * c + x1 * s], axis=-1)

def mla_attention(q_nope, q_rope, k_nope, k_rope, v):
    B, S, H, dn = q_nope.shape
    dr = q_rope.shape[-1]
    nb = S // Q_BLOCK
    scale = (MLA_NOPE + MLA_ROPE) ** -0.5
    qn = q_nope.reshape(B, nb, Q_BLOCK, H, dn).transpose(1, 0, 2, 3, 4)
    qr = q_rope.reshape(B, nb, Q_BLOCK, H, dr).transpose(1, 0, 2, 3, 4)
    key_pos = jnp.arange(S)

    def one_block(args):
        qn_b, qr_b, start = args
        s = (jnp.einsum('bqhd,bkhd->bhqk', qn_b, k_nope)
             + jnp.einsum('bqhd,bkd->bhqk', qr_b, k_rope)).astype(jnp.float32) * scale
        q_pos = start + jnp.arange(Q_BLOCK)
        mask = key_pos[None, :] <= q_pos[:, None]
        s = jnp.where(mask[None, None], s, jnp.finfo(jnp.float32).min)
        p = jax.nn.softmax(s, axis=-1).astype(v.dtype)
        return jnp.einsum('bhqk,bkhd->bqhd', p, v)

    out = lax.map(one_block, (qn, qr, jnp.arange(nb) * Q_BLOCK))
    return out.transpose(1, 0, 2, 3, 4).reshape(B, S, H, v.shape[-1])

def mla_branch(c_q, c_kv, k_rope, q_norm, w_uq, kv_norm, w_ukv, cos, sin):
    B, S, _ = c_q.shape
    q = (rmsnorm(c_q, q_norm) @ w_uq).reshape(B, S, MLA_HEADS, MLA_NOPE + MLA_ROPE)
    q_nope, q_rope = q[..., :MLA_NOPE], apply_rope(q[..., MLA_NOPE:], cos, sin)
    kv = (rmsnorm(c_kv, kv_norm) @ w_ukv).reshape(B, S, MLA_HEADS, MLA_NOPE + MLA_V)
    k_nope, v = kv[..., :MLA_NOPE], kv[..., MLA_NOPE:]
    k_r = apply_rope(k_rope[:, :, None, :], cos, sin)[:, :, 0, :]
    return mla_attention(q_nope, q_rope, k_nope, k_r, v)

def gla_chunked(q, k, v, log_a):
    B, S, H, dk = q.shape
    dv = v.shape[-1]
    C = GLA_CHUNK
    n = S // C
    to_chunks = lambda t: t.astype(jnp.float32).reshape(B, n, C, H, t.shape[-1]).transpose(1, 0, 3, 2, 4)
    qc, kc, vc, gc = to_chunks(q), to_chunks(k), to_chunks(v), to_chunks(log_a)
    tril = jnp.tril(jnp.ones((C, C), dtype=bool))

    def step(state, inp):
        qb, kb, vb, gb = inp
        b = jnp.cumsum(gb, axis=-2)
        inter = jnp.einsum('bhik,bhkv->bhiv', qb * jnp.exp(b), state)
        diff = b[..., :, None, :] - b[..., None, :, :]
        dec = jnp.where(tril[:, :, None], jnp.exp(jnp.where(tril[:, :, None], diff, 0.0)), 0.0)
        A = jnp.einsum('bhik,bhjk,bhijk->bhij', qb, kb, dec)
        intra = jnp.einsum('bhij,bhjv->bhiv', A, vb)
        b_end = b[..., -1:, :]
        new_state = state * jnp.exp(b_end)[..., 0, :, None] + jnp.einsum(
            'bhjk,bhjv->bhkv', kb * jnp.exp(b_end - b), vb)
        return new_state, inter + intra

    state0 = jnp.zeros((B, H, dk, dv), jnp.float32)
    _, out = lax.scan(step, state0, (qc, kc, vc, gc))
    return out.transpose(1, 0, 3, 2, 4).reshape(B, S, H, dv).astype(v.dtype)

def gla_branch(q, k, v, gate_lr, g, w_gate, b_gate, out_norm):
    B, S, _ = q.shape
    qh = q.reshape(B, S, GLA_HEADS, GLA_DK) * (GLA_DK ** -0.5)
    kh = k.reshape(B, S, GLA_HEADS, GLA_DK)
    vh = v.reshape(B, S, GLA_HEADS, GLA_DV)
    gk = (gate_lr @ w_gate + b_gate).astype(jnp.float32)
    log_a = (jax.nn.log_sigmoid(gk) / GLA_GATE_NORM).reshape(B, S, GLA_HEADS, GLA_DK)
    o = gla_chunked(qh, kh, vh, log_a)
    o = head_rmsnorm(o, out_norm).reshape(B, S, GLA_HEADS * GLA_DV)
    return o * jax.nn.silu(g)

def retention_chunked(q, k, v):
    B, S, H, dk = q.shape
    dv = v.shape[-1]
    C = RET_CHUNK
    n = S // C
    to_chunks = lambda t: t.astype(jnp.float32).reshape(B, n, C, H, t.shape[-1]).transpose(0, 3, 1, 2, 4)
    qc, kc, vc = to_chunks(q), to_chunks(k), to_chunks(v)
    log_g = jnp.log(1.0 - 2.0 ** (-5.0 - jnp.arange(H, dtype=jnp.float32)))
    idx = jnp.arange(C, dtype=jnp.float32)
    diff = idx[:, None] - idx[None, :]
    D = jnp.where(diff >= 0, jnp.exp(log_g[:, None, None] * jnp.maximum(diff, 0.0)), 0.0)
    scores = jnp.einsum('bhnid,bhnjd->bhnij', qc, kc) * D[None, :, None]
    intra = jnp.einsum('bhnij,bhnjv->bhniv', scores, vc)
    k_dec = kc * jnp.exp(log_g[:, None] * (C - 1 - idx)[None, :])[None, :, None, :, None]
    U = jnp.einsum('bhnjd,bhnjv->nbhdv', k_dec, vc)
    chunk_decay = jnp.exp(log_g * C)[None, :, None, None]

    def step(R, u):
        return R * chunk_decay + u, R

    _, R_prev = lax.scan(step, jnp.zeros((B, H, dk, dv), jnp.float32), U)
    q_dec = qc * jnp.exp(log_g[:, None] * (idx + 1.0)[None, :])[None, :, None, :, None]
    inter = jnp.einsum('bhnid,nbhdv->bhniv', q_dec, R_prev)
    out = (intra + inter).transpose(0, 2, 3, 1, 4).reshape(B, S, H, dv)
    return out.astype(v.dtype)

def retention_branch(q, k, v, g, out_norm, cos, sin):
    B, S, _ = q.shape
    qh = apply_rope(q.reshape(B, S, RET_HEADS, RET_DK), cos, sin)
    kh = apply_rope(k.reshape(B, S, RET_HEADS, RET_DK), cos, sin) * (RET_DK ** -0.5)
    vh = v.reshape(B, S, RET_HEADS, RET_DV)
    o = retention_chunked(qh, kh, vh)
    o = head_rmsnorm(o, out_norm).reshape(B, S, RET_HEADS * RET_DV)
    return o * jax.nn.silu(g)

def causal_dwconv(a, w, b):
    S = a.shape[1]
    p = jnp.pad(a, ((0, 0), (CONV_W - 1, 0), (0, 0)))
    out = b
    for kk in range(CONV_W):
        out = out + p[:, kk:kk + S] * w[kk]
    return out

def first_inputs(seed: int = 0) -> dict:
    key = jax.random.key(seed)
    ks = jax.random.split(key, 19)
    f32 = jnp.float32
    nrm = lambda k, shape, scale: jax.random.normal(k, shape, f32) * scale
    gain = lambda k, shape: 1.0 + 0.02 * jax.random.normal(k, shape, f32)
    return {
        "x": nrm(ks[0], (BATCH, SEQ, D_MODEL), 1.0),
        "attn_norm": gain(ks[1], (DEPTH, D_MODEL)),
        "w_in": nrm(ks[2], (DEPTH, D_MODEL, D_IN), D_MODEL ** -0.5),
        "mla_q_norm": gain(ks[3], (DEPTH, MLA_Q_RANK)),
        "mla_w_uq": nrm(ks[4], (DEPTH, MLA_Q_RANK, MLA_HEADS * (MLA_NOPE + MLA_ROPE)), MLA_Q_RANK ** -0.5),
        "mla_kv_norm": gain(ks[5], (DEPTH, MLA_KV_RANK)),
        "mla_w_ukv": nrm(ks[6], (DEPTH, MLA_KV_RANK, MLA_HEADS * (MLA_NOPE + MLA_V)), MLA_KV_RANK ** -0.5),
        "mla_out_norm": gain(ks[7], (DEPTH, MLA_HEADS * MLA_V)),
        "gla_w_gate": nrm(ks[8], (DEPTH, GLA_GATE_RANK, GLA_HEADS * GLA_DK), GLA_GATE_RANK ** -0.5),
        "gla_b_gate": nrm(ks[9], (DEPTH, GLA_HEADS * GLA_DK), 0.02),
        "gla_out_norm": gain(ks[10], (DEPTH, GLA_HEADS * GLA_DV)),
        "ret_out_norm": gain(ks[11], (DEPTH, RET_HEADS * RET_DV)),
        "w_out": nrm(ks[12], (DEPTH, D_MIX, D_MODEL), D_MIX ** -0.5),
        "ffn_norm": gain(ks[13], (DEPTH, D_MODEL)),
        "ffn_w_up": nrm(ks[14], (DEPTH, D_MODEL, 2 * D_FF), D_MODEL ** -0.5),
        "ffn_conv_w": nrm(ks[15], (DEPTH, CONV_W, D_FF), CONV_W ** -0.5),
        "ffn_conv_b": nrm(ks[16], (DEPTH, D_FF), 0.02),
        "ffn_w_down": nrm(ks[17], (DEPTH, D_FF, D_MODEL), D_FF ** -0.5),
        "final_norm": gain(ks[18], (D_MODEL,)),
    }

def first_block(x, attn_norm, w_in, mla_q_norm, mla_w_uq, mla_kv_norm, mla_w_ukv, mla_out_norm,
              gla_w_gate, gla_b_gate, gla_out_norm, ret_out_norm, w_out, ffn_norm, ffn_w_up,
              ffn_conv_w, ffn_conv_b, ffn_w_down, final_norm):
    B, S, _ = x.shape
    mla_cos, mla_sin = rope_tables(S, MLA_ROPE, MLA_ROPE_BASE)
    ret_cos, ret_sin = rope_tables(S, RET_DK, RET_ROPE_BASE)
    split_points = []
    acc = 0
    for sz in IN_SIZES[:-1]:
        acc += sz
        split_points.append(acc)

    for l in range(DEPTH):
        h = rmsnorm(x, attn_norm[l])
        z = h @ w_in[l]
        (c_q, c_kv, k_rope, g_q, g_k, g_v, g_lr, g_g, r_q, r_k, r_v, r_g) = jnp.split(z, split_points, axis=-1)
        y_a = mla_branch(c_q, c_kv, k_rope, mla_q_norm[l], mla_w_uq[l], mla_kv_norm[l], mla_w_ukv[l],
                         mla_cos, mla_sin)
        y_a = head_rmsnorm(y_a, mla_out_norm[l]).reshape(B, S, MLA_HEADS * MLA_V)
        y_b = gla_branch(g_q, g_k, g_v, g_lr, g_g, gla_w_gate[l], gla_b_gate[l], gla_out_norm[l])
        y_c = retention_branch(r_q, r_k, r_v, r_g, ret_out_norm[l], ret_cos, ret_sin)
        x = x + jnp.concatenate([y_a, y_b, y_c], axis=-1) @ w_out[l]
        h = rmsnorm(x, ffn_norm[l])
        u = h @ ffn_w_up[l]
        a, bv = u[..., :D_FF], u[..., D_FF:]
        a = causal_dwconv(a, ffn_conv_w[l], ffn_conv_b[l])
        x = x + (jax.nn.silu(a) * bv) @ ffn_w_down[l]

    return rmsnorm(x, final_norm)


DEPTH_2 = 1

HEAD_DIM = 64
BRANCH_WIDTH = D_MODEL // 2
A_GROUPS = ((128, 1), (512, 4), (2048, 16))
A_HEADS = BRANCH_WIDTH // HEAD_DIM
B_HEADS = BRANCH_WIDTH // HEAD_DIM
B_KV_HEADS = B_HEADS // 4
M_HEADS = 4
M_HEAD_DIM = BRANCH_WIDTH // M_HEADS
N_MEM = 256
GRID_W = 64
ROPE_THETA = 10000.0
NORM_EPS = 1e-6
NEG_INF = -1e30
N_BRANCHES = 3

A_QKV = 3 * len(A_GROUPS) * A_HEADS * HEAD_DIM
B_Q = B_HEADS * HEAD_DIM
B_KV = B_KV_HEADS * HEAD_DIM
M_Q = M_HEADS * M_HEAD_DIM
SPLIT_SIZES = (A_QKV, B_Q, B_KV, B_KV, M_Q, BRANCH_WIDTH, BRANCH_WIDTH, BRANCH_WIDTH, N_BRANCHES * D_MODEL)
IN_WIDTH = A_QKV + B_Q + 2 * B_KV + M_Q + 3 * BRANCH_WIDTH + N_BRANCHES * D_MODEL


def rms_norm(x, g):
    xf = x.astype(jnp.float32)
    y = xf * lax.rsqrt(jnp.mean(xf * xf, axis=-1, keepdims=True) + NORM_EPS)
    return (y * g.astype(jnp.float32)).astype(x.dtype)

def rope(x, pos):
    dr = x.shape[-1]
    half = dr // 2
    inv = jnp.power(ROPE_THETA, -jnp.arange(half, dtype=jnp.float32) * 2.0 / dr)
    ang = pos.astype(jnp.float32)[:, None] * inv[None, :]
    cos = jnp.cos(ang)[:, None, :]
    sin = jnp.sin(ang)[:, None, :]
    xf = x.astype(jnp.float32)
    x1, x2 = xf[..., :half], xf[..., half:]
    return jnp.concatenate([x1 * cos - x2 * sin, x1 * sin + x2 * cos], axis=-1).astype(x.dtype)

def axial_rope(x, row_pos, col_pos):
    half = x.shape[-1] // 2
    return jnp.concatenate([rope(x[..., :half], row_pos), rope(x[..., half:], col_pos)], axis=-1)

def dilated_window_attention(q, k, v, window, dilation):
    b, s, h, dh = q.shape
    half = window // (2 * dilation)
    blk = half
    L = s // dilation
    nb = -(-L // blk)
    lp = nb * blk
    z = b * dilation

    def regroup(t):
        return t.reshape(b, L, dilation, h, dh).transpose(0, 2, 1, 3, 4).reshape(z, L, h, dh)

    qg, kg, vg = regroup(q), regroup(k), regroup(v)
    qb = jnp.pad(qg, ((0, 0), (0, lp - L), (0, 0), (0, 0))).reshape(z, nb, blk, h, dh)

    def band(t):
        tp = jnp.pad(t, ((0, 0), (blk, lp - L + blk), (0, 0), (0, 0))).reshape(z, nb + 2, blk, h, dh)
        return jnp.concatenate([tp[:, :-2], tp[:, 1:-1], tp[:, 2:]], axis=2)

    kw, vw = band(kg), band(vg)
    qpos = jnp.arange(nb)[:, None] * blk + jnp.arange(blk)[None, :]
    kpos = (jnp.arange(nb)[:, None] - 1) * blk + jnp.arange(3 * blk)[None, :]
    valid = ((jnp.abs(qpos[:, :, None] - kpos[:, None, :]) <= half)
             & (kpos[:, None, :] >= 0) & (kpos[:, None, :] < L))
    sc = jnp.einsum('znqhd,znkhd->znhqk', qb, kw).astype(jnp.float32) * (dh ** -0.5)
    sc = jnp.where(valid[None, :, None], sc, NEG_INF)
    m = jnp.max(sc, axis=-1, keepdims=True)
    p = jnp.exp(sc - m)
    l = jnp.sum(p, axis=-1, keepdims=True)
    o = jnp.einsum('znhqk,znkhd->znqhd', (p / l).astype(v.dtype), vw)
    lse = (m + jnp.log(l))[..., 0]
    o = o.reshape(b, dilation, lp, h, dh)[:, :, :L].transpose(0, 2, 1, 3, 4).reshape(b, s, h, dh)
    lse = lse.transpose(0, 1, 3, 2).reshape(b, dilation, lp, h)[:, :, :L]
    lse = lse.transpose(0, 2, 1, 3).reshape(b, s, h)
    return o, lse

def second_inputs(seed: int = 0) -> dict:
    key = jax.random.key(seed)
    ks = jax.random.split(key, 16)
    nrm = jax.random.normal
    f32 = jnp.float32
    return {
        'x': nrm(ks[0], (BATCH, SEQ, D_MODEL), f32),
        'mem': nrm(ks[1], (BATCH, N_MEM, D_MODEL), f32),
        'g_pre': 1.0 + 0.05 * nrm(ks[2], (DEPTH_2, D_MODEL), f32),
        'w_in': nrm(ks[3], (DEPTH_2, D_MODEL, IN_WIDTH), f32) * D_MODEL ** -0.5,
        'b_merge': 0.1 * nrm(ks[4], (DEPTH_2, N_BRANCHES * D_MODEL), f32),
        'q_norm': 1.0 + 0.05 * nrm(ks[5], (DEPTH_2, HEAD_DIM), f32),
        'k_norm': 1.0 + 0.05 * nrm(ks[6], (DEPTH_2, HEAD_DIM), f32),
        'g_mem': 1.0 + 0.05 * nrm(ks[7], (DEPTH_2, D_MODEL), f32),
        'w_mem_kv': nrm(ks[8], (DEPTH_2, D_MODEL, 2 * M_Q), f32) * D_MODEL ** -0.5,
        'w_br_a': nrm(ks[9], (DEPTH_2, BRANCH_WIDTH, D_MODEL), f32) * BRANCH_WIDTH ** -0.5,
        'w_br_b': nrm(ks[10], (DEPTH_2, BRANCH_WIDTH, D_MODEL), f32) * BRANCH_WIDTH ** -0.5,
        'w_br_m': nrm(ks[11], (DEPTH_2, BRANCH_WIDTH, D_MODEL), f32) * BRANCH_WIDTH ** -0.5,
        'w_out': nrm(ks[12], (DEPTH_2, D_MODEL, D_MODEL), f32) * D_MODEL ** -0.5,
        'g_post': 1.0 + 0.05 * nrm(ks[13], (DEPTH_2, D_MODEL), f32),
    }

def second_block(x, mem, g_pre, w_in, b_merge, q_norm, k_norm, g_mem, w_mem_kv, w_br_a, w_br_b, w_br_m, w_out, g_post):
    b, s, d = x.shape
    dt = x.dtype
    pos = jnp.arange(s, dtype=jnp.float32)
    rows = s // GRID_W
    row_pos = jnp.repeat(jnp.arange(rows, dtype=jnp.float32), GRID_W)
    col_pos = (jnp.arange(s) % GRID_W).astype(jnp.float32)
    split_at = np.cumsum(SPLIT_SIZES)[:-1].tolist()
    n_groups = len(A_GROUPS)
    kv_rep = B_HEADS // B_KV_HEADS
    n_q_blocks = s // Q_BLOCK

    for layer in range(DEPTH_2):
        h = rms_norm(x, g_pre[layer])
        a_qkv, bq, bk, bv, mq, ga, gb, gm, mg = jnp.split(h @ w_in[layer], split_at, axis=-1)

        a_qkv = a_qkv.reshape(b, s, 3, n_groups * A_HEADS, HEAD_DIM)
        aq = rope(a_qkv[:, :, 0], pos)
        ak = rope(a_qkv[:, :, 1], pos)
        av = a_qkv[:, :, 2]
        outs, lses = [], []
        for gi, (window, dil) in enumerate(A_GROUPS):
            hs = slice(gi * A_HEADS, (gi + 1) * A_HEADS)
            o_g, lse_g = dilated_window_attention(aq[:, :, hs], ak[:, :, hs], av[:, :, hs], window, dil)
            outs.append(o_g)
            lses.append(lse_g)
        wts = jax.nn.softmax(jnp.stack(lses, axis=0), axis=0).astype(dt)
        oa = jnp.einsum('gbsh,gbshd->bshd', wts, jnp.stack(outs, axis=0)).reshape(b, s, BRANCH_WIDTH)

        qb_ = axial_rope(rms_norm(bq.reshape(b, s, B_HEADS, HEAD_DIM), q_norm[layer]), row_pos, col_pos)
        kb_ = axial_rope(rms_norm(bk.reshape(b, s, B_KV_HEADS, HEAD_DIM), k_norm[layer]), row_pos, col_pos)
        vb_ = bv.reshape(b, s, B_KV_HEADS, HEAD_DIM)
        q_blocks = qb_.reshape(b, n_q_blocks, Q_BLOCK, B_KV_HEADS, kv_rep, HEAD_DIM).transpose(1, 0, 2, 3, 4, 5)

        def attend(qc, kb_=kb_, vb_=vb_):
            sc = jnp.einsum('bqkgd,bskd->bkgqs', qc, kb_).astype(jnp.float32) * (HEAD_DIM ** -0.5)
            p = jax.nn.softmax(sc, axis=-1).astype(vb_.dtype)
            return jnp.einsum('bkgqs,bskd->bqkgd', p, vb_)

        ob = lax.map(attend, q_blocks).transpose(1, 0, 2, 3, 4, 5).reshape(b, s, B_Q)

        kvm = rms_norm(mem, g_mem[layer]) @ w_mem_kv[layer]
        n_mem = mem.shape[1]
        km = kvm[..., :M_Q].reshape(b, n_mem, M_HEADS, M_HEAD_DIM)
        vm = kvm[..., M_Q:].reshape(b, n_mem, M_HEADS, M_HEAD_DIM)
        sm = jnp.einsum('bshd,bnhd->bhsn', mq.reshape(b, s, M_HEADS, M_HEAD_DIM), km).astype(jnp.float32)
        pm = jax.nn.softmax(sm * (M_HEAD_DIM ** -0.5), axis=-1).astype(dt)
        om = jnp.einsum('bhsn,bnhd->bshd', pm, vm).reshape(b, s, M_Q)

        ya = (oa * jax.nn.silu(ga)) @ w_br_a[layer]
        yb = (ob * jax.nn.silu(gb)) @ w_br_b[layer]
        ym = (om * jax.nn.silu(gm)) @ w_br_m[layer]
        gates = jax.nn.sigmoid((mg + b_merge[layer]).astype(jnp.float32)).astype(dt).reshape(b, s, N_BRANCHES, d)
        merged = gates[:, :, 0] * ya + gates[:, :, 1] * yb + gates[:, :, 2] * ym
        out = merged @ w_out[layer]
        x = x + rms_norm(out, g_post[layer])
    return x


def setup_inputs(seed=0):
    out = dict(first_inputs(seed))
    for name, value in second_inputs(seed + 1).items():
        if name != "x":
            out[name + "_2"] = value
    return out


def reference(
    x, attn_norm, w_in, mla_q_norm, mla_w_uq, mla_kv_norm, mla_w_ukv, mla_out_norm, gla_w_gate,
    gla_b_gate, gla_out_norm, ret_out_norm, w_out, ffn_norm, ffn_w_up, ffn_conv_w, ffn_conv_b,
    ffn_w_down, final_norm, mem_2, g_pre_2, w_in_2, b_merge_2, q_norm_2, k_norm_2, g_mem_2,
    w_mem_kv_2, w_br_a_2, w_br_b_2, w_br_m_2, w_out_2, g_post_2,
):
    x = first_block(
        x, attn_norm, w_in, mla_q_norm, mla_w_uq, mla_kv_norm, mla_w_ukv, mla_out_norm,
        gla_w_gate, gla_b_gate, gla_out_norm, ret_out_norm, w_out, ffn_norm, ffn_w_up,
        ffn_conv_w, ffn_conv_b, ffn_w_down, final_norm,
    )
    return second_block(
        x, mem_2, g_pre_2, w_in_2, b_merge_2, q_norm_2, k_norm_2, g_mem_2, w_mem_kv_2, w_br_a_2,
        w_br_b_2, w_br_m_2, w_out_2, g_post_2,
    )


_drawn_inputs = setup_inputs


def setup_inputs(seed=0):
    import zlib

    import numpy as np

    out = dict(_drawn_inputs(seed))
    spreads = {}
    factors = {'mla_q_norm': 3.836,
     'gla_b_gate': 8.0,
     'gla_out_norm': 7.28,
     'ret_out_norm': 7.267,
     'ffn_norm': 2.8,
     'ffn_conv_b': 3.773,
     'q_norm_2': 8.0,
     'k_norm_2': 8.0,
     'g_mem_2': 4.842}
    for name, (base, spread) in spreads.items():
        noise = np.random.default_rng([zlib.crc32(name.encode()), seed]).standard_normal(out[name].shape)
        drawn = base * np.exp(spread * noise) if base else spread * noise
        out[name] = __import__('jax').numpy.asarray(drawn.astype(out[name].dtype))
    for name, factor in factors.items():
        out[name] = (out[name] * factor).astype(out[name].dtype)
    return out
```

```python
import math
from collections import defaultdict
from contextlib import ExitStack

import numpy as np
import concourse.bass as bass
from concourse import mybir

F32 = mybir.dt.float32
F32R = mybir.dt.float32r
BF16 = mybir.dt.bfloat16
U8 = mybir.dt.uint8
ALU = mybir.AluOpType
ACT = mybir.ActivationFunctionType
AX = mybir.AxisListType

P = 128
S = 512
NT = S // P
D = 1024
KD = D // P
DEPTH = 2
EPS = 1e-6
Q_RANK, KV_RANK, ROPE = 384, 256, 64
HEADS, NOPE, VDIM = 4, 128, 128
LIN_DK, LIN_DV = 32, 64
GATE_RANK, GATE_NORM = 16, 16.0
FF = 2816
KF = FF // P
CQ, CKV, KR, GQ, GK, GV, GLR, GG, RQ, RK, RV, RG, Z_END = np.cumsum(
    [0, 384, 256, 64, 128, 128, 256, 16, 256, 128, 128, 256, 256]).tolist()
RES = 4
HD = 64
A_GROUPS, A_HEADS = 3, 8
B_HEADS, B_KV = 8, 2
M_HEADS, N_MEM = 4, 256
AQ, AK, AV, BQ, BK, BV, MQ, GA, GB, GM, MG, IN2 = np.cumsum(
    [0, 1536, 1536, 1536, 512, 128, 128, 512, 512, 512, 512, 3072]).tolist()

CH_Z, CH_UQ, CH_UKV, CH_OUT, CH_UP, CH_DOWN = 9, 3, 4, 4, KF, 12
C_UQ = CH_Z
C_UKV = C_UQ + CH_UQ
C_OUT = C_UKV + CH_UKV
C_UP = C_OUT + CH_OUT
C_DOWN = C_UP + CH_UP
CH_LAYER = C_DOWN + CH_DOWN
DOWN_K = (8, 8, 6)
T_UP, T_DOWN = 2 * C_UP, 2 * C_DOWN
TILES_LAYER = T_DOWN + 8

G_ATTN, G_Q, G_KV, G_FFN, G_CONVW, G_CONVB, G_GATE, G_OUT, G_N = np.cumsum(
    [0, 8, 3, 2, 8, 3 * KF, KF, 1, 8]).tolist()

LEVELS = (64, 32, 16, 8, 4, 2, 1)
CREDIT = {"w_split": 2, "tile_done": 1, "x_down": 1}


def constants():
    f = np.float32
    eye = np.eye(P, dtype=f)
    idx = np.arange(P)

    def swap(n):
        m = np.zeros((P, P), f)
        m[idx, (idx // n) * n + (idx + n // 2) % n] = 1
        return m

    dup, dup_swap = np.zeros((P, P), f), np.zeros((P, P), f)
    dup[:64, :64] = dup[:64, 64:] = np.eye(64)
    dup_swap[:64, :64] = dup_swap[:64, 64:] = swap(64)[:64, :64]
    sel = [np.zeros((P, P), f) for _ in range(2)]
    for j in range(2):
        sel[j][64 * j:64 * j + 64] = np.concatenate([np.eye(64), np.eye(64)], 1)
    block64 = (idx[:, None] // 64 == idx[None] // 64).astype(f)
    causal = np.where(idx[None] <= idx[:, None], 0, -1e30).astype(f)
    head = idx // LIN_DK
    block = (head[:, None] == (np.arange(256) // LIN_DV)[None]).astype(f)
    log_g = np.log(1.0 - 2.0 ** (-5.0 - np.arange(4, dtype=np.float64)))
    ks = LIN_DK ** -0.5
    dif = idx[None] - idx[:, None]
    dt = np.where(dif[:, None] >= 0, np.exp(log_g[None, :, None] * np.maximum(dif, 0)[:, None]), 0) * ks
    qdec = np.exp(log_g[head][:, None] * (idx + 1.0)[None])
    kdec = np.exp(log_g[head][:, None] * (P - 1.0 - idx)[None]) * ks
    cdec = np.exp(log_g[head] * P)[:, None]

    def table(freq, pos, half):
        ang = (pos.astype(f) * freq.astype(f)[:, None]).astype(f)
        sign = np.where(idx % (2 * half) < half, -1, 1).astype(f)[:, None]
        return np.cos(ang), np.sin(ang) * sign

    t = np.arange(S)
    base = f(10000.0)
    inv64 = base ** (-(np.arange(0, 64, 2, dtype=f) / f(64)))
    inv32 = base ** (-(np.arange(0, 32, 2, dtype=f) / f(32)))
    mc, ms = table(inv64[idx % 32], np.tile(t, (P, 1)), 32)
    rc, rs = table(inv32[idx % 16], np.tile(t, (P, 1)), 16)
    perm = (np.arange(S) % P) * RES + np.arange(S) // P
    pos = np.where((idx % 64 < 32)[:, None], perm[None] // 64, perm[None] % 64)
    ac, as_ = table(inv32[idx % 16], pos, 16)
    a_rope = np.stack([mc[:, perm], ms[:, perm]], 1).astype(f)
    main = np.concatenate([eye, swap(64), swap(32), dup, dup_swap, causal, block, dt.reshape(P, -1), qdec, kdec,
                           cdec], 1).astype(f)
    rope = np.stack([mc, ms, rc, rs], 1).astype(f)
    late = np.concatenate([sel[0], sel[1], block64, ac, as_], 1).astype(f)
    lev = [((idx[:, None] // (2 * s)) == (idx[None] // (2 * s))) & (idx[:, None] % (2 * s) < s) & (idx[None] % (2 * s) >= s)
           for s in LEVELS] + [eye > 0]
    levels = np.stack(lev, 1).astype(f)
    win = np.zeros((P, RES, 768), f)
    for r in range(RES):
        for c in range(RES):
            win[:, r, c * P:c * P + P] = np.abs(RES * (idx[:, None] - idx[None]) + r - c) <= 64
        win[:, r, 512:640] = np.abs(idx[:, None] - idx[None]) <= 64
        win[:, r, 640:768] = (idx[:, None] % 4) == (idx[None] % 4)
    win = np.where(win > 0, 0, -1e30).astype(f)
    return dict(c_main=main, c_rope=rope, c_late=late, c_levels=levels, c_win=win, c_arope=a_rope)


def build(nc, A, out, PER):
    ctx = ExitStack()
    sems = {}

    def sem(name):
        if name not in sems:
            sems[name] = ctx.enter_context(nc.semaphore(name))
        return sems[name]

    with ctx:
        def sb(name, shape, dt=F32):
            return ctx.enter_context(nc.sbuf_tensor(name, shape, dt))

        x_t = sb("x_t", [P, KD, S])
        h_hi, h_lo = sb("h_hi", [P, KD, S], F32R), sb("h_lo", [P, KD, S], F32R)
        w_raw = sb("w_raw", [P, 2, 2048])
        w_hi, w_lo = sb("w_hi", [P, 2, 2048], F32R), sb("w_lo", [P, 2, 2048], F32R)
        NMAIN = 6 * P + 256 + 512 + 2 * P + 1
        cm = sb("cm", [P, NMAIN])
        ident, swap64, swap32, dup, dup_swap, causal = (cm[:, i * P:(i + 1) * P] for i in range(6))
        o = 6 * P
        block_mask, o = cm[:, o:o + 256], o + 256
        ret_d, o = cm[:, o:o + 512].rearrange("p (h i) -> p h i", h=4), o + 512
        ret_q, ret_k, ret_c = cm[:, o:o + P], cm[:, o + P:o + 2 * P], cm[:, o + 2 * P:o + 2 * P + 1]
        levels = sb("levels", [P, 8, P], U8)
        ones = sb("ones", [P, P])
        eps = sb("eps", [P, 1])
        gains = sb("gains", [P, DEPTH, G_N])
        g = sb("g", [P, G_N])
        wg_all = sb("wg_all", [P, DEPTH, P])
        wg = sb("wg", [P, P])
        g2 = sb("g2", [P, 8 * 4 + 24 + 2])
        stats = sb("stats", [P, 160])
        rms_a = sb("rms_a", [P, S])
        spare = sb("spare", [P, 8])

        ARENA = (nc.sbuf_base + 63) // 64 * 64
        room = nc.sbuf_usable_end - ARENA

        def at(name, kib, shape, dt=F32):
            n = int(np.prod(shape[1:])) * (4 if dt in (F32, F32R) else 2)
            assert kib * 1024 + n <= room, (name, kib, n, room)
            return nc.alloc_sbuf_tensor_at(name, shape, dt, offset=ARENA + int(kib * 1024))

        levels_in = at("levels_in", 0, [P, 8, P])
        sq = at("sq", 0, [P, KD, S])
        tm = at("tm", 0, [P, NT, 1024])
        cq = at("cq", 16, [P, 5, S])
        y_mla = at("y_mla", 16, [P, NT, S])
        kg = at("kg", 26, [P, S])
        lin = at("lin", 28, [P, 4, S])
        tab = at("tab", 36, [P, 4, S])
        tmp = at("tmp", 44, [P, 3, S])
        rms_b = at("rms_b", 50, [P, S])
        qn = at("qn", 52, [P, HEADS, S])
        sq2 = at("sq2", 52, [P, 5, S])
        kn = at("kn", 60, [P, HEADS, S])
        v_mla = at("v_mla", 68, [P, NT, S])
        qr = at("qr", 76, [P, 2, S])
        kr = at("kr", 80, [P, S])
        prob = at("prob", 82, [P, 2, 768])
        prob_t = at("prob_t", 88, [P, 2, 768])
        amat = at("amat", 52, [P, 4, NT, P])
        um = at("um", 60, [P, NT, 256])
        sig = at("sig", 64, [P, NT, 256])
        o_sb = at("o_sb", 68, [P, NT, 256])
        kd_t = at("kd_t", 72, [P, NT, P])
        gl = at("gl", 76, [P, 7, S])
        x_in = at("x_in", 52, [P, NT, D])
        hid_hi, hid_lo = at("hid_hi", 0, [P, KF, S], F32R), at("hid_lo", 44, [P, KF, S], F32R)
        a_pad = at("a_pad", 88, [P, 2, S + 2])
        b_sb = at("b_sb", 92.25, [P, 2, S])
        conv = rms_a
        gt_hi, gt_lo = at("gt_hi", 0, [P, 4, S], F32R), at("gt_lo", 8, [P, 4, S], F32R)
        mem_hi, mem_lo = at("mem_hi", 0, [P, KD, N_MEM], F32R), at("mem_lo", 8, [P, KD, N_MEM], F32R)
        sq_2 = at("sq_2", 0, [P, KD, S])
        av = at("av", 16, [P, NT, 1536])
        merged = at("merged", 16, [P, KD, S])
        late = at("late", 32, [P, 3 * P + 2 * S])
        win_in = at("win_in", 0, [P, RES, 768])
        win = at("win", 40, [P, RES, 768], BF16)
        sgate = at("sgate", 40, [P, 4, S])
        qk = at("qk", 48, [P, 2, 6, S])
        q_b = at("q_b", 48, [P, 5, S])
        k_b = at("k_b", 58, [P, 2, S])
        v_b = at("v_b", 62, [P, NT, P])
        q_m = at("q_m", 48, [P, 4, S])
        mem_in = at("mem_in", 56, [P, 2, D])
        km = at("km", 56, [P, M_HEADS, N_MEM])
        vm = at("vm", 60, [P, 2, S])
        mem_t = at("mem_t", 64, [P, KD, N_MEM])
        out_t = at("out_t", 48, [P, KD, S])
        o_br = at("o_br", 72, [P, NT, S])
        prob2, prob2_t = at("prob2", 80, [P, 2, 768]), at("prob2_t", 86, [P, 2, 768])
        out_sb = at("out_sb", 72, [P, 2, D])
        tmp2 = at("tmp2", 92, [P, S])
        a_sin, a_cos = at("a_sin", 46, [P, S]), at("a_cos", 94, [P, S])

        ps = ctx.enter_context(nc.psum_tensor("ps", [P, 8, 512], F32))
        MAIN, STAT_BANK = 4, 7

        layer = {}
        count = defaultdict(int)
        total = {}

        def upto(eng, name, k=None):
            k = count[name] if k is None else k
            return layer[eng] * PER.get(name, 0) + CREDIT.get(name, 0) + k

        def tick(name, by=1):
            count[name] += by
            return by

        def end_layer(names):
            for n in list(count):
                total.setdefault(n, count.pop(n))
            count.clear()

        def wsrc(name, l, c0, n, k0=0, k=None):
            a = A[name]
            k = a.shape[1] // P if k is None else k
            return a[bass.ds(l, 1), k0 * P:(k0 + k) * P, c0:c0 + n].rearrange("a (k p) n -> p (a k) n", p=P)

        def layer_chunks(l):
            out = []
            z = lambda *parts: out.append((KD, [(c, wsrc("w_in", l, c0, n)) for c, c0, n in parts]))
            z((0, CQ, P), (P, CQ + P, P))
            z((0, CQ + 2 * P, P), (P, CQ + 3 * P, P))
            z((0, CKV + 128, 128), (128, KR, 64), (192, GLR, GATE_RANK))
            for c0 in (GQ, RQ, GV, GG, RV, RG):
                z((0, c0, 256))
            q = NOPE + ROPE
            for h in (0, 2):
                out.append((3, [(i * P, wsrc("mla_w_uq", l, (h + i) * q, P)) for i in range(2)]))
            out.append((3, [(h * ROPE, wsrc("mla_w_uq", l, h * q + NOPE, ROPE)) for h in range(4)]))
            for off in (0, NOPE):
                for h in (0, 2):
                    out.append((2, [(i * P, wsrc("mla_w_ukv", l, (h + i) * 256 + off, P)) for i in range(2)]))
            for m in range(4):
                out.append((KD, [(0, wsrc("w_out", l, m * 256, 256))]))
            assert len(out) == C_UP
            return out

        n_dma = [2, 2, 3] + [1] * 6 + [2, 2, 4] + [2] * 4 + [1] * 4 + [2] * (KF + CH_DOWN)

        def two(name, c0, n=256, k0=0, k=None):
            return (k or A[name].shape[1] // P, [(0, wsrc(name, 0, c0, n, k0, k))])

        def second_chunks():
            out = [(KD, [(i * P, wsrc("w_in_2", 0, AV + c0 + i * P, P)) for i in range(2)]) for c0 in (0, 256)]
            out += [two("w_in_2", AV + i * 256) for i in range(2, 6)]
            for hp in range(4):
                for gi in range(A_GROUPS):
                    c0 = (gi * A_HEADS + 2 * hp) * HD
                    out.append((KD, [(0, wsrc("w_in_2", 0, AQ + c0, P)), (P, wsrc("w_in_2", 0, AK + c0, P))]))
            def branch(gate, br, b):
                out.extend(two("w_in_2", gate + i * 256) for i in range(2))
                for m in range(4):
                    out.append(two(br, m * 256))
                    out.append(two("w_in_2", MG + b * D + m * 256))
            branch(GA, "w_br_a_2", 0)
            out.extend(two("w_in_2", BQ + i * 256) for i in range(3))
            branch(GB, "w_br_b_2", 1)
            out.extend(two("w_mem_kv_2", i * 256) for i in range(4))
            out.extend(two("w_in_2", MQ + i * 256) for i in range(2))
            branch(GM, "w_br_m_2", 2)
            out.extend(two("w_out_2", i * 256) for i in range(4))
            return out

        second = second_chunks()
        C2_QK = 6
        C2_GA = C2_QK + 12
        C2_BQ = C2_GA + 10
        C2_GB = C2_BQ + 3
        C2_KV = C2_GB + 10
        C2_MQ = C2_KV + 4
        C2_GM = C2_MQ + 2
        C2_OUT = C2_GM + 10
        assert len(second) == C2_OUT + 4

        def slot_view(buf, slot, K):
            return buf[:, slot, 0:K * 256].rearrange("p (k n) -> p k n", n=256)

        att_base = defaultdict(int)

        class Inst:

            def __init__(self, width, score, mask, pv, o_col, o_width):
                self.width, self.score, self.mask, self.pv = width, score, mask, pv
                self.o_col, self.o_width = o_col, o_width

        def mla_groups():
            groups = []
            for t in range(NT):
                insts = []
                for h in range(HEADS):
                    L, lo = (t + 1) * P, 64 * (h % 2)
                    q0 = t * P
                    score = [(0, L, qn[:, h, q0:q0 + P], kn[:, h, 0:L], True, False),
                             (0, L, qr[lo:lo + 64, h // 2, q0:q0 + P], kr[lo:lo + 64, 0:L], False, True)]
                    insts.append(Inst(L, score, (q0, causal), [v_mla[:, k, h * P:h * P + P] for k in range(t + 1)],
                                      h * VDIM, VDIM))
                groups.append((insts, y_mla[:, t, :].rearrange("p (h d) -> p h d", h=HEADS)))
            return groups

        def a_groups(hp):
            groups = []
            buf = qk[:, hp % 2]
            for hh in range(2):
                lo, head = 64 * hh, 2 * hp + hh
                insts = []
                for r in range(RES):
                    q = [buf[lo:lo + 64, 2 * gi, r * P:r * P + P] for gi in range(3)]
                    k = [buf[lo:lo + 64, 2 * gi + 1, :] for gi in range(3)]
                    score = [(0, S, q[0], k[0], True, True),
                             (512, P, q[1], k[1][:, r * P:r * P + P], True, True),
                             (640, P, q[2], k[2][:, r * P:r * P + P], True, True)]
                    vcol = lambda gi: slice((gi * A_HEADS + head) * HD, (gi * A_HEADS + head + 1) * HD)
                    pv = [av[:, c, vcol(0)] for c in range(RES)] + [av[:, r, vcol(1)], av[:, r, vcol(2)]]
                    insts.append(Inst(768, score, (0, win[:, r, :]), pv, HD * r, HD))
                groups.append((insts, o_br[:, :, head * HD:head * HD + HD]))
            return groups

        def b_groups():
            groups = []
            for r in range(RES):
                insts = []
                for h in range(B_HEADS):
                    lo, j = 64 * (h % 2), h // (B_HEADS // B_KV)
                    score = [(0, S, q_b[lo:lo + 64, h // 2, r * P:r * P + P], k_b[lo:lo + 64, j, :], True, True)]
                    insts.append(Inst(S, score, None, [v_b[:, c, j * HD:j * HD + HD] for c in range(RES)], h * HD, HD))
                groups.append((insts, o_br[:, r, :].rearrange("p (h d) -> p h d", h=B_HEADS)))
            return groups

        def m_groups():
            groups = []
            for r in range(RES):
                insts = []
                for h in range(M_HEADS):
                    score = [(0, N_MEM, q_m[:, h, r * P:r * P + P], km[:, h, :], True, True)]
                    insts.append(Inst(N_MEM, score, None, [vm[:, c, h * P:h * P + P] for c in range(2)], h * P, P))
                groups.append((insts, o_br[:, r, :].rearrange("p (h d) -> p h d", h=M_HEADS)))
            return groups

        S_BANK, T_BANK, O_BANK = (4, 6), 2, 1

        def score_ps(i, c0, n):
            b = S_BANK[i % 2] + c0 // 512
            c = c0 % 512
            return ps[:, b, c:c + n]

        def wide_ps(bank, n):
            return ps[:, bank:bank + 2, :].rearrange("p b n -> p (b n)")[:, 0:n]

        def att_pe(pe, groups, probs, probs_t):
            base, obase = att_base["pe"], att_base["pe_o"]
            insts = [i for g_, _ in groups for i in g_]
            size = len(groups[0][0])

            def scores(i):
                for c0, n, lhs, rhs, a, b in insts[i].score:
                    ins = pe.matmul(score_ps(i, c0, n), lhs, rhs, start=a, stop=b)
                ins.then_inc(sem("score"), tick("score"))

            def turn(i):
                pe.wait_ge(sem("p_exp"), upto(pe, "p_exp", base + i + 1))
                if base + i:
                    pe.wait_ge(sem("pt_copied"), upto(pe, "pt_copied", base + i))
                for k in range(len(insts[i].pv)):
                    c = k * P
                    ins = pe.transpose(ps[:, T_BANK + c // 512, c % 512:c % 512 + P],
                                       probs[:, i % 2, c:c + P], ident)
                ins.then_inc(sem("pt_done"), tick("pt_done"))

            def values(i):
                pe.wait_ge(sem("pt_copied"), upto(pe, "pt_copied", base + i + 1))
                if i % size == 0 and obase + i // size:
                    pe.wait_ge(sem("o_norm"), upto(pe, "o_norm", obase + i // size))
                it = insts[i]

                for k, v in enumerate(it.pv):
                    ins = pe.matmul(ps[:, O_BANK, it.o_col:it.o_col + it.o_width], probs_t[:, i % 2, k * P:k * P + P], v,
                                    start=(k == 0), stop=(k == len(it.pv) - 1))
                ins.then_inc(sem("pv"), tick("pv"))

            n = len(insts)
            scores(0)
            for i in range(n):
                if i + 1 < n:
                    scores(i + 1)
                turn(i)
                if i:
                    values(i - 1)
            values(n - 1)
            att_base["pe"] += n
            att_base["pe_o"] += len(groups)

        def att_act(act, groups, pr, pt):
            base = att_base["act"]
            insts = [i for g_, _ in groups for i in g_]

            def copy(i):
                n = len(insts[i].pv) * P
                act.wait_ge(sem("pt_done"), upto(act, "pt_done", base + i + 1))
                act.activation(pt[:, i % 2, 0:n], wide_ps(T_BANK, n), ACT.Copy).then_inc(sem("pt_copied"), tick("pt_copied"))
                act.wait_ge(sem("pt_copied"), upto(act, "pt_copied"))

            for i, it in enumerate(insts):
                act.wait_ge(sem("nmax"), upto(act, "nmax", base + i + 1))
                c = i % 16
                act.activation(pr[:, i % 2, 0:it.width], wide_ps(S_BANK[i % 2], it.width), ACT.Exp,
                                         bias=stats[:, c:c + 1], accum_out=stats[:, 16 + c:17 + c]).then_inc(sem("p_exp"), tick("p_exp"))
                act.wait_ge(sem("p_exp"), upto(act, "p_exp"))
                if i:
                    copy(i - 1)
            copy(len(insts) - 1)
            att_base["act"] += len(insts)

        def att_dve(dve, groups):
            base = att_base["dve"]
            insts = [i for g_, _ in groups for i in g_]
            size = len(groups[0][0])

            def norm(q):
                dve.wait_ge(sem("pv"), upto(dve, "pv", base + (q + 1) * size))
                c = 16 + (q * size) % 16
                r = stats[:, 32:32 + size]
                dve.reciprocal(r, stats[:, c:c + size]).then_inc(sem("rinv"), tick("rinv"))
                dve.wait_ge(sem("rinv"), upto(dve, "rinv"))
                it = groups[q][0][0]
                src = ps[:, O_BANK, it.o_col:it.o_col + size * it.o_width].rearrange("p (h d) -> p h d", h=size)
                dve.tensor_tensor(groups[q][1], src, r.unsqueeze(2).to_broadcast([P, size, it.o_width]),
                                            ALU.mult).then_inc(sem("o_norm"), tick("o_norm"))
                dve.wait_ge(sem("o_norm"), upto(dve, "o_norm"))

            for i, it in enumerate(insts):
                dve.wait_ge(sem("score"), upto(dve, "score", base + i + 1))
                if it.mask is not None:
                    c0, table = it.mask
                    n = table.shape[-1]
                    part = wide_ps(S_BANK[i % 2], 1024)[:, c0:c0 + n]
                    dve.tensor_tensor(part, part, table, ALU.add).then_inc(sem("masked"), tick("masked"))
                    dve.wait_ge(sem("masked"), upto(dve, "masked"))
                c = i % 16
                dve.tensor_reduce(stats[:, c:c + 1], wide_ps(S_BANK[i % 2], it.width), AX.X, ALU.max,
                                            negate=True).then_inc(sem("nmax"), tick("nmax"))
                dve.wait_ge(sem("nmax"), upto(dve, "nmax"))
                if i % size == 0 and i:
                    norm(i // size - 1)
            norm(len(groups) - 1)
            att_base["dve"] += len(insts)

        def norm_sq(act, tiles, buf):
            for k, t in enumerate(tiles):
                act.activation(buf[:, k], t, ACT.Square).then_inc(sem("sq"), tick("sq"))
                act.wait_ge(sem("sq"), upto(act, "sq"))

        def norm_stat(pe, first, k, buf, bank, weights=None):
            for i in range(k):
                pe.wait_ge(sem("sq"), upto(pe, "sq", first + i + 1))
                n = buf.shape[-1]
                ins = pe.matmul(ps[:, bank, 0:n], weights if weights is not None else ones[:, :], buf[:, i],
                                start=(i == 0), stop=(i == k - 1))
            ins.then_inc(sem("stat"), tick("stat"))

        def norm_factor(act, first, bank, dim, dst):
            act.wait_ge(sem("stat"), upto(act, "stat", first + 1))
            n = dst.shape[-1]
            act.activation(dst, ps[:, bank, 0:n], ACT.Ln, bias=eps[:, 0:1], scale=1.0 / dim).then_inc(sem("log_ms"), tick("log_ms"))
            act.wait_ge(sem("log_ms"), upto(act, "log_ms"))
            act.activation(dst, dst, ACT.Exp, scale=-0.5).then_inc(sem("rms"), tick("rms"))
            act.wait_ge(sem("rms"), upto(act, "rms"))

        def parts_act(act, first, hi, fulls):
            for k, t in enumerate(hi):
                act.wait_ge(sem("h_full"), upto(act, "h_full", first + k + 1))
                act.activation(t, fulls[k % 2], ACT.Copy).then_inc(sem("h_hi"), tick("h_hi"))
                act.wait_ge(sem("h_hi"), upto(act, "h_hi"))

        def parts_dve(dve, first, full, hi, lo, fulls):
            n = len(lo)

            def low(k):
                dve.wait_ge(sem("h_hi"), upto(dve, "h_hi", first + k + 1))
                dve.tensor_tensor(lo[k], fulls[k % 2], hi[k].bitcast(F32), ALU.subtract).then_inc(sem("h_lo"), tick("h_lo"))
                dve.wait_ge(sem("h_lo"), upto(dve, "h_lo"))

            for k in range(n):
                full(k, fulls[k % 2])
                if k:
                    low(k - 1)
            low(n - 1)

        def normed(dve, tiles, gain, factor, stat_no):
            def full(k, dst):
                if k == 0:
                    dve.wait_ge(sem("rms"), upto(dve, "rms", stat_no + 1))
                dve.scalar_tensor_tensor(dst, tiles[k], gain[:, k:k + 1], factor, ALU.mult, ALU.mult).then_inc(sem("h_full"), tick("h_full"))
                dve.wait_ge(sem("h_full"), upto(dve, "h_full"))
            return full

        def product(pe, dst, lhs, rhs, K, first=True, last=True, n0=0):
            for k in range(K):
                (lh, ll), (rh, rl) = lhs(k), rhs(k)
                pe.matmul(dst, lh, rh, start=first and k == 0, stop=False)
                pe.matmul(dst, lh, rl, start=False, stop=False)
                ins = pe.matmul(dst, ll, rh, start=False, stop=last and k == K - 1)
            return ins

        def features(pe, slot, half, K, hi, lo, bank, cols=P, n=S, k0=0, first=True, last=True):
            wh, wl = slot_view(w_hi, slot, K), slot_view(w_lo, slot, K)
            c = slice(half * P, half * P + cols)
            return product(pe, ps[0:cols, bank, 0:n], lambda k: (wh[:, k, c], wl[:, k, c]),
                           lambda k: (hi[:, k0 + k, :], lo[:, k0 + k, :]), K, first, last)

        def tokens(pe, slot, half, K, hi, lo, bank, tiles=(0, 1), c0=0, n=256):
            wh, wl = slot_view(w_hi, slot, K), slot_view(w_lo, slot, K)
            for j, t in enumerate(tiles):
                ins = product(pe, ps[:, bank, j * n:j * n + n],
                              lambda k: (hi[:, k, t * P:t * P + P], lo[:, k, t * P:t * P + P]),
                              lambda k: (wh[:, k, c0:c0 + n], wl[:, k, c0:c0 + n]), K)
            return ins

        norm_tiles = {"x": (0, 8, 0), "q": (8, 3, 1), "kv": (11, 2, 2), "ffn": (13, 8, 3)}
        PART = {"x": 0, "q": 8, "kv": 11, "y": 13, "ffn": 21}
        col = lambda c, n: g[:, c:c + n]
        block = ctx.enter_context(nc.Block())
        LIN = {"gla": dict(q=0, k=1, v=0, gate=256, col=16), "ret": dict(q=2, k=3, v=512, gate=768, col=48)}

        @block.sync
        def _(sp):
            sp.dma_start(x_in[:], A["x"][0].rearrange("(t p) d -> p t d", p=P)).then_inc(sem("init_x"), 16)
            sp.dma_start(cm[:], A["c_main"]).then_inc(sem("init_c"), 16)
            sp.dma_start(levels_in[:], A["c_levels"]).then_inc(sem("init_c"), 16)

            def load(c, slot, parts, K):
                sp.wait_ge(sem("w_split"), upto(sp, "w_split", c - 1))
                for c0, src in parts:
                    n = src.shape[-1]
                    sp.dma_start(slot_view(w_raw, slot, K)[:, :, c0:c0 + n], src).then_inc(sem(f"w_loaded{slot}"), 16)

            with sp.Fori(0, DEPTH) as l:
                layer[sp] = l
                for c, (K, parts) in enumerate(layer_chunks(l)):
                    load(c, c % 2, parts, K)
                    if c == 3:
                        sp.wait_ge(sem("x_down"), upto(sp, "x_down", 0))
                        sp.dma_start(tab[:], A["c_rope"]).then_inc(sem("tab_loaded"), tick("tab_loaded", 16))
                with sp.Fori(0, KF // 2) as i:
                    for s in range(2):
                        f = 2 * i + s
                        sp.wait_ge(sem("w_split"), upto(sp, "w_split", C_UP + f - 1))
                        for half in range(2):
                            src = A["ffn_w_up"][bass.ds(l, 1), :, bass.ds(f * P + half * FF, P)]
                            sp.dma_start(slot_view(w_raw, s, KD)[:, :, half * P:half * P + P],
                                         src.rearrange("a (k p) n -> p (a k) n", p=P)).then_inc(sem(f"w_loaded{s}"), 16)
                with sp.Fori(0, 2) as i:
                    for j in range(6):
                        m, kg = 2 * i + j // 3, j % 3
                        sp.wait_ge(sem("w_split"), upto(sp, "w_split", C_DOWN + 6 * i + j - 1))
                        K = DOWN_K[kg]
                        for k0 in (0, K // 2):
                            src = A["ffn_w_down"][bass.ds(l, 1), (8 * kg + k0) * P:(8 * kg + k0 + K // 2) * P, bass.ds(m * 256, 256)]
                            sp.dma_start(slot_view(w_raw, j % 2, K)[:, k0:k0 + K // 2, :],
                                         src.rearrange("a (k p) n -> p (a k) n", p=P)).then_inc(sem(f"w_loaded{j % 2}"), 16)
            end_layer("sp")
            layer[sp] = 2
            for c, (K, parts) in enumerate(second):
                if c == C2_QK:
                    sp.wait_ge(sem("stat"), upto(sp, "stat", 2))
                    sp.dma_start(win_in[:], A["c_win"]).then_inc(sem("win_loaded"), 16)
                    sp.dma_start(a_cos[:], A["c_arope"][:, 0]).then_inc(sem("win_loaded"), 16)
                    sp.dma_start(a_sin[:], A["c_arope"][:, 1]).then_inc(sem("win_loaded"), 16)
                if c == C2_BQ:
                    sp.wait_ge(sem("pv"), upto(sp, "pv", 32))
                    sp.dma_start(late[:], A["c_late"]).then_inc(sem("late_loaded"), 16)
                if c == C2_KV:
                    sp.wait_ge(sem("pv"), upto(sp, "pv", 64))
                    sp.dma_start(mem_in[:], A["mem_2"][0].rearrange("(t p) d -> p t d", p=P)).then_inc(sem("mem_loaded"), 16)
                load(c, c % 2, parts, K)
            for r in range(RES):
                sp.wait_ge(sem("out_copied"), upto(sp, "out_copied", 2 * r + 2))
                sp.dma_start(out[0].rearrange("(n r) d -> r n d", r=RES)[r], out_sb[:, r % 2]).then_inc(sem(f"out_stored{r % 2}"), 16)
            for r in range(2):
                sp.wait_ge(sem(f"out_stored{r}"), 16 * RES // 2)
            end_layer("sp")

        @block.gpsimd
        def _(pool):
            pool.memset(ones[:], 1.0).then_inc(sem("w_split"), 1)
            pool.memset(eps[:], EPS).then_inc(sem("w_split"), 1)
            pool.wait_ge(sem("w_split"), 2)
            with nc.allow_non_contiguous_dma("gains go one to a partition"):
                def gain(name, c0, k):
                    for l in range(DEPTH):
                        pool.dma_start(gains[:, l, c0:c0 + k],
                                       A[name][l].rearrange("(k p) -> p k", p=P)).then_inc(sem("init_g"), 16)
                for name, c0, k in (("attn_norm", G_ATTN, 8), ("mla_q_norm", G_Q, 3), ("mla_kv_norm", G_KV, 2),
                                    ("ffn_norm", G_FFN, 8), ("ffn_conv_b", G_CONVB, KF), ("gla_b_gate", G_GATE, 1),
                                    ("mla_out_norm", G_OUT, 4), ("gla_out_norm", G_OUT + 4, 2),
                                    ("ret_out_norm", G_OUT + 6, 2)):
                    gain(name, c0, k)
                for l in range(DEPTH):
                    for w in range(3):
                        c0 = G_CONVW + w * KF
                        pool.dma_start(gains[:, l, c0:c0 + KF],
                                       A["ffn_conv_w"][l, w].rearrange("(k p) -> p k", p=P)).then_inc(sem("init_g"), 16)
                pool.dma_start(wg_all[64:64 + GATE_RANK], A["gla_w_gate"].rearrange("l r n -> r l n")).then_inc(sem("init_g"), 16)
                for c0, k, src in ((0, 8, A["final_norm"]), (8, 8, A["g_pre_2"][0]), (16, 8, A["g_mem_2"][0]),
                                   (24, 8, A["g_post_2"][0]), (32, 24, A["b_merge_2"][0])):
                    pool.dma_start(g2[:, c0:c0 + k], src.rearrange("(k p) -> p k", p=P)).then_inc(sem("init_g"), 16)
                for c, name in ((56, "q_norm_2"), (57, "k_norm_2")):
                    for half in range(2):
                        pool.dma_start(g2[64 * half:64 * half + 64, c:c + 1],
                                       A[name][0].rearrange("(p k) -> p k", k=1)).then_inc(sem("init_g"), 16)

            def split(c, slot, K):
                n = K * 256
                pool.wait_ge(sem("w_high"), upto(pool, "w_high", c + 1))
                pool.tensor_tensor(w_lo[:, slot, 0:n], w_raw[:, slot, 0:n], w_hi[:, slot, 0:n].bitcast(F32),
                                   ALU.subtract).then_inc(sem("w_split"), 1)

            with pool.Fori(0, DEPTH) as l:
                layer[pool] = l
                for c, (K, _) in enumerate(layer_chunks(0)):
                    split(c, c % 2, K)
                with pool.Fori(0, KF // 2) as i:
                    for q in range(2):
                        split(C_UP + 2 * i + q, q, KD)
                with pool.Fori(0, 2) as i:
                    for j in range(6):
                        split(C_DOWN + 6 * i + j, j % 2, DOWN_K[j % 3])
            layer[pool] = 2
            for c, (K, _) in enumerate(second):
                split(c, c % 2, K)

        @block.tensor
        def _(pe):
            def split_ready(c):
                pe.wait_ge(sem("w_split"), upto(pe, "w_split", c + 1))

            def bank_free(t):
                if not isinstance(t, int) or t > 3:
                    pe.wait_ge(sem("tile_copied"), upto(pe, "tile_copied", t - 3))

            def feature_chunk(c, slot, K, tile, hi, lo, widths=(P, P)):
                split_ready(c)
                for half in range(2):
                    bank_free(tile + half)
                    features(pe, slot, half, K, hi, lo, (2 * slot + half), widths[half]).then_inc(sem("tile_done"), tick("tile_done"))

            def token_chunk(c, slot, K, tile, hi, lo):
                split_ready(c)
                for half in range(2):
                    bank_free(tile + half)
                    tokens(pe, slot, half, K, hi, lo, 2 * slot + half, (2 * half, 2 * half + 1)).then_inc(sem("tile_done"), tick("tile_done"))

            pe.wait_ge(sem("init_x"), 16)
            pe.wait_ge(sem("init_c"), 32)
            pe.wait_ge(sem("w_split"), 2)
            for k in range(KD):
                if k > 3:
                    pe.wait_ge(sem("init_xt"), k - 3)
                for t in range(NT):
                    ins = pe.transpose(ps[:, MAIN + k % 4, t * P:t * P + P], x_in[:, t, k * P:k * P + P], ident)
                ins.then_inc(sem("init_turn"), 1)
            pe.matmul(ps[0:1, 0, 0:1], ones[:, 0:1], ones[:, 0:1], start=True, stop=True).then_inc(sem("tile_done"), 1)

            with pe.Fori(0, DEPTH) as l:
                layer[pe] = l
                att_base.update(pe=0, pe_o=0)
                norm_stat(pe, 0, 8, sq, STAT_BANK)
                pe.wait_ge(sem("h_lo"), upto(pe, "h_lo", 8))
                for c in range(CH_Z):
                    if c < 5:
                        feature_chunk(c, c % 2, KD, 2 * c, h_hi, h_lo, (P, 80) if c == 2 else (P, P))
                    else:
                        token_chunk(c, c % 2, KD, 2 * c, h_hi, h_lo)
                norm_stat(pe, 8, 3, sq2, 5)
                norm_stat(pe, 11, 2, sq2[:, 3:5], 6)
                pe.wait_ge(sem("h_lo"), upto(pe, "h_lo", PART["q"] + 3))
                for j in range(CH_UQ):
                    feature_chunk(C_UQ + j, (C_UQ + j) % 2, 3, 2 * (C_UQ + j), h_hi, h_lo)
                pe.wait_ge(sem("h_lo"), upto(pe, "h_lo", PART["kv"] + 2))
                kv_hi, kv_lo = h_hi[:, 3:5, :], h_lo[:, 3:5, :]
                for j in range(2):
                    c = C_UKV + j
                    feature_chunk(c, c % 2, 2, 2 * c, kv_hi, kv_lo)
                for j in range(2, 4):
                    c = C_UKV + j
                    token_chunk(c, c % 2, 2, 2 * c, kv_hi, kv_lo)
                pe.wait_ge(sem("tile_copied"), upto(pe, "tile_copied", 2 * C_OUT))
                pe.matmul(ps[:, 4, :], dup_swap[0:64, :], kg[0:64, :], start=True, stop=True)
                pe.matmul(ps[:, 7, :], dup[0:64, :], kg[0:64, :], start=True, stop=True).then_inc(sem("rot"), tick("rot"))
                for j in range(2):
                    pe.matmul(ps[:, 5 + j, :], swap32, lin[:, 2 + j, :], start=True, stop=True).then_inc(sem("rot"), tick("rot"))
                for j in range(2):
                    pe.wait_ge(sem("roped"), upto(pe, "roped", 1 + j))
                    pe.matmul(ps[:, 4 + j, :], swap64, qr[:, j, :], start=True, stop=True).then_inc(sem("rot"), tick("rot"))
                pe.wait_ge(sem("roped"), upto(pe, "roped", 5))
                att_pe(pe, mla_groups(), prob, prob_t)

                pe.wait_ge(sem("o_norm"), upto(pe, "o_norm", 4))
                pe.matmul(ps[:, 6, :], wg[64:64 + GATE_RANK, :], kg[64:64 + GATE_RANK, :], start=True, stop=True).then_inc(sem("gate"), tick("gate"))

                def pairs(q, k, no):
                    if no:
                        pe.wait_ge(sem("lvl_kept"), upto(pe, "lvl_kept", no))
                    for h in range(4):
                        r = slice(LIN_DK * h, LIN_DK * h + LIN_DK)
                        for t in range(NT):
                            c = slice(t * P, t * P + P)
                            ins = pe.matmul(ps[:, MAIN + h, c], k[r, c], q[r, c], start=True, stop=True,
                                            tile_position=(LIN_DK * h, 0))
                    ins.then_inc(sem("lvl_a"), tick("lvl_a"))

                for no, name in enumerate(LIN):
                    p_ = LIN[name]
                    if name == "gla":
                        pe.wait_ge(sem("gk"), upto(pe, "gk", 1))
                        pairs(lin[:, 0], lin[:, 1], 0)
                        for i in range(len(LEVELS)):
                            pe.wait_ge(sem("lvl_k"), upto(pe, "lvl_k", i + 1))
                            pairs(gl[:, 2], gl[:, 3], i + 1)
                    else:
                        pe.wait_ge(sem("o_copied"), upto(pe, "o_copied", 2))
                        pairs(lin[:, 2], lin[:, 3], 8)
                    pe.wait_ge(sem("lin_qk"), upto(pe, "lin_qk", 2 * no + 2))
                    for t in range(NT):
                        ins = pe.transpose(ps[:, 2, t * P:t * P + P], gl[:, 6, t * P:t * P + P], ident)
                    ins.then_inc(sem("kd_turned"), tick("kd_turned"))
                    pe.wait_ge(sem("kd_t"), upto(pe, "kd_t", no + 1))
                    for t in range(NT):
                        ins = pe.matmul(ps[:, t // 2, t % 2 * 256:t % 2 * 256 + 256], kd_t[:, t, :],
                                        tm[:, t, p_["v"]:p_["v"] + 256], start=True, stop=True)
                    ins.then_inc(sem("u_sum"), tick("u_sum"))
                    pe.wait_ge(sem("state"), upto(pe, "state", 2 * no + 2))
                    pe.wait_ge(sem("lvl_kept"), upto(pe, "lvl_kept", 8 + no))
                    for t in range(NT):
                        b, c0 = 2 + t // 2, t % 2 * 256
                        if t:
                            pe.matmul(ps[:, b, c0:c0 + 256], gl[:, 5, t * P:t * P + P], um[:, t - 1, :],
                                      start=True, stop=False, skip_group_check=True)
                        for h in range(4):
                            ins = pe.matmul(ps[:, b, c0 + h * 64:c0 + h * 64 + 64], amat[:, h, t, :],
                                            tm[:, t, p_["v"] + h * 64:p_["v"] + h * 64 + 64],
                                            start=(t == 0), stop=(t == 0 or h == 3), skip_group_check=True)
                    ins.then_inc(sem("o_lin"), tick("o_lin"))
                pe.wait_ge(sem("y_lin"), upto(pe, "y_lin", 2))
                for k in range(KD):
                    if k > 3:
                        pe.wait_ge(sem("h_full"), upto(pe, "h_full", PART["y"] + k - 3))
                    for t in range(NT):
                        src = (y_mla[:, t, k * P:k * P + P] if k < 4 else
                               tm[:, t, 256 + (k - 4) * P:256 + (k - 3) * P] if k < 6 else
                               tm[:, t, 768 + (k - 6) * P:768 + (k - 5) * P])
                        ins = pe.transpose(ps[:, MAIN + k % 4, t * P:t * P + P], src, ident)
                    ins.then_inc(sem("y_turned"), tick("y_turned"))
                pe.wait_ge(sem("h_lo"), upto(pe, "h_lo", PART["y"] + 8))
                for j in range(CH_OUT):
                    c = C_OUT + j
                    feature_chunk(c, c % 2, KD, 2 * c, h_hi, h_lo)
                norm_stat(pe, 13, 8, sq, STAT_BANK)
                with pe.Fori(0, KF // 2) as i:
                    for s in range(2):
                        if s == 0:
                            pe.wait_ge(sem("h_lo"), upto(pe, "h_lo", PART["ffn"] + 8))
                        c = C_UP + 2 * i + s
                        feature_chunk(c, s, KD, 2 * c, h_hi, h_lo)
                count["tile_done"] = 2 * C_DOWN
                with pe.Fori(0, 2) as i:
                    for q in range(2):
                        for part, K in enumerate(DOWN_K):
                            j = 3 * q + part
                            split_ready(C_DOWN + 6 * i + j)
                            pe.wait_ge(sem("hid_lo"), upto(pe, "hid_lo", 8 * part + K))
                            for half in range(2):
                                if part == 0:
                                    pe.wait_ge(sem("tile_copied"), upto(pe, "tile_copied", T_DOWN + 4 * i + 2 * q + half - 3))
                                features(pe, j % 2, half, K, hid_hi, hid_lo, 2 * q + half, k0=8 * part,
                                             first=part == 0, last=part == 2).then_inc(sem("tile_done"), tick("tile_done"))
                count["tile_done"] = 2 * CH_LAYER
            end_layer("pe")

            layer[pe] = 2
            att_base.update(pe=0, pe_o=0)
            norm_stat(pe, 0, 8, sq_2, STAT_BANK)
            norm_stat(pe, 8, 8, sq_2, 6)
            pe.wait_ge(sem("h_lo"), upto(pe, "h_lo", 8))

            def bank(tile):
                if tile > 3:
                    pe.wait_ge(sem("tile_copied"), upto(pe, "tile_copied", tile - 3))
                return tile % 4

            def chunk2(c, kind="f", K=KD, hi=h_hi, lo=h_lo, n=S):
                split_ready(c)
                for half in range(2):
                    b = bank(2 * c + half)
                    if kind == "f" or (kind == "kv" and half == 0):
                        ins = features(pe, c % 2, half, K, hi, lo, b, n=n)
                    elif kind == "t":
                        ins = tokens(pe, c % 2, half, K, hi, lo, b, (2 * half, 2 * half + 1))
                    else:
                        ins = tokens(pe, c % 2, half, K, hi, lo, b, range(hi.shape[-1] // P), half * P, P)
                    ins.then_inc(sem("tile_done"), tick("tile_done"))

            def turn_branch(first):
                for k in range(4):
                    for r in range(RES):
                        ins = pe.transpose(ps[:, 4 + k, r * P:r * P + P], o_br[:, r, k * P:k * P + P], ident)
                    ins.then_inc(sem("o_turned"), tick("o_turned"))
                pe.wait_ge(sem("h_lo"), upto(pe, "h_lo", first + 4))

            def merge(c0):
                for m in range(4):
                    chunk2(c0 + 2 * m, K=4, hi=gt_hi, lo=gt_lo)
                    chunk2(c0 + 2 * m + 1)

            for c in range(C2_QK):
                chunk2(c, "t")
            for hp in range(4):
                if hp:
                    pe.wait_ge(sem("o_norm"), upto(pe, "o_norm", 2 * hp))
                for gi in range(3):
                    chunk2(C2_QK + 3 * hp + gi)
                for j in range(6):
                    pe.wait_ge(sem("tile_copied"), upto(pe, "tile_copied", 2 * (C2_QK + 3 * hp) + j + 1))
                    if 6 * hp + j > 3:
                        pe.wait_ge(sem("roped"), upto(pe, "roped", 6 * hp + j - 3))
                    pe.matmul(ps[:, 4 + j % 4 if hp % 2 == 0 else 4 + (j + 2) % 4, :], swap64,
                                  qk[:, hp % 2, j, :], start=True, stop=True).then_inc(sem("rot"), tick("rot"))
                pe.wait_ge(sem("roped"), upto(pe, "roped", 6 * hp + 6))
                att_pe(pe, a_groups(hp), prob2, prob2_t)
            pe.wait_ge(sem("o_norm"), upto(pe, "o_norm", 8))
            chunk2(C2_GA)
            chunk2(C2_GA + 1)
            turn_branch(8)
            merge(C2_GA + 2)
            for c in range(C2_BQ, C2_GB):
                chunk2(c, "f" if c < C2_GB - 1 else "kv")
            pe.wait_ge(sem("late_loaded"), 16)
            for j in range(5):
                pe.wait_ge(sem("sq"), upto(pe, "sq", 16 + j + 1))
                pe.matmul(ps[:, 4 + j % 2, :], late[:, 2 * P:3 * P], sq_2[:, j], start=True, stop=True).then_inc(sem("stat"), tick("stat"))
                pe.wait_ge(sem("h_norm"), upto(pe, "h_norm", j + 1))
                if j > 1:
                    pe.wait_ge(sem("roped"), upto(pe, "roped", 24 + j - 1))
                pe.matmul(ps[:, 6 + j % 2, :], swap32, q_b[:, j, :], start=True, stop=True).then_inc(sem("rot"), tick("rot"))
            pe.wait_ge(sem("roped"), upto(pe, "roped", 29))
            for j in range(2):
                ins = pe.matmul(ps[:, 4 + j, :], late[:, j * P:j * P + P], q_b[:, 4, :], start=True, stop=True)
            ins.then_inc(sem("k_spread"), tick("k_spread"))
            pe.wait_ge(sem("k_b"), upto(pe, "k_b", 2))
            pe.wait_ge(sem("tile_copied"), upto(pe, "tile_copied", 2 * C2_GB))
            att_pe(pe, b_groups(), prob2, prob2_t)
            pe.wait_ge(sem("o_norm"), upto(pe, "o_norm", 12))
            chunk2(C2_GB)
            chunk2(C2_GB + 1)
            turn_branch(12)
            merge(C2_GB + 2)
            pe.wait_ge(sem("mem_loaded"), 16)
            for k in range(KD):
                if k > 3:
                    pe.wait_ge(sem("mem_t"), upto(pe, "mem_t", k - 3))
                for t in range(2):
                    ins = pe.transpose(ps[:, 4 + k % 4, t * P:t * P + P], mem_in[:, t, k * P:k * P + P], ident)
                ins.then_inc(sem("mem_turned"), tick("mem_turned"))
            pe.wait_ge(sem("mem_t"), upto(pe, "mem_t", 8))
            norm_stat(pe, 21, 8, sq_2[:, :, 0:N_MEM], STAT_BANK)
            pe.wait_ge(sem("h_lo"), upto(pe, "h_lo", 24))
            for j in range(4):
                chunk2(C2_KV + j, "f" if j < 2 else "m", hi=mem_hi, lo=mem_lo, n=N_MEM)
            for j in range(2):
                chunk2(C2_MQ + j)
            pe.wait_ge(sem("tile_copied"), upto(pe, "tile_copied", 2 * C2_GM))
            att_pe(pe, m_groups(), prob2, prob2_t)
            pe.wait_ge(sem("o_norm"), upto(pe, "o_norm", 16))
            chunk2(C2_GM)
            chunk2(C2_GM + 1)
            turn_branch(24)
            merge(C2_GM + 2)
            pe.wait_ge(sem("h_lo"), upto(pe, "h_lo", 36))
            for j in range(4):
                chunk2(C2_OUT + j)
            norm_stat(pe, 29, 8, sq_2, STAT_BANK)
            for r in range(RES):
                for q in range(2):
                    if 2 * r + q > 1:
                        pe.wait_ge(sem("out_copied"), upto(pe, "out_copied", 2 * r + q - 1))
                    for k in range(4):
                        pe.wait_ge(sem("out_full"), upto(pe, "out_full", 8))
                        ins = pe.transpose(ps[:, 4 + q, k * P:k * P + P], out_t[:, 4 * q + k, r * P:r * P + P], ident)
                    ins.then_inc(sem("out_turned"), tick("out_turned"))
            end_layer("pe")

        fulls1 = [tmp[:, 0], tmp[:, 1]]
        fulls2 = [prob2[:, 0, 0:S], prob2[:, 1, 0:S]]
        x1 = [qk[:, 0, 0], qk[:, 0, 1]]
        fulls3 = [qk[:, 0, 2], qk[:, 0, 3]]
        y_br = [prob2_t[:, i, 0:S] for i in range(2)]
        gate_br = fulls2
        heads16 = lambda t, d: t.rearrange("p t (h d) -> p (t h) d", d=d)

        def init_count():
            return 16 * (9 * DEPTH + 3 * DEPTH + 1 + 5 + 4)

        @block.scalar
        def _(act):
            def copy_tile(tile, bank, dst, rows=P, func=ACT.Copy, n=S, **kw):
                act.wait_ge(sem("tile_done"), upto(act, "tile_done", tile + 1))
                src = ps[0:rows, bank, 0:n]
                if len(dst.shape) == 3:
                    src = src.rearrange("p (a n) -> p a n", a=dst.shape[1])
                act.activation(dst, src, func, **kw).then_inc(sem("tile_copied"), tick("tile_copied"))
                act.wait_ge(sem("tile_copied"), upto(act, "tile_copied"))

            def high(c, slot, K, loaded):
                n = K * 256
                act.wait_ge(sem(f"w_loaded{slot}"), upto(act, f"w_loaded{slot}", 16 * loaded))
                act.activation(w_hi[:, slot, 0:n], w_raw[:, slot, 0:n], ACT.Copy).then_inc(sem("w_high"), 1)

            act.preload_act_table_set("natural_log_exp_and_others")
            for slot in range(2):
                act.wait_ge(sem(f"w_loaded{slot}"), 32)
                act.activation(w_hi[:, slot], w_raw[:, slot], ACT.Copy).then_inc(sem("w_high"), 1)
            for k in range(KD):
                act.wait_ge(sem("init_turn"), k + 1)
                act.activation(x_t[:, k], ps[:, MAIN + k % 4, :], ACT.Copy).then_inc(sem("init_xt"), 1)
            act.wait_ge(sem("init_xt"), KD)
            dmas = [n_dma[0::2], n_dma[1::2]]
            Ks = [K for K, _ in layer_chunks(0)]

            def next_high(c):
                high(c + 2, c % 2, Ks[c + 2] if c + 2 < C_UP else KD, sum(dmas[c % 2][:c // 2 + 2]))

            with act.Fori(0, DEPTH) as l:
                layer[act] = l
                att_base.update(act=0)
                act.preload_act_table_set("natural_log_exp_and_others")
                act.wait_ge(sem("g"), upto(act, "g", 2))
                act.wait_ge(sem("x_down"), upto(act, "x_down", 0))
                norm_sq(act, [x_t[:, k] for k in range(KD)], sq)
                norm_factor(act, 0, STAT_BANK, D, rms_a[:])
                parts_act(act, 0, [h_hi[:, k] for k in range(KD)], fulls1)
                dst = [cq[:, k] for k in range(5)] + [kg[0:80, :]] + [lin[:, k] for k in range(4)]
                for t, d in enumerate(dst):
                    copy_tile(t, t % 4, d, rows=d.shape[0], scale=LIN_DK ** -0.5 if t == 6 else 1.0)
                    if t % 2:
                        next_high(t // 2)
                    if t == 5:
                        norm_sq(act, [cq[:, k] for k in range(5)], sq2)
                for j in range(8):
                    t = 10 + j
                    copy_tile(t, t % 4, tm[:, 2 * (j % 2):2 * (j % 2) + 2, j // 2 * 256:j // 2 * 256 + 256])
                    if t % 2:
                        next_high(t // 2)
                norm_factor(act, 1, 5, Q_RANK, rms_a[:])
                norm_factor(act, 2, 6, KV_RANK, rms_b[:])
                parts_act(act, PART["q"], [h_hi[:, k] for k in range(3)], fulls1)
                parts_act(act, PART["kv"], [h_hi[:, 3 + k] for k in range(2)], fulls1)
                for j, d in enumerate([qn[:, h] for h in range(4)] + [qr[:, i] for i in range(2)]):
                    t = 2 * C_UQ + j
                    copy_tile(t, t % 4, d, scale=(NOPE + ROPE) ** -0.5)
                    if t % 2:
                        next_high(t // 2)
                for j, d in enumerate([kn[:, h] for h in range(4)] +
                                      [v_mla[:, 2 * a:2 * a + 2, b * 256:b * 256 + 256] for b in range(2) for a in range(2)]):
                    t = 2 * C_UKV + j
                    copy_tile(t, t % 4, d)
                    if t % 2:
                        next_high(t // 2)
                att_act(act, mla_groups(), prob, prob_t)
                act.wait_ge(sem("ymla_ss"), upto(act, "ymla_ss", 1))
                s16 = stats[:, 96:112]
                act.activation(s16, s16, ACT.Ln, bias=eps[:, 0:1], scale=1.0 / VDIM).then_inc(sem("ymla_log"), tick("ymla_log"))
                act.wait_ge(sem("ymla_log"), upto(act, "ymla_log"))
                act.activation(s16, s16, ACT.Exp, scale=-0.5).then_inc(sem("ymla_rms"), tick("ymla_rms"))
                act.wait_ge(sem("ymla_rms"), upto(act, "ymla_rms"))
                act.wait_ge(sem("gate"), upto(act, "gate", 1))
                act.activation(gl[:, 1], ps[:, 6, :], ACT.Identity, bias=col(G_GATE, 1)).then_inc(sem("gk"), tick("gk"))
                act.wait_ge(sem("gk"), upto(act, "gk"))
                act.activation(gl[:, 2], gl[:, 1], ACT.Abs).then_inc(sem("gate_abs"), tick("gate_abs"))
                act.wait_ge(sem("gate_abs"), upto(act, "gate_abs"))
                act.activation(gl[:, 2], gl[:, 2], ACT.Exp, scale=-1.0).then_inc(sem("gate_exp"), tick("gate_exp"))
                act.wait_ge(sem("gate_exp"), upto(act, "gate_exp"))
                act.activation(gl[:, 2], gl[:, 2], ACT.Ln, bias=1.0).then_inc(sem("gate_ln"), tick("gate_ln"))
                act.wait_ge(sem("gate_ln"), upto(act, "gate_ln"))
                act.wait_ge(sem("decay_sum"), upto(act, "decay_sum", 1))
                act.activation(gl[:, 4], gl[:, 0], ACT.Exp, scale=1.0 / GATE_NORM).then_inc(sem("decay_exp"), tick("decay_exp"))
                act.wait_ge(sem("decay_exp"), upto(act, "decay_exp"))
                act.wait_ge(sem("decay_rest"), upto(act, "decay_rest", 1))
                act.activation(gl[:, 6], gl[:, 6], ACT.Exp, scale=1.0 / GATE_NORM).then_inc(sem("decay_exp"), tick("decay_exp"))
                act.wait_ge(sem("decay_exp"), upto(act, "decay_exp"))
                for i in range(len(LEVELS)):
                    act.wait_ge(sem("lvl_diff"), upto(act, "lvl_diff", i + 1))
                    act.activation(gl[:, 1], gl[:, 1], ACT.Abs).then_inc(sem("lvl_abs"), tick("lvl_abs"))
                    act.wait_ge(sem("lvl_abs"), upto(act, "lvl_abs"))
                    act.activation(gl[:, 1], gl[:, 1], ACT.Exp, scale=-1.0 / GATE_NORM).then_inc(sem("lvl_exp"), tick("lvl_exp"))
                    act.wait_ge(sem("lvl_exp"), upto(act, "lvl_exp"))
                for no, name in enumerate(LIN):
                    p_ = LIN[name]
                    act.wait_ge(sem("kd_turned"), upto(act, "kd_turned", no + 1))
                    act.activation(kd_t[:], ps[:, 2, :].rearrange("p (t n) -> p t n", t=NT), ACT.Copy).then_inc(sem("kd_t"), tick("kd_t"))
                    act.wait_ge(sem("kd_t"), upto(act, "kd_t"))
                    if no:
                        act.wait_ge(sem("y_lin"), upto(act, "y_lin", 1))
                    act.activation(sig[:], tm[:, :, p_["gate"]:p_["gate"] + 256], ACT.Exp, scale=-1.0).then_inc(sem("g_exp"), tick("g_exp"))
                    act.wait_ge(sem("g_exp"), upto(act, "g_exp"))
                    act.wait_ge(sem("o_lin"), upto(act, "o_lin", no + 1))
                    for b in range(2):
                        act.activation(o_sb[:, 2 * b:2 * b + 2],
                                                 ps[:, 2 + b, :].rearrange("p (t n) -> p t n", t=2), ACT.Copy).then_inc(sem("o_copied"), tick("o_copied"))
                        act.wait_ge(sem("o_copied"), upto(act, "o_copied"))
                    act.wait_ge(sem("o_ss"), upto(act, "o_ss", no + 1))
                    s16 = stats[:, 64 + 16 * no:80 + 16 * no]
                    act.activation(s16, s16, ACT.Ln, bias=eps[:, 0:1], scale=1.0 / LIN_DV).then_inc(sem("o_log"), tick("o_log"))
                    act.wait_ge(sem("o_log"), upto(act, "o_log"))
                    act.activation(s16, s16, ACT.Exp, scale=-0.5).then_inc(sem("o_rms"), tick("o_rms"))
                    act.wait_ge(sem("o_rms"), upto(act, "o_rms"))
                parts_act(act, PART["y"], [h_hi[:, k] for k in range(KD)], fulls1)
                for m in range(KD):
                    t = 2 * C_OUT + m
                    if m > 1:
                        act.wait_ge(sem("x_mix"), upto(act, "x_mix", m - 1))
                    copy_tile(t, t % 4, tmp[:, m % 2])
                    if t % 2:
                        next_high(t // 2)
                for k in range(KD):
                    act.wait_ge(sem("x_mix"), upto(act, "x_mix", k + 1))
                    act.activation(sq[:, k], x_t[:, k], ACT.Square).then_inc(sem("sq"), tick("sq"))
                    act.wait_ge(sem("sq"), upto(act, "sq"))
                norm_factor(act, 3, STAT_BANK, D, rms_a[:])
                parts_act(act, PART["ffn"], [h_hi[:, k] for k in range(KD)], fulls1)
                act.activation(spare[:, 4:5], eps[:], ACT.Copy).then_inc(sem("held_act"), tick("held_act"))
                act.preload_act_table_set("silu_and_others")
                with act.Fori(0, KF // 2) as i:
                    for s in range(2):
                        f = 2 * i + s
                        t = T_UP + 2 * f
                        act.wait_ge(sem("tile_done"), upto(act, "tile_done", t + 1))
                        act.activation(a_pad[:, s, 2:S + 2], ps[:, 2 * s, :], ACT.Copy).then_inc(sem("tile_copied"), 1)
                        act.wait_ge(sem("tile_copied"), upto(act, "tile_copied", t + 1))
                        act.activation(conv[:], a_pad[:, s, 2:S + 2], ACT.Identity,
                                                    scale=g[:, bass.ds(G_CONVW + 2 * KF + f, 1)],
                                                    bias=g[:, bass.ds(G_CONVB + f, 1)]).then_inc(sem("conv0"), 1)
                        act.wait_ge(sem("conv0"), upto(act, "conv0", f + 1))
                        act.wait_ge(sem("conv"), upto(act, "conv", f + 1))
                        act.activation(conv[:], conv[:], ACT.Silu).then_inc(sem("silu"), 1)
                        act.wait_ge(sem("silu"), upto(act, "silu", f + 1))
                        act.wait_ge(sem("tile_done"), upto(act, "tile_done", t + 2))
                        act.activation(b_sb[:, s], ps[:, 2 * s + 1, :], ACT.Copy).then_inc(sem("tile_copied"), 1)
                        act.wait_ge(sem("tile_copied"), upto(act, "tile_copied", t + 2))
                        high(C_UP + f + 2, s, KD, sum(dmas[s][:C_UP // 2]) + 2 * (i + 2))
                        act.wait_ge(sem("gated"), upto(act, "gated", f + 1))
                        act.activation(hid_hi[:, bass.ds(f, 1), :].rearrange("p a n -> p (a n)"), b_sb[:, s], ACT.Copy).then_inc(sem("hid_hi"), 1)
                        act.wait_ge(sem("hid_hi"), upto(act, "hid_hi", f + 1))
                count["tile_copied"] = T_DOWN
                for n in ("conv0", "silu", "hid_hi"):
                    count[n] = KF
                with act.Fori(0, 2) as i:
                    act.wait_ge(sem("x_down"), upto(act, "x_down", 4 * i))
                    for q in range(2):
                        for j in (3 * q, 3 * q + 1):
                            act.wait_ge(sem("tile_done"), upto(act, "tile_done", 2 * (C_DOWN + 6 * i + j) + 2))
                            high(C_DOWN + 6 * i + j + 2, j % 2, DOWN_K[(j + 2) % 3],
                                 sum(dmas[j % 2][:C_DOWN // 2]) + 2 * (3 * i + j // 2 + 2))
                        for half in range(2):
                            act.wait_ge(sem("tile_done"), upto(act, "tile_done", 2 * (C_DOWN + 6 * i + 3 * q + 2) + half + 1))
                            dst = b_sb[:, half] if q == 0 else a_pad[:, half, 0:S]
                            act.activation(dst, ps[:, 2 * q + half, :], ACT.Copy).then_inc(sem("tile_copied"), 1)
                            act.wait_ge(sem("tile_copied"), upto(act, "tile_copied", T_DOWN + 4 * i + 2 * q + half + 1))
                        j = 3 * q + 2
                        high(C_DOWN + 6 * i + j + 2, j % 2, DOWN_K[(j + 2) % 3],
                             sum(dmas[j % 2][:C_DOWN // 2]) + 2 * (3 * i + j // 2 + 2))
                count["tile_copied"] = TILES_LAYER
            end_layer("act")

            layer[act] = 2
            att_base.update(act=0)
            act.preload_act_table_set("natural_log_exp_and_others")
            act.wait_ge(sem("x_down"), upto(act, "x_down", 0))
            norm_sq(act, [x_t[:, k] for k in range(KD)], sq_2)
            norm_factor(act, 0, STAT_BANK, D, rms_a[:])
            for k in range(KD):
                act.wait_ge(sem("x1_full"), upto(act, "x1_full", k + 1))
                act.activation(x_t[:, k], x1[k % 2], ACT.Copy).then_inc(sem("x1"), tick("x1"))
                act.wait_ge(sem("x1"), upto(act, "x1"))
                act.activation(sq_2[:, k], x1[k % 2], ACT.Square).then_inc(sem("sq"), tick("sq"))
                act.wait_ge(sem("sq"), upto(act, "sq"))
            norm_factor(act, 1, 6, D, rms_a[:])
            parts_act(act, 0, [h_hi[:, k] for k in range(KD)], fulls3)

            def copy2(tile, dst, **kw):
                copy_tile(tile, tile % 4, dst, **kw)
                c = tile // 2 + 2
                if tile % 2 and c < len(second):
                    high(c, c % 2, second[c][0], sum(len(p_) for _, p_ in second[c % 2:c + 1:2]))

            def branch(b, c0, first):
                for k in range(4):
                    copy2(2 * c0 + k, sgate[:, k], func=ACT.Silu)
                parts_act(act, first, [gt_hi[:, k] for k in range(4)], fulls2)
                act.wait_ge(sem("h_lo"), upto(act, "h_lo", first + 4 + (0 if b < 2 else 0)))
                for m in range(4):
                    for half in range(2):
                        if m:
                            act.wait_ge(sem("merged"), upto(act, "merged", 8 * b + 2 * m - 1 + half))
                        copy2(2 * (c0 + 2 + 2 * m) + half, y_br[half])
                    for half in range(2):
                        copy2(2 * (c0 + 3 + 2 * m) + half, gate_br[half], func=ACT.Sigmoid,
                              bias=g2[:, 32 + 8 * b + 2 * m + half:33 + 8 * b + 2 * m + half])

            for j in range(2 * C2_QK):
                copy2(j, av[:, 2 * (j % 2):2 * (j % 2) + 2, j // 2 * 256:j // 2 * 256 + 256])
            for hp in range(4):
                for j in range(6):
                    copy2(2 * (C2_QK + 3 * hp) + j, qk[:, hp % 2, j], scale=HD ** -0.5 if j % 2 == 0 else 1.0)
                att_act(act, a_groups(hp), prob2, prob2_t)
            act.wait_ge(sem("o_norm"), upto(act, "o_norm", 8))
            branch(0, C2_GA, 8)
            act.preload_act_table_set("natural_log_exp_and_others")
            for j in range(5):
                copy2(2 * C2_BQ + j, q_b[:, j])
            copy2(2 * C2_BQ + 5, v_b[:])
            norm_sq(act, [q_b[:, j] for j in range(5)], sq_2)
            for j in range(5):
                if j:
                    act.wait_ge(sem("h_norm"), upto(act, "h_norm", j))
                norm_factor(act, 2 + j, 4 + j % 2, HD, rms_a[:])
            att_act(act, b_groups(), prob2, prob2_t)
            act.wait_ge(sem("o_norm"), upto(act, "o_norm", 12))
            branch(1, C2_GB, 12)
            act.preload_act_table_set("natural_log_exp_and_others")
            for k in range(KD):
                act.wait_ge(sem("mem_turned"), upto(act, "mem_turned", k + 1))
                act.activation(mem_t[:, k], ps[:, 4 + k % 4, 0:N_MEM], ACT.Copy).then_inc(sem("mem_t"), tick("mem_t"))
                act.wait_ge(sem("mem_t"), upto(act, "mem_t"))
            norm_sq(act, [mem_t[:, k] for k in range(KD)], sq_2[:, :, 0:N_MEM])
            norm_factor(act, 7, STAT_BANK, D, rms_a[:, 0:N_MEM])
            parts_act(act, 16, [mem_hi[:, k] for k in range(KD)], [f[:, 0:N_MEM] for f in fulls2])
            for j in range(4):
                copy2(2 * C2_KV + j, km[:, j], n=N_MEM)
            for j in range(4):
                copy2(2 * C2_KV + 4 + j, vm[:, :, j * P:j * P + P], n=256)
            for j in range(4):
                copy2(2 * C2_MQ + j, q_m[:, j], scale=P ** -0.5)
            att_act(act, m_groups(), prob2, prob2_t)
            act.wait_ge(sem("o_norm"), upto(act, "o_norm", 16))
            branch(2, C2_GM, 24)
            act.preload_act_table_set("natural_log_exp_and_others")
            act.wait_ge(sem("tile_done"), upto(act, "tile_done", 2 * C2_OUT))
            for k in range(KD):
                act.wait_ge(sem("merged"), upto(act, "merged", 16 + k + 1))
                act.activation(h_hi[:, k], merged[:, k], ACT.Copy).then_inc(sem("h_hi"), tick("h_hi"))
                act.wait_ge(sem("h_hi"), upto(act, "h_hi"))
            for k in range(KD):
                copy2(2 * C2_OUT + k, out_t[:, k])
                act.activation(sq_2[:, k], out_t[:, k], ACT.Square).then_inc(sem("sq"), tick("sq"))
                act.wait_ge(sem("sq"), upto(act, "sq"))
            norm_factor(act, 8, STAT_BANK, D, rms_a[:])
            for r in range(RES):
                if r > 1:
                    act.wait_ge(sem(f"out_stored{r % 2}"), 16)
                for q in range(2):
                    act.wait_ge(sem("out_turned"), upto(act, "out_turned", 2 * r + q + 1))
                    act.activation(out_sb[:, r % 2, q * 512:q * 512 + 512], ps[:, 4 + q, :], ACT.Copy).then_inc(sem("out_copied"), tick("out_copied"))
                    act.wait_ge(sem("out_copied"), upto(act, "out_copied"))
            end_layer("act")

        @block.vector
        def _(dve):
            dve.wait_ge(sem("init_g"), init_count())
            dve.wait_ge(sem("w_split"), 2)
            dve.tensor_scalar(g2[:, 56:57], g2[:, 56:57], HD ** -0.5, None, ALU.mult).then_inc(sem("g_scaled"), 1)
            dve.wait_ge(sem("g_scaled"), 1)
            dve.wait_ge(sem("init_c"), 32)
            dve.tensor_copy(levels[:], levels_in[:]).then_inc(sem("x_down"), 1)
            dve.wait_ge(sem("x_down"), 1)

            def rope(no, z, rot, cos, sin, dst, t):
                dve.wait_ge(sem("rot"), upto(dve, "rot", no + 1))
                dve.tensor_tensor(dst, z, cos, ALU.mult).then_inc(sem("rope_cos"), tick("rope_cos"))
                dve.wait_ge(sem("rope_cos"), upto(dve, "rope_cos"))
                dve.tensor_tensor(t, rot, sin, ALU.mult).then_inc(sem("rope_sin"), tick("rope_sin"))
                dve.wait_ge(sem("rope_sin"), upto(dve, "rope_sin"))
                dve.tensor_tensor(dst, dst, t, ALU.add).then_inc(sem("roped"), tick("roped"))
                dve.wait_ge(sem("roped"), upto(dve, "roped"))

            with dve.Fori(0, DEPTH) as l:
                layer[dve] = l
                att_base.update(dve=0)
                dve.tensor_copy(g[:], gains[:, bass.ds(l, 1), :].rearrange("p a n -> p (a n)")).then_inc(sem("g"), tick("g"))
                dve.wait_ge(sem("g"), upto(dve, "g"))
                dve.tensor_copy(wg[64:80, :], wg_all[64:80, bass.ds(l, 1), :].rearrange("p a n -> p (a n)")).then_inc(sem("g"), tick("g"))
                dve.wait_ge(sem("g"), upto(dve, "g"))
                dve.wait_ge(sem("init_xt"), KD)
                hi, lo = [h_hi[:, k] for k in range(KD)], [h_lo[:, k] for k in range(KD)]
                xs = [x_t[:, k] for k in range(KD)]
                parts_dve(dve, 0, normed(dve, xs, col(G_ATTN, 8), rms_a[:], 0), hi, lo, fulls1)
                parts_dve(dve, PART["q"], normed(dve, [cq[:, k] for k in range(3)], col(G_Q, 3), rms_a[:], 1),
                          hi[0:3], lo[0:3], fulls1)
                parts_dve(dve, PART["kv"], normed(dve, [cq[:, 3 + k] for k in range(2)], col(G_KV, 2), rms_b[:], 2),
                          hi[3:5], lo[3:5], fulls1)
                dve.wait_ge(sem("tab_loaded"), upto(dve, "tab_loaded", 16))
                rope(0, ps[:, 7, :], ps[:, 4, :], tab[:, 0], tab[:, 1], kr[:], tmp[:, 2])
                for j in range(2):
                    rope(1 + j, lin[:, 2 + j], ps[:, 5 + j, :], tab[:, 2], tab[:, 3], lin[:, 2 + j], tmp[:, 2])
                for j in range(2):
                    rope(3 + j, qr[:, j], ps[:, 4 + j, :], tab[:, 0], tab[:, 1], qr[:, j], tmp[:, 2])
                att_dve(dve, mla_groups())
                ysq = amat[:].rearrange("p h t n -> p (h t) n")
                ym = heads16(y_mla[:], VDIM)
                dve.tensor_tensor(ysq, ym, ym, ALU.mult).then_inc(sem("ymla_sq"), tick("ymla_sq"))
                dve.wait_ge(sem("ymla_sq"), upto(dve, "ymla_sq"))
                dve.tensor_reduce(stats[:, 96:112], ysq, AX.X, ALU.add).then_inc(sem("ymla_ss"), tick("ymla_ss"))
                dve.wait_ge(sem("ymla_ss"), upto(dve, "ymla_ss"))
                dve.memset(gl[:, 4], 1.0).then_inc(sem("reset"), tick("reset"))
                dve.wait_ge(sem("reset"), upto(dve, "reset"))
                dve.memset(gl[:, 4].rearrange("p (t n) -> p t n", t=NT)[:, :, 0:1], 0.0).then_inc(sem("reset"), tick("reset"))
                dve.wait_ge(sem("reset"), upto(dve, "reset"))
                dve.wait_ge(sem("ymla_rms"), upto(dve, "ymla_rms", 1))
                dve.tensor_tensor(ym, ym, stats[:, 96:112].unsqueeze(2).to_broadcast([P, 16, VDIM]), ALU.mult).then_inc(sem("ymla"), tick("ymla"))
                dve.wait_ge(sem("ymla"), upto(dve, "ymla"))
                dve.memset(amat[:], 0.0).then_inc(sem("amat0"), tick("amat0"))
                dve.wait_ge(sem("amat0"), upto(dve, "amat0"))
                dve.wait_ge(sem("gk"), upto(dve, "gk", 1))
                dve.tensor_scalar(gl[:, 3], gl[:, 1], 0.0, None, ALU.min).then_inc(sem("gate_min"), tick("gate_min"))
                dve.wait_ge(sem("gate_min"), upto(dve, "gate_min"))
                dve.wait_ge(sem("gate_ln"), upto(dve, "gate_ln", 1))
                dve.tensor_tensor(gl[:, 3], gl[:, 3], gl[:, 2], ALU.subtract).then_inc(sem("gate_log"), tick("gate_log"))
                dve.wait_ge(sem("gate_log"), upto(dve, "gate_log"))
                dve.tensor_tensor_scan(gl[:, 0], gl[:, 4], gl[:, 3], 0.0, ALU.mult, ALU.add).then_inc(sem("decay_sum"), tick("decay_sum"))
                dve.wait_ge(sem("decay_sum"), upto(dve, "decay_sum"))
                by_tile = lambda t: t.rearrange("p (t n) -> p t n", t=NT)
                b4 = by_tile(gl[:, 0])
                dve.tensor_tensor(by_tile(gl[:, 6]), b4[:, :, P - 1:P].to_broadcast([P, NT, P]), b4,
                                            ALU.subtract).then_inc(sem("decay_rest"), tick("decay_rest"))
                dve.wait_ge(sem("decay_rest"), upto(dve, "decay_rest"))
                def diff(i):
                    s = LEVELS[i]
                    v = gl[:, 0].rearrange("p (b n) -> p b n", n=2 * s)
                    dve.tensor_tensor(gl[:, 1].rearrange("p (b n) -> p b n", n=2 * s), v,
                                                v[:, :, s - 1:s].to_broadcast([P, S // (2 * s), 2 * s]), ALU.subtract).then_inc(sem("lvl_diff"), tick("lvl_diff"))
                    dve.wait_ge(sem("lvl_diff"), upto(dve, "lvl_diff"))

                def keep(i, lv):
                    dve.wait_ge(sem("lvl_a"), upto(dve, "lvl_a", i + 1))
                    dve.memset(spare[:, 2:3], 0.0).then_inc(sem("held_dve"), tick("held_dve"))
                    ins = dve.copy_predicated(amat[:].rearrange("p h t n -> p (h t) n"),
                                              levels[:, lv:lv + 1, :].to_broadcast([P, 4 * NT, P]),
                                              ps[:, MAIN:MAIN + 4, :].rearrange("p h (t n) -> p (h t) n", t=NT))
                    ins.then_inc(sem("lvl_kept"), tick("lvl_kept"))
                    dve.wait_ge(sem("lvl_kept"), upto(dve, "lvl_kept"))

                diff(0)
                keep(0, len(LEVELS))
                for i in range(len(LEVELS)):
                    dve.wait_ge(sem("lvl_exp"), upto(dve, "lvl_exp", i + 1))
                    dve.tensor_tensor(gl[:, 2], lin[:, 0], gl[:, 1], ALU.mult).then_inc(sem("lvl_q"), tick("lvl_q"))
                    dve.wait_ge(sem("lvl_q"), upto(dve, "lvl_q"))
                    dve.tensor_tensor(gl[:, 3], lin[:, 1], gl[:, 1], ALU.mult).then_inc(sem("lvl_k"), tick("lvl_k"))
                    dve.wait_ge(sem("lvl_k"), upto(dve, "lvl_k"))
                    if i + 1 < len(LEVELS):
                        diff(i + 1)
                    keep(i + 1, i)
                for no, name in enumerate(LIN):
                    p_ = LIN[name]
                    q, k = lin[:, p_["q"]], lin[:, p_["k"]]
                    if no == 0:
                        dve.wait_ge(sem("decay_exp"), upto(dve, "decay_exp", 2))
                        dve.tensor_tensor(gl[:, 5], q, gl[:, 4], ALU.mult).then_inc(sem("lin_qk"), tick("lin_qk"))
                        dve.wait_ge(sem("lin_qk"), upto(dve, "lin_qk"))
                        dve.tensor_tensor(gl[:, 6], k, gl[:, 6], ALU.mult).then_inc(sem("lin_qk"), tick("lin_qk"))
                        dve.wait_ge(sem("lin_qk"), upto(dve, "lin_qk"))
                    else:
                        for j, (src, dec) in enumerate(((q, ret_q), (k, ret_k))):
                            dve.tensor_tensor(by_tile(gl[:, 5 + j]), by_tile(src),
                                                        dec.unsqueeze(1).to_broadcast([P, NT, P]), ALU.mult).then_inc(sem("lin_qk"), tick("lin_qk"))
                            dve.wait_ge(sem("lin_qk"), upto(dve, "lin_qk"))
                        dve.wait_ge(sem("lvl_a"), upto(dve, "lvl_a", 9))
                        for h in range(4):
                            ins = dve.tensor_tensor(amat[:, h], ps[:, MAIN + h, :].rearrange("p (t n) -> p t n", t=NT),
                                                    ret_d[:, h:h + 1, :].to_broadcast([P, NT, P]), ALU.mult)
                            if h < 3:
                                ins.then_inc(sem("lvl_head"), tick("lvl_head"))
                                dve.wait_ge(sem("lvl_head"), upto(dve, "lvl_head"))
                        ins.then_inc(sem("lvl_kept"), tick("lvl_kept"))
                        dve.wait_ge(sem("lvl_kept"), upto(dve, "lvl_kept"))
                    dve.wait_ge(sem("u_sum"), upto(dve, "u_sum", no + 1))
                    for b in range(2):
                        dve.tensor_tensor(um[:, 2 * b:2 * b + 2], ps[:, b, :].rearrange("p (t n) -> p t n", t=2),
                                                    block_mask.unsqueeze(1).to_broadcast([P, 2, 256]), ALU.mult).then_inc(sem("um"), tick("um"))
                        dve.wait_ge(sem("um"), upto(dve, "um"))
                    for t in (1, 2):
                        dec = gl[:, 4, t * P + P - 1:t * P + P] if no == 0 else ret_c
                        dve.scalar_tensor_tensor(um[:, t], um[:, t - 1], dec, um[:, t], ALU.mult, ALU.add).then_inc(sem("state"), tick("state"))
                        dve.wait_ge(sem("state"), upto(dve, "state"))
                    gate = tm[:, :, p_["gate"]:p_["gate"] + 256]
                    dve.wait_ge(sem("g_exp"), upto(dve, "g_exp", no + 1))
                    dve.tensor_scalar(sig[:], sig[:], 1.0, None, ALU.add).then_inc(sem("silu_sum"), tick("silu_sum"))
                    dve.wait_ge(sem("silu_sum"), upto(dve, "silu_sum"))
                    dve.reciprocal(sig[:], sig[:]).then_inc(sem("silu_sig"), tick("silu_sig"))
                    dve.wait_ge(sem("silu_sig"), upto(dve, "silu_sig"))
                    dve.tensor_tensor(sig[:], sig[:], gate, ALU.mult).then_inc(sem("silu_g"), tick("silu_g"))
                    dve.wait_ge(sem("silu_g"), upto(dve, "silu_g"))
                    dve.wait_ge(sem("o_copied"), upto(dve, "o_copied", 2 * no + 2))
                    dve.tensor_tensor(um[:], o_sb[:], o_sb[:], ALU.mult).then_inc(sem("o_sq"), tick("o_sq"))
                    dve.wait_ge(sem("o_sq"), upto(dve, "o_sq"))
                    ss = stats[:, 64 + 16 * no:80 + 16 * no]
                    dve.tensor_reduce(ss, heads16(um[:], LIN_DV), AX.X, ALU.add).then_inc(sem("o_ss"), tick("o_ss"))
                    dve.wait_ge(sem("o_ss"), upto(dve, "o_ss"))
                    dve.wait_ge(sem("o_rms"), upto(dve, "o_rms", no + 1))
                    oh = heads16(o_sb[:], LIN_DV)
                    dve.tensor_tensor(oh, oh, ss.unsqueeze(2).to_broadcast([P, 16, LIN_DV]), ALU.mult).then_inc(sem("o_scaled"), tick("o_scaled"))
                    dve.wait_ge(sem("o_scaled"), upto(dve, "o_scaled"))
                    dve.tensor_tensor(gate, o_sb[:], sig[:], ALU.mult).then_inc(sem("y_lin"), tick("y_lin"))
                    dve.wait_ge(sem("y_lin"), upto(dve, "y_lin"))

                def y_full(k, dst):
                    dve.wait_ge(sem("y_turned"), upto(dve, "y_turned", k + 1))
                    dve.tensor_scalar(dst, ps[:, MAIN + k % 4, :], g[:, G_OUT + k:G_OUT + k + 1], None, ALU.mult).then_inc(sem("h_full"), tick("h_full"))
                    dve.wait_ge(sem("h_full"), upto(dve, "h_full"))
                parts_dve(dve, PART["y"], y_full, hi, lo, fulls1)
                for m in range(KD):
                    dve.wait_ge(sem("tile_copied"), upto(dve, "tile_copied", 2 * C_OUT + m + 1))
                    dve.tensor_tensor(x_t[:, m], x_t[:, m], tmp[:, m % 2], ALU.add).then_inc(sem("x_mix"), tick("x_mix"))
                    dve.wait_ge(sem("x_mix"), upto(dve, "x_mix"))
                parts_dve(dve, PART["ffn"], normed(dve, xs, col(G_FFN, 8), rms_a[:], 3), hi, lo, fulls1)
                dve.memset(a_pad[:, :, 0:2], 0.0).then_inc(sem("pad"), tick("pad"))
                with dve.Fori(0, KF // 2) as i:
                    for s in range(2):
                        f = 2 * i + s
                        dve.wait_ge(sem("conv0"), upto(dve, "conv0", f + 1))
                        if s == 0:
                            dve.wait_ge(sem("pad"), upto(dve, "pad", 1))
                        for w in (1, 0):
                            dve.scalar_tensor_tensor(conv[:], a_pad[:, s, w:w + S],
                                                                  g[:, bass.ds(G_CONVW + w * KF + f, 1)], conv[:],
                                                                  ALU.mult, ALU.add).then_inc(sem("conv1" if w else "conv"), 1)
                            dve.wait_ge(sem("conv1" if w else "conv"), upto(dve, "conv1" if w else "conv", f + 1))
                        dve.wait_ge(sem("silu"), upto(dve, "silu", f + 1))
                        dve.wait_ge(sem("tile_copied"), upto(dve, "tile_copied", T_UP + 2 * f + 2))
                        dve.tensor_tensor(b_sb[:, s], b_sb[:, s], conv[:], ALU.mult).then_inc(sem("gated"), 1)
                        dve.wait_ge(sem("gated"), upto(dve, "gated", f + 1))
                        dve.wait_ge(sem("hid_hi"), upto(dve, "hid_hi", f + 1))
                        dve.tensor_tensor(hid_lo[:, bass.ds(f, 1), :].rearrange("p a n -> p (a n)"), b_sb[:, s],
                                                       hid_hi[:, bass.ds(f, 1), :].rearrange("p a n -> p (a n)").bitcast(F32),
                                                       ALU.subtract).then_inc(sem("hid_lo"), 1)
                        dve.wait_ge(sem("hid_lo"), upto(dve, "hid_lo", f + 1))
                for n in ("conv1", "conv", "gated", "hid_lo"):
                    count[n] = KF
                with dve.Fori(0, 2) as i:
                    for q in range(2):
                        for half in range(2):
                            j = 2 * q + half
                            dve.wait_ge(sem("tile_copied"), upto(dve, "tile_copied", T_DOWN + 4 * i + j + 1))
                            src = b_sb[:, half] if q == 0 else a_pad[:, half, 0:S]
                            x_m = x_t[:, bass.ds(4 * i + j, 1), :].rearrange("p a n -> p (a n)")
                            dve.tensor_tensor(x_m, x_m, src, ALU.add).then_inc(sem("x_down"), 1)
                            dve.wait_ge(sem("x_down"), upto(dve, "x_down", 4 * i + j + 1))
                count["x_down"] = KD
            end_layer("dve")

            layer[dve] = 2
            att_base.update(dve=0)
            by_class = lambda t: t.rearrange("p (n r) -> p r n", r=RES)
            for k in range(KD):
                if k == 0:
                    dve.wait_ge(sem("rms"), upto(dve, "rms", 1))
                if k > 1:
                    dve.wait_ge(sem("sq"), upto(dve, "sq", 8 + k - 1))
                dve.scalar_tensor_tensor(x1[k % 2].rearrange("p (r n) -> p r n", r=RES), by_class(x_t[:, k]),
                                                   g2[:, k:k + 1], by_class(rms_a[:]), ALU.mult, ALU.mult).then_inc(sem("x1_full"), tick("x1_full"))
                dve.wait_ge(sem("x1_full"), upto(dve, "x1_full"))
            dve.wait_ge(sem("x1"), upto(dve, "x1", 8))
            parts_dve(dve, 0, normed(dve, xs, g2[:, 8:16], rms_a[:], 1), hi, lo, fulls3)

            def branch(b, c0, first):
                def gated(k, dst):
                    dve.wait_ge(sem("tile_copied"), upto(dve, "tile_copied", 2 * c0 + k + 1))
                    dve.wait_ge(sem("o_turned"), upto(dve, "o_turned", 4 * b + k + 1))
                    dve.tensor_tensor(dst, ps[:, 4 + k, :], sgate[:, k], ALU.mult).then_inc(sem("h_full"), tick("h_full"))
                    dve.wait_ge(sem("h_full"), upto(dve, "h_full"))
                parts_dve(dve, first, gated, [gt_hi[:, k] for k in range(4)], [gt_lo[:, k] for k in range(4)], fulls2)
                for m in range(4):
                    for half in range(2):
                        dve.wait_ge(sem("tile_copied"), upto(dve, "tile_copied", 2 * (c0 + 3 + 2 * m) + half + 1))
                        dst = merged[:, 2 * m + half]
                        if b == 0:
                            dve.tensor_tensor(dst, y_br[half], gate_br[half], ALU.mult).then_inc(sem("merged"), tick("merged"))
                            dve.wait_ge(sem("merged"), upto(dve, "merged"))
                        else:
                            dve.tensor_tensor(tmp2[:], y_br[half], gate_br[half], ALU.mult).then_inc(sem("merge_term"), tick("merge_term"))
                            dve.wait_ge(sem("merge_term"), upto(dve, "merge_term"))
                            dve.tensor_tensor(dst, dst, tmp2[:], ALU.add).then_inc(sem("merged"), tick("merged"))
                            dve.wait_ge(sem("merged"), upto(dve, "merged"))

            dve.wait_ge(sem("win_loaded"), 48)
            dve.tensor_copy(win[:], win_in[:]).then_inc(sem("win_cast"), 1)
            dve.wait_ge(sem("win_cast"), 1)
            for hp in range(4):
                for j in range(6):
                    n = 6 * hp + j
                    z = qk[:, hp % 2, j]
                    rope(n, z, ps[:, 4 + j % 4 if hp % 2 == 0 else 4 + (j + 2) % 4, :], a_cos[:], a_sin[:], z, tmp2[:])
                att_dve(dve, a_groups(hp))
            branch(0, C2_GA, 8)
            dve.wait_ge(sem("late_loaded"), 16)
            ax_cos, ax_sin = late[:, 3 * P:3 * P + S], late[:, 3 * P + S:3 * P + 2 * S]
            for j in range(5):
                dve.wait_ge(sem("rms"), upto(dve, "rms", 2 + j + 1))
                z = q_b[:, j]
                dve.scalar_tensor_tensor(z, z, g2[:, 56 + j // 4:57 + j // 4], rms_a[:], ALU.mult, ALU.mult).then_inc(sem("h_norm"), tick("h_norm"))
                dve.wait_ge(sem("h_norm"), upto(dve, "h_norm"))
                rope(24 + j, z, ps[:, 6 + j % 2, :], ax_cos, ax_sin, z, tmp2[:])
            dve.wait_ge(sem("k_spread"), upto(dve, "k_spread", 1))
            for j in range(2):
                dve.tensor_copy(k_b[:, j], ps[:, 4 + j, :]).then_inc(sem("k_b"), tick("k_b"))
                dve.wait_ge(sem("k_b"), upto(dve, "k_b"))
            att_dve(dve, b_groups())
            branch(1, C2_GB, 12)
            parts_dve(dve, 16, normed(dve, [mem_t[:, k] for k in range(KD)], g2[:, 16:24], rms_a[:, 0:N_MEM], 7),
                      [mem_hi[:, k] for k in range(KD)], [mem_lo[:, k] for k in range(KD)], [f[:, 0:N_MEM] for f in fulls2])
            att_dve(dve, m_groups())
            branch(2, C2_GM, 24)
            for k in range(KD):
                dve.wait_ge(sem("h_hi"), upto(dve, "h_hi", 28 + k + 1))
                dve.tensor_tensor(h_lo[:, k], merged[:, k], h_hi[:, k].bitcast(F32), ALU.subtract).then_inc(sem("h_lo"), tick("h_lo"))
                dve.wait_ge(sem("h_lo"), upto(dve, "h_lo"))
            dve.wait_ge(sem("rms"), upto(dve, "rms", 9))
            for k in range(KD):
                dve.scalar_tensor_tensor(out_t[:, k], out_t[:, k], g2[:, 24 + k:25 + k], rms_a[:], ALU.mult, ALU.mult).then_inc(sem("out_scaled"), tick("out_scaled"))
                dve.wait_ge(sem("out_scaled"), upto(dve, "out_scaled"))
                dve.tensor_tensor(out_t[:, k], out_t[:, k], x_t[:, k], ALU.add).then_inc(sem("out_full"), tick("out_full"))
                dve.wait_ge(sem("out_full"), upto(dve, "out_full"))
            end_layer("dve")
        return total


PER_LAYER = {
    "tab_loaded": 16, "stat": 4, "tile_done": 2 * CH_LAYER, "rot": 5, "score": 16, "pt_done": 16, "pv": 16,
    "gate": 1, "lvl_a": 9, "kd_turned": 2, "u_sum": 2, "o_lin": 2, "y_turned": 8, "sq": 21, "log_ms": 4, "rms": 4,
    "h_hi": 29, "tile_copied": TILES_LAYER, "p_exp": 16, "pt_copied": 16, "ymla_log": 1, "ymla_rms": 1, "gk": 1,
    "gate_abs": 1, "gate_exp": 1, "gate_ln": 1, "decay_exp": 2, "lvl_abs": len(LEVELS), "lvl_exp": len(LEVELS),
    "kd_t": 2, "g_exp": 2, "o_copied": 4, "o_log": 2, "o_rms": 2, "held_act": 1, "conv0": KF, "silu": KF,
    "hid_hi": KF, "g": 2, "h_full": 29, "h_lo": 29, "rope_cos": 5, "rope_sin": 5, "roped": 5, "masked": 16,
    "nmax": 16, "rinv": 4, "o_norm": 4, "ymla_sq": 1, "ymla_ss": 1, "reset": 2, "ymla": 1, "amat0": 1,
    "gate_min": 1, "gate_log": 1, "decay_sum": 1, "decay_rest": 1, "lvl_diff": len(LEVELS), "held_dve": 8,
    "lvl_kept": 9, "lvl_q": len(LEVELS), "lvl_k": len(LEVELS), "lin_qk": 4, "um": 4, "state": 4, "silu_sum": 2,
    "silu_sig": 2, "silu_g": 2, "o_sq": 2, "o_ss": 2, "o_scaled": 2, "y_lin": 2, "lvl_head": 3, "x_mix": 8,
    "pad": 1, "conv1": KF, "conv": KF, "gated": KF, "hid_lo": KF, "x_down": 8, "w_split": CH_LAYER,
    "w_high": CH_LAYER, "w_loaded0": 16 * 50, "w_loaded1": 16 * 51,
}


_INS = ["x", "attn_norm", "w_in", "mla_q_norm", "mla_w_uq", "mla_kv_norm", "mla_w_ukv", "mla_out_norm", "gla_w_gate",
        "gla_b_gate", "gla_out_norm", "ret_out_norm", "w_out", "ffn_norm", "ffn_w_up", "ffn_conv_w", "ffn_conv_b",
        "ffn_w_down", "final_norm", "mem_2", "g_pre_2", "w_in_2", "b_merge_2", "q_norm_2", "k_norm_2", "g_mem_2",
        "w_mem_kv_2", "w_br_a_2", "w_br_b_2", "w_br_m_2", "w_out_2", "g_post_2"]


def kernel(**inputs):
    import numpy as _np
    import concourse.bacc as _bacc
    from concourse import mybir as _mybir
    from concourse.bass_utils import run_bass_kernel_spmd as _run

    arrays = {n: _np.ascontiguousarray(inputs[n]) for n in _INS}
    arrays.update(constants())
    nc = _bacc.Bacc("TRN2", target_bir_lowering=False, num_devices=1)
    aps = {n: nc.dram_tensor(f"in_{n}_dram", a.shape, _mybir.dt.from_np(a.dtype), kind="ExternalInput").ap()
           for n, a in arrays.items()}
    out = nc.dram_tensor("out_0_dram", (1, S, D), _mybir.dt.float32, kind="ExternalOutput").ap()
    build(nc, aps, out, PER_LAYER)
    r = _run(nc, [{f"in_{n}_dram": a for n, a in arrays.items()}], core_ids=[0])
    return r.results[0]["out_0_dram"]
```

```python
import math
from collections import defaultdict
from contextlib import ExitStack
from functools import partial

import numpy as np
import concourse.bass as bass
from concourse import mybir

F32 = mybir.dt.float32
F32R = mybir.dt.float32r
BF16 = mybir.dt.bfloat16
U8 = mybir.dt.uint8
ALU = mybir.AluOpType
ACT = mybir.ActivationFunctionType
AX = mybir.AxisListType

P = 128
S = 512
NT = S // P
D = 1024
KD = D // P
DEPTH = 2
EPS = 1e-6
Q_RANK, KV_RANK, ROPE = 384, 256, 64
HEADS, NOPE, VDIM = 4, 128, 128
LIN_DK, LIN_DV = 32, 64
GATE_RANK, GATE_NORM = 16, 16.0
FF = 2816
KF = FF // P
CQ, CKV, KR, GQ, GK, GV, GLR, GG, RQ, RK, RV, RG, Z_END = np.cumsum(
    [0, 384, 256, 64, 128, 128, 256, 16, 256, 128, 128, 256, 256]).tolist()
RES = 4
HD = 64
A_GROUPS, A_HEADS = 3, 8
B_HEADS, B_KV = 8, 2
M_HEADS, N_MEM = 4, 256
AQ, AK, AV, BQ, BK, BV, MQ, GA, GB, GM, MG, IN2 = np.cumsum(
    [0, 1536, 1536, 1536, 512, 128, 128, 512, 512, 512, 512, 3072]).tolist()

CH_Z, CH_UQ, CH_UKV, CH_OUT, CH_UP, CH_DOWN = 9, 3, 4, 4, KF, 12
C_UQ = CH_Z
C_UKV = C_UQ + CH_UQ
C_OUT = C_UKV + CH_UKV
C_UP = C_OUT + CH_OUT
C_DOWN = C_UP + CH_UP
CH_LAYER = C_DOWN + CH_DOWN
DOWN_K = (8, 8, 6)
T_UP, T_DOWN = 2 * C_UP, 2 * C_DOWN
TILES_LAYER = T_DOWN + 8

G_ATTN, G_Q, G_KV, G_FFN, G_CONVW, G_CONVB, G_GATE, G_OUT, G_N = np.cumsum(
    [0, 8, 3, 2, 8, 3 * KF, KF, 1, 8]).tolist()

LEVELS = (64, 32, 16, 8, 4, 2, 1)
CREDIT = {"w_split": 2, "tile_done": 1, "x_down": 1, "sq_sum": KD}


def constants():
    f = np.float32
    eye = np.eye(P, dtype=f)
    idx = np.arange(P)

    def swap(n):
        m = np.zeros((P, P), f)
        m[idx, (idx // n) * n + (idx + n // 2) % n] = 1
        return m

    dup, dup_swap = np.zeros((P, P), f), np.zeros((P, P), f)
    dup[:64, :64] = dup[:64, 64:] = np.eye(64)
    dup_swap[:64, :64] = dup_swap[:64, 64:] = swap(64)[:64, :64]
    sel = [np.zeros((P, P), f) for _ in range(2)]
    for j in range(2):
        sel[j][64 * j:64 * j + 64] = np.concatenate([np.eye(64), np.eye(64)], 1)
    block64 = (idx[:, None] // 64 == idx[None] // 64).astype(f)
    causal = np.where(idx[None] <= idx[:, None], 0, -1e30).astype(f)
    head = idx // LIN_DK
    block = (head[:, None] == (np.arange(256) // LIN_DV)[None]).astype(f)
    log_g = np.log(1.0 - 2.0 ** (-5.0 - np.arange(4, dtype=np.float64)))
    ks = LIN_DK ** -0.5
    dif = idx[None] - idx[:, None]
    dt = np.where(dif[:, None] >= 0, np.exp(log_g[None, :, None] * np.maximum(dif, 0)[:, None]), 0) * ks
    qdec = np.exp(log_g[head][:, None] * (idx + 1.0)[None])
    kdec = np.exp(log_g[head][:, None] * (P - 1.0 - idx)[None]) * ks
    cdec = np.exp(log_g[head] * P)[:, None]

    def table(freq, pos, half):
        ang = (pos.astype(f) * freq.astype(f)[:, None]).astype(f)
        sign = np.where(idx % (2 * half) < half, -1, 1).astype(f)[:, None]
        return np.cos(ang), np.sin(ang) * sign

    t = np.arange(S)
    base = f(10000.0)
    inv64 = base ** (-(np.arange(0, 64, 2, dtype=f) / f(64)))
    inv32 = base ** (-(np.arange(0, 32, 2, dtype=f) / f(32)))
    mc, ms = table(inv64[idx % 32], np.tile(t, (P, 1)), 32)
    rc, rs = table(inv32[idx % 16], np.tile(t, (P, 1)), 16)
    perm = (np.arange(S) % P) * RES + np.arange(S) // P
    pos = np.where((idx % 64 < 32)[:, None], perm[None] // 64, perm[None] % 64)
    ac, as_ = table(inv32[idx % 16], pos, 16)
    a_rope = np.stack([mc[:, perm], ms[:, perm]], 1).astype(f)
    main = np.concatenate([eye, swap(64), swap(32), dup, dup_swap, causal, block, dt.reshape(P, -1), qdec, kdec,
                           cdec], 1).astype(f)
    rope = np.stack([mc, ms, rc, rs], 1).astype(f)
    late = np.concatenate([sel[0], sel[1], block64, ac, as_], 1).astype(f)
    lev = [((idx[:, None] // (2 * s)) == (idx[None] // (2 * s))) & (idx[:, None] % (2 * s) < s) & (idx[None] % (2 * s) >= s)
           for s in LEVELS] + [eye > 0]
    levels = np.stack(lev, 1).astype(f)
    win = np.zeros((P, RES, 768), f)
    for r in range(RES):
        for c in range(RES):
            win[:, r, c * P:c * P + P] = np.abs(RES * (idx[:, None] - idx[None]) + r - c) <= 64
        win[:, r, 512:640] = np.abs(idx[:, None] - idx[None]) <= 64
        win[:, r, 640:768] = (idx[:, None] % 4) == (idx[None] % 4)
    win = np.where(win > 0, 0, -1e30).astype(f)
    return dict(c_main=main, c_rope=rope, c_late=late, c_levels=levels, c_win=win, c_arope=a_rope)


def build(nc, A, out, PER):
    ctx = ExitStack()
    sems = {}

    def sem(name):
        if name not in sems:
            sems[name] = ctx.enter_context(nc.semaphore(name))
        return sems[name]

    with ctx:
        def sb(name, shape, dt=F32):
            return ctx.enter_context(nc.sbuf_tensor(name, shape, dt))

        x_t = sb("x_t", [P, KD, S])
        w_raw = sb("w_raw", [P, 2, 2048])
        w_hi, w_lo = sb("w_hi", [P, 2, 2048], F32R), sb("w_lo", [P, 2, 2048], F32R)
        NMAIN = 6 * P + 256 + 512 + 2 * P + 1
        cm = sb("cm", [P, NMAIN])
        ident, swap64, swap32, dup, dup_swap, causal = (cm[:, i * P:(i + 1) * P] for i in range(6))
        o = 6 * P
        block_mask, o = cm[:, o:o + 256], o + 256
        ret_d, o = cm[:, o:o + 512].rearrange("p (h i) -> p h i", h=4), o + 512
        ret_q, ret_k, ret_c = cm[:, o:o + P], cm[:, o + P:o + 2 * P], cm[:, o + 2 * P:o + 2 * P + 1]
        levels = sb("levels", [P, 8, P], U8)
        ones = sb("ones", [P, P])
        eps = sb("eps", [P, 1])
        gains = sb("gains", [P, DEPTH, G_N])
        g = sb("g", [P, G_N])
        wg_all = sb("wg_all", [P, DEPTH, P])
        wg = sb("wg", [P, P])
        g2 = sb("g2", [P, 8 * 4 + 24 + 2])
        stats = sb("stats", [P, 160])
        rms_a = sb("rms_a", [P, S])
        spare = sb("spare", [P, 8])

        ARENA = (nc.sbuf_base + 63) // 64 * 64
        room = nc.sbuf_usable_end - ARENA

        H_KIB = 32

        def at(name, kib, shape, dt=F32):
            n = int(np.prod(shape[1:])) * (4 if dt in (F32, F32R) else 2)
            assert (kib + H_KIB) * 1024 + n <= room, (name, kib, n, room)
            return nc.alloc_sbuf_tensor_at(name, shape, dt, offset=ARENA + int((kib + H_KIB) * 1024))

        h_hi, h_lo = at("h_hi", -32, [P, KD, S], F32R), at("h_lo", -16, [P, KD, S], F32R)
        levels_in = at("levels_in", 0, [P, 8, P])
        gains_in = at("gains_in", 5, [P, DEPTH, P])
        tm = at("tm", 0, [P, NT, 1024])
        cq = at("cq", 16, [P, 5, S])
        y_mla = at("y_mla", 16, [P, NT, S])
        kg = at("kg", 26, [P, S])
        lin = at("lin", 28, [P, 4, S])
        tab = at("tab", 36, [P, 4, S])
        tmp = at("tmp", 44, [P, 3, S])
        cq_hi, cq_lo = at("cq_hi", 36, [P, 3, S], F32R), at("cq_lo", 16, [P, 3, S], F32R)
        rms_b = at("rms_b", 50, [P, S])
        qn = at("qn", 52, [P, HEADS, S])
        sq2 = at("sq2", 52, [P, 4, S])
        kn = at("kn", 60, [P, HEADS, S])
        v_mla = at("v_mla", 68, [P, NT, S])
        qr = at("qr", 76, [P, 2, S])
        kr = at("kr", 80, [P, S])
        prob = at("prob", 82, [P, 2, 768])
        prob_t = at("prob_t", 88, [P, 2, 768])
        amat = at("amat", 60, [P, 4, NT, P])
        um = at("um", 68, [P, NT, 256])
        o_sb = at("o_sb", 72, [P, NT, 256])
        sig = at("sig", 76, [P, NT, 256])
        kd_t = at("kd_t", 80, [P, NT, P])
        gl = at("gl", 82, [P, 7, S])
        amat_r = at("amat_r", -32, [P, 4, NT, P])
        um_r = at("um_r", -24, [P, NT, 256])
        o_sb_r = at("o_sb_r", -20, [P, NT, 256])
        sig_r = at("sig_r", -16, [P, NT, 256])
        kd_t_r = at("kd_t_r", -12, [P, NT, P])
        qk_r = at("qk_r", -10, [P, 2, S])
        x_in = at("x_in", 52, [P, NT, D])
        sq_in = at("sq_in", 44, [P, S])
        hid_hi, hid_lo = at("hid_hi", 0, [P, KF, S], F32R), at("hid_lo", 44, [P, KF, S], F32R)
        a_pad = at("a_pad", 88, [P, 2, S + 2])
        b_sb = at("b_sb", 92.25, [P, S])
        rms_f = at("rms_f", 94.25, [P, S])
        conv = rms_a
        gt_hi, gt_lo = at("gt_hi", 0, [P, 4, S], F32R), at("gt_lo", 8, [P, 4, S], F32R)
        mem_hi, mem_lo = at("mem_hi", 80, [P, KD, N_MEM], F32R), at("mem_lo", 40, [P, KD, N_MEM], F32R)
        mem_sq = at("mem_sq", 40, [P, KD, N_MEM])
        sq_b = at("sq_b", 80, [P, 5, S])
        sq_2 = at("sq_2", 0, [P, KD, S])
        av = at("av", 16, [P, NT, 1536])
        merged = at("merged", 16, [P, KD, S])
        late = at("late", 32, [P, 3 * P + 2 * S])
        win_in = at("win_in", 0, [P, RES, 768])
        win = at("win", 40, [P, RES, 768], BF16)
        sgates = [at("sgate_a", 40, [P, 4, S]), at("sgate_b", 56, [P, 4, S])]
        sgates.append(sgates[1])
        y_br = at("y_br", 64, [P, 2, S])
        gate_br = at("gate_br", 68, [P, 2, S])
        qk = at("qk", 48, [P, 2, 6, S])
        q_b = at("q_b", 48, [P, 5, S])
        k_b = at("k_b", 60, [P, 2, S])
        v_b = at("v_b", 58, [P, NT, P])
        q_m = at("q_m", 48, [P, 4, S])
        mem_in = at("mem_in", 40, [P, 2, D])
        km = at("km", 32, [P, M_HEADS, N_MEM])
        vm = at("vm", 36, [P, 2, S])
        mem_t = at("mem_t", 64, [P, KD, N_MEM])
        out_t = at("out_t", 48, [P, KD, S])
        o_br = at("o_br", 72, [P, NT, S])
        prob2, prob2_t = at("prob2", 80, [P, 2, 768]), at("prob2_t", 86, [P, 2, 768])
        out_sb = at("out_sb", 72, [P, RES, D])
        tmp2 = at("tmp2", 92, [P, S])
        fulls2 = [at("full0", 90, [P, S])[:], at("full1", 94, [P, S])[:]]
        a_sin, a_cos = at("a_sin", 46, [P, S]), at("a_cos", 94, [P, S])

        ps = ctx.enter_context(nc.psum_tensor("ps", [P, 8, 512], F32))
        MAIN, STAT_BANK = 4, 7

        layer = {}
        count = defaultdict(int)
        total = {}

        def upto(eng, name, k=None):
            k = count[name] if k is None else k
            return layer[eng] * PER.get(name, 0) + CREDIT.get(name, 0) + k

        def tick(name, by=1):
            count[name] += by
            return by

        def end_layer(names):
            for n in list(count):
                total.setdefault(n, count.pop(n))
            count.clear()

        def wsrc(name, l, c0, n, k0=0, k=None):
            a = A[name]
            k = a.shape[1] // P if k is None else k
            return a[bass.ds(l, 1), k0 * P:(k0 + k) * P, c0:c0 + n].rearrange("a (k p) n -> p (a k) n", p=P)

        def layer_chunks(l):
            out = []
            z = lambda *parts: out.append((KD, [(c, wsrc("w_in", l, c0, n)) for c, c0, n in parts]))
            z((0, CKV + P, P + ROPE), (P + ROPE, GLR, GATE_RANK))
            z((0, GQ, P), (P, GK, P))
            z((P, CQ + P, P), (0, CQ, P))
            for c0 in (CQ + 256, GV, GG, RQ, RV, RG):
                z((0, c0, 256))
            q = NOPE + ROPE
            for h in (0, 2):
                out.append((3, [(i * P, wsrc("mla_w_uq", l, (h + i) * q, P)) for i in range(2)]))
            out.append((3, [(h * ROPE, wsrc("mla_w_uq", l, h * q + NOPE, ROPE)) for h in range(4)]))
            for off in (0, NOPE):
                for h in (0, 2):
                    out.append((2, [(i * P, wsrc("mla_w_ukv", l, (h + i) * 256 + off, P)) for i in range(2)]))
            for m in range(4):
                out.append((KD, [(0, wsrc("w_out", l, m * 256, 256))]))
            assert len(out) == C_UP
            return out

        n_dma = [2, 2, 2] + [1] * 6 + [2, 2, 4] + [2] * 4 + [1] * 4 + [2] * (KF + CH_DOWN)

        def two(name, c0, n=256, k0=0, k=None):
            return (k or A[name].shape[1] // P, [(0, wsrc(name, 0, c0, n, k0, k))])

        def second_chunks():
            out = [(KD, [(i * P, wsrc("w_in_2", 0, AV + c0 + i * P, P)) for i in range(2)]) for c0 in (0, 256)]
            out += [two("w_in_2", AV + i * 256) for i in range(2, 6)]
            for hp in range(4):
                for gi in range(A_GROUPS):
                    c0 = (gi * A_HEADS + 2 * hp) * HD
                    out.append((KD, [(0, wsrc("w_in_2", 0, AQ + c0, P)), (P, wsrc("w_in_2", 0, AK + c0, P))]))
            def gate(c0):
                out.extend(two("w_in_2", c0 + i * 256) for i in range(2))

            def merge(br, b):
                for m in range(4):
                    out.append(two("w_in_2", MG + b * D + m * 256))
                    out.append(two(br, m * 256))

            out.extend(two("w_in_2", BQ + i * 256) for i in range(3))
            gate(GA)
            merge("w_br_a_2", 0)
            gate(GB)
            out.extend(two("w_in_2", MQ + i * 256) for i in range(2))
            out.extend(two("w_mem_kv_2", i * 256) for i in range(4))
            merge("w_br_b_2", 1)
            gate(GM)
            merge("w_br_m_2", 2)
            out.extend(two("w_out_2", i * 256) for i in range(4))
            return out

        second = second_chunks()
        C2_QK = 6
        C2_BQ = C2_QK + 12
        C2_GA = C2_BQ + 3
        C2_MA = C2_GA + 2
        C2_GB = C2_MA + 8
        C2_MQ = C2_GB + 2
        C2_KV = C2_MQ + 2
        C2_MB = C2_KV + 4
        C2_GM = C2_MB + 8
        C2_MM = C2_GM + 2
        C2_OUT = C2_MM + 8
        assert len(second) == C2_OUT + 4
        bank2 = [0 if C2_QK + 3 <= t // 2 < C2_GA else
                 (0, 3)[t % 2] if C2_GA <= t // 2 < C2_MQ or C2_MB <= t // 2 < C2_MM else t % 4
                 for t in range(2 * len(second))]
        before2 = [max((u for u in range(t) if bank2[u] == bank2[t]), default=None) for t in range(len(bank2))]

        def slot_view(buf, slot, K):
            return buf[:, slot, 0:K * 256].rearrange("p (k n) -> p k n", n=256)

        att_base = defaultdict(int)

        class Inst:

            def __init__(self, width, score, mask, pv, o_col, o_width):
                self.width, self.score, self.mask, self.pv = width, score, mask, pv
                self.o_col, self.o_width = o_col, o_width

        def mla_groups():
            groups = []
            for t in range(NT):
                insts = []
                for h in range(HEADS):
                    L, lo = (t + 1) * P, 64 * (h % 2)
                    q0 = t * P
                    score = [(0, L, qn[:, h, q0:q0 + P], kn[:, h, 0:L], True, False),
                             (0, L, qr[lo:lo + 64, h // 2, q0:q0 + P], kr[lo:lo + 64, 0:L], False, True)]
                    insts.append(Inst(L, score, (q0, causal), [v_mla[:, k, h * P:h * P + P] for k in range(t + 1)],
                                      h * VDIM, VDIM))
                groups.append((insts, y_mla[:, t, :].rearrange("p (h d) -> p h d", h=HEADS)))
            return groups

        def a_groups(hp):
            groups = []
            buf = qk[:, hp % 2]
            for hh in range(2):
                lo, head = 64 * hh, 2 * hp + hh
                insts = []
                for r in range(RES):
                    q = [buf[lo:lo + 64, 2 * gi, r * P:r * P + P] for gi in range(3)]
                    k = [buf[lo:lo + 64, 2 * gi + 1, :] for gi in range(3)]
                    score = [(0, S, q[0], k[0], True, True),
                             (512, P, q[1], k[1][:, r * P:r * P + P], True, True),
                             (640, P, q[2], k[2][:, r * P:r * P + P], True, True)]
                    vcol = lambda gi: slice((gi * A_HEADS + head) * HD, (gi * A_HEADS + head + 1) * HD)
                    pv = [av[:, c, vcol(0)] for c in range(RES)] + [av[:, r, vcol(1)], av[:, r, vcol(2)]]
                    insts.append(Inst(768, score, (0, win[:, r, :]), pv, HD * r, HD))
                groups.append((insts, o_br[:, :, head * HD:head * HD + HD]))
            return groups

        def b_groups():
            groups = []
            for r in range(RES):
                insts = []
                for h in range(B_HEADS):
                    lo, j = 64 * (h % 2), h // (B_HEADS // B_KV)
                    score = [(0, S, q_b[lo:lo + 64, h // 2, r * P:r * P + P], k_b[lo:lo + 64, j, :], True, True)]
                    insts.append(Inst(S, score, None, [v_b[:, c, j * HD:j * HD + HD] for c in range(RES)], h * HD, HD))
                groups.append((insts, o_br[:, r, :].rearrange("p (h d) -> p h d", h=B_HEADS)))
            return groups

        def m_groups():
            groups = []
            for r in range(RES):
                insts = []
                for h in range(M_HEADS):
                    score = [(0, N_MEM, q_m[:, h, r * P:r * P + P], km[:, h, :], True, True)]
                    insts.append(Inst(N_MEM, score, None, [vm[:, c, h * P:h * P + P] for c in range(2)], h * P, P))
                groups.append((insts, o_br[:, r, :].rearrange("p (h d) -> p h d", h=M_HEADS)))
            return groups

        T_BANK, O_BANK = 2, 1
        RET_BANKS = (0, 3, 7, 0)

        def score_banks(insts):
            return (4, 5, 6) if max(i.width for i in insts) <= 512 else (4, 6)

        def score_ps(banks, i, c0, n):
            b = banks[i % len(banks)] + c0 // 512
            c = c0 % 512
            return ps[:, b, c:c + n]

        def wide_ps(bank, n):
            return ps[:, bank:bank + 2, :].rearrange("p b n -> p (b n)")[:, 0:n]

        def att_pe(pe, groups, probs, probs_t, fill={}, early={}):
            base, obase = att_base["pe"], att_base["pe_o"]
            insts = [i for g_, _ in groups for i in g_]
            banks = score_banks(insts)
            ahead = len(banks) - 1
            size = len(groups[0][0])

            def scores(i):
                for c0, n, lhs, rhs, a, b in insts[i].score:
                    ins = pe.matmul(score_ps(banks, i, c0, n), lhs, rhs, start=a, stop=b)
                ins.then_inc(sem("score"), tick("score"))

            def turn(i):
                pe.wait_ge(sem("p_exp"), upto(pe, "p_exp", base + i + 1))
                if base + i:
                    pe.wait_ge(sem("pt_copied"), upto(pe, "pt_copied", base + i))
                for k in range(len(insts[i].pv)):
                    c = k * P
                    ins = pe.transpose(ps[:, T_BANK + c // 512, c % 512:c % 512 + P],
                                       probs[:, i % 2, c:c + P], ident)
                ins.then_inc(sem("pt_done"), tick("pt_done"))

            def values(i):
                pe.wait_ge(sem("pt_copied"), upto(pe, "pt_copied", base + i + 1))
                if i % size == 0 and obase + i // size:
                    pe.wait_ge(sem("o_norm"), upto(pe, "o_norm", obase + i // size))
                it = insts[i]

                for k, v in enumerate(it.pv):
                    ins = pe.matmul(ps[:, O_BANK, it.o_col:it.o_col + it.o_width], probs_t[:, i % 2, k * P:k * P + P], v,
                                    start=(k == 0), stop=(k == len(it.pv) - 1))
                ins.then_inc(sem("pv"), tick("pv"))

            n = len(insts)
            for i in range(ahead):
                scores(i)
            for i in range(n):
                if i + ahead < n:
                    scores(i + ahead)
                if i in early:
                    early[i]()
                turn(i)
                if i:
                    values(i - 1)
                if i in fill:
                    fill[i]()
            values(n - 1)
            att_base["pe"] += n
            att_base["pe_o"] += len(groups)

        def att_act(act, groups, pr, pt, fill={}):
            base = att_base["act"]
            insts = [i for g_, _ in groups for i in g_]
            banks = score_banks(insts)

            def copy(i):
                n = len(insts[i].pv) * P
                act.wait_ge(sem("pt_done"), upto(act, "pt_done", base + i + 1))
                act.activation(pt[:, i % 2, 0:n], wide_ps(T_BANK, n), ACT.Copy).then_inc(sem("pt_copied"), tick("pt_copied"))
                act.wait_ge(sem("pt_copied"), upto(act, "pt_copied"))

            for i, it in enumerate(insts):
                act.wait_ge(sem("nmax"), upto(act, "nmax", base + i + 1))
                c = i % 16
                act.activation(pr[:, i % 2, 0:it.width], wide_ps(banks[i % len(banks)], it.width), ACT.Exp,
                                         bias=stats[:, c:c + 1], accum_out=stats[:, 16 + c:17 + c]).then_inc(sem("p_exp"), tick("p_exp"))
                act.wait_ge(sem("p_exp"), upto(act, "p_exp"))
                if i:
                    copy(i - 1)
                    if i - 1 in fill:
                        fill[i - 1]()
            copy(len(insts) - 1)
            if len(insts) - 1 in fill:
                fill[len(insts) - 1]()
            att_base["act"] += len(insts)

        def att_dve(dve, groups, fill={}):
            base = att_base["dve"]
            insts = [i for g_, _ in groups for i in g_]
            banks = score_banks(insts)
            size = len(groups[0][0])

            def norm(q):
                dve.wait_ge(sem("pv"), upto(dve, "pv", base + (q + 1) * size))
                c = 16 + (q * size) % 16
                r = stats[:, 32:32 + size]
                dve.reciprocal(r, stats[:, c:c + size]).then_inc(sem("rinv"), tick("rinv"))
                dve.wait_ge(sem("rinv"), upto(dve, "rinv"))
                it = groups[q][0][0]
                src = ps[:, O_BANK, it.o_col:it.o_col + size * it.o_width].rearrange("p (h d) -> p h d", h=size)
                dve.tensor_tensor(groups[q][1], src, r.unsqueeze(2).to_broadcast([P, size, it.o_width]),
                                            ALU.mult).then_inc(sem("o_norm"), tick("o_norm"))
                dve.wait_ge(sem("o_norm"), upto(dve, "o_norm"))

            for i, it in enumerate(insts):
                dve.wait_ge(sem("score"), upto(dve, "score", base + i + 1))
                if it.mask is not None:
                    c0, table = it.mask
                    n = table.shape[-1]
                    part = wide_ps(banks[i % len(banks)], c0 + n)[:, c0:c0 + n]
                    dve.tensor_tensor(part, part, table, ALU.add).then_inc(sem("masked"), tick("masked"))
                    dve.wait_ge(sem("masked"), upto(dve, "masked"))
                c = i % 16
                dve.tensor_reduce(stats[:, c:c + 1], wide_ps(banks[i % len(banks)], it.width), AX.X, ALU.max,
                                            negate=True).then_inc(sem("nmax"), tick("nmax"))
                dve.wait_ge(sem("nmax"), upto(dve, "nmax"))
                if i - 2 in fill:
                    fill[i - 2]()
                if i % size == 1 and i > 1:
                    norm(i // size - 1)
            norm(len(groups) - 1)
            for i in (len(insts) - 2, len(insts) - 1):
                if i in fill:
                    fill[i]()
            att_base["dve"] += len(insts)

        def tiles_of(t):
            return [t[:, k] for k in range(t.shape[1])]

        def norm_sq(act, tiles, buf):
            for k, t in enumerate(tiles):
                act.activation(buf[k], t, ACT.Square).then_inc(sem("sq"), tick("sq"))
                act.wait_ge(sem("sq"), upto(act, "sq"))

        def norm_stat(pe, first, tiles, bank, weights=None):
            for i, t in enumerate(tiles):
                pe.wait_ge(sem("sq"), upto(pe, "sq", first + i + 1))
                n = t.shape[-1]
                ins = pe.matmul(ps[:, bank, 0:n], weights if weights is not None else ones[:, :], t,
                                start=(i == 0), stop=(i == len(tiles) - 1))
            ins.then_inc(sem("stat"), tick("stat"))

        def sum_stat(pe, k):
            pe.wait_ge(sem("sq_sum"), upto(pe, "sq_sum", k))
            pe.matmul(ps[:, STAT_BANK, :], ones[:, :], rms_a[:], start=True, stop=True).then_inc(sem("stat"), tick("stat"))

        def norm_factor(act, first, bank, dim, dst):
            act.wait_ge(sem("stat"), upto(act, "stat", first + 1))
            n = dst.shape[-1]
            act.activation(dst, ps[:, bank, 0:n], ACT.Ln, bias=eps[:, 0:1], scale=1.0 / dim).then_inc(sem("log_ms"), tick("log_ms"))
            act.wait_ge(sem("log_ms"), upto(act, "log_ms"))
            act.activation(dst, dst, ACT.Exp, scale=-0.5).then_inc(sem("rms"), tick("rms"))
            act.wait_ge(sem("rms"), upto(act, "rms"))

        def parts_act(act, first, hi, fulls):
            for k, t in enumerate(hi):
                act.wait_ge(sem("h_full"), upto(act, "h_full", first + k + 1))
                act.activation(t, fulls[k % 2], ACT.Copy).then_inc(sem("h_hi"), tick("h_hi"))
                act.wait_ge(sem("h_hi"), upto(act, "h_hi"))

        def parts_dve(dve, first, full, hi, lo, fulls):
            n = len(lo)

            def low(k):
                dve.wait_ge(sem("h_hi"), upto(dve, "h_hi", first + k + 1))
                dve.tensor_tensor(lo[k], fulls[k % 2], hi[k].bitcast(F32), ALU.subtract).then_inc(sem("h_lo"), tick("h_lo"))
                dve.wait_ge(sem("h_lo"), upto(dve, "h_lo"))

            for k in range(n):
                full(k, fulls[k % 2])
                if k:
                    low(k - 1)
            low(n - 1)

        def normed(dve, tiles, gain, factor, stat_no):
            def full(k, dst):
                if k == 0:
                    dve.wait_ge(sem("rms"), upto(dve, "rms", stat_no + 1))
                dve.scalar_tensor_tensor(dst, tiles[k], gain[:, k:k + 1], factor, ALU.mult, ALU.mult).then_inc(sem("h_full"), tick("h_full"))
                dve.wait_ge(sem("h_full"), upto(dve, "h_full"))
            return full

        def product(pe, dst, lhs, rhs, order, first=True, last=True, ready=None):
            for j, k in enumerate(order):
                (lh, ll), (rh, rl) = lhs(k), rhs(k)
                if ready is not None:
                    pe.wait_ge(sem("h_lo"), upto(pe, "h_lo", ready + j + 1))
                pe.matmul(dst, lh, rh, start=first and j == 0, stop=False)
                pe.matmul(dst, lh, rl, start=False, stop=False)
                ins = pe.matmul(dst, ll, rh, start=False, stop=last and j == len(order) - 1)
            return ins

        def features(pe, slot, half, K, hi, lo, bank, cols=P, n=S, k0=0, first=True, last=True, ready=None, order=None):
            wh, wl = slot_view(w_hi, slot, K), slot_view(w_lo, slot, K)
            c = slice(half * P, half * P + cols)
            return product(pe, ps[0:cols, bank, 0:n], lambda k: (wh[:, k, c], wl[:, k, c]),
                           lambda k: (hi[:, k0 + k, :], lo[:, k0 + k, :]), order or range(K), first, last, ready)

        def two_tiles(pe, slot, K, hi, lo, banks, widths, ready, order=None):
            wh, wl = slot_view(w_hi, slot, K), slot_view(w_lo, slot, K)
            order = order or range(K)
            for j, k in enumerate(order):
                pe.wait_ge(sem("h_lo"), upto(pe, "h_lo", ready + j + 1))
                for half in range(2):
                    c, dst = slice(half * P, half * P + widths[half]), ps[0:widths[half], banks[half], :]
                    last = j == len(order) - 1
                    pe.matmul(dst, wh[:, k, c], hi[:, k, :], start=j == 0, stop=False)
                    pe.matmul(dst, wh[:, k, c], lo[:, k, :], start=False, stop=False)
                    ins = pe.matmul(dst, wl[:, k, c], hi[:, k, :], start=False, stop=last)
                    if last:
                        ins.then_inc(sem("tile_done"), tick("tile_done"))

        def tokens(pe, slot, half, K, hi, lo, bank, tiles=(0, 1), c0=0, n=256, ready=None):
            wh, wl = slot_view(w_hi, slot, K), slot_view(w_lo, slot, K)
            for j, t in enumerate(tiles):
                ins = product(pe, ps[:, bank, j * n:j * n + n],
                              lambda k: (hi[:, k, t * P:t * P + P], lo[:, k, t * P:t * P + P]),
                              lambda k: (wh[:, k, c0:c0 + n], wl[:, k, c0:c0 + n]), range(K),
                              ready=ready if j == 0 else None)
            return ins

        FILL_B = {k * 32 // 12: k + 4 for k in range(12)}
        FILL_M = {k: k for k in range(16)}

        sq_c = tiles_of(sq2) + [tmp[:, 2]]
        norm_tiles = {"x": (0, 8, 0), "q": (8, 3, 1), "kv": (11, 2, 2), "ffn": (13, 8, 3)}
        Y_ORDER = (4, 5, 6, 7, 0, 1, 2, 3)
        Z_KIND = "ffffttftt"
        PART = {"x": 0, "q": 8, "kv": 11, "y": 13, "ffn": 21}
        col = lambda c, n: g[:, c:c + n]
        fulls1 = [tmp[:, 0], tmp[:, 1]]
        x1 = [qk[:, j // 6, j % 6] for j in range(KD)]
        fulls3 = [qk[:, 1, 2], qk[:, 1, 3]]
        heads16 = lambda t, d: t.rearrange("p t (h d) -> p (t h) d", d=d)

        block = ctx.enter_context(nc.Block())
        LIN = {"gla": dict(q=0, k=1, v=0, gate=256, col=16), "ret": dict(q=2, k=3, v=512, gate=768, col=48)}

        GAINS = (("attn_norm", G_ATTN, 8), ("mla_q_norm", G_Q, 3), ("mla_kv_norm", G_KV, 2), ("ffn_norm", G_FFN, 8),
                 ("ffn_conv_b", G_CONVB, KF), ("gla_b_gate", G_GATE, 1), ("mla_out_norm", G_OUT, 4),
                 ("gla_out_norm", G_OUT + 4, 2), ("ret_out_norm", G_OUT + 6, 2))

        @block.sync
        def _(sp):
            sp.dma_start(cm[:, 0:P], A["c_main"][:, 0:P]).then_inc(sem("init_i"), 16)
            for t in range(NT):
                sp.dma_start(x_in[:, t], A["x"][0, t * P:t * P + P]).then_inc(sem("init_x"), 16)
            for name, c0, k in GAINS:
                sp.dma_start(gains_in[c0:c0 + k], A[name].rearrange("l (k p) -> k l p", p=P)).then_inc(sem("init_gain"), 16)
            sp.dma_start(gains_in[G_CONVW:G_CONVB],
                         A["ffn_conv_w"].rearrange("l w (k p) -> (w k) l p", p=P)).then_inc(sem("init_gain"), 16)
            sp.dma_start(cm[:, P:], A["c_main"][:, P:]).then_inc(sem("init_c"), 16)
            sp.dma_start(levels_in[:], A["c_levels"]).then_inc(sem("init_c"), 16)

            def load(c, slot, parts, K):
                sp.wait_ge(sem("w_split"), upto(sp, "w_split", c - 1))
                for c0, src in parts:
                    n = src.shape[-1]
                    sp.dma_start(slot_view(w_raw, slot, K)[:, :, c0:c0 + n], src).then_inc(sem(f"w_loaded{slot}"), 16)

            with sp.Fori(0, DEPTH) as l:
                layer[sp] = l
                for c, (K, parts) in enumerate(layer_chunks(l)):
                    load(c, c % 2, parts, K)
                    if c == C_OUT - 1:
                        sp.wait_ge(sem("tile_done"), upto(sp, "tile_done", 2 * C_UKV))
                        sp.dma_start(tab[:], A["c_rope"]).then_inc(sem("tab_loaded"), tick("tab_loaded", 16))
                with sp.Fori(0, KF // 2) as i:
                    for s in range(2):
                        f = 2 * i + s
                        sp.wait_ge(sem("w_split"), upto(sp, "w_split", C_UP + f - 1))
                        for half in range(2):
                            src = A["ffn_w_up"][bass.ds(l, 1), :, bass.ds(f * P + half * FF, P)]
                            sp.dma_start(slot_view(w_raw, s, KD)[:, :, half * P:half * P + P],
                                         src.rearrange("a (k p) n -> p (a k) n", p=P)).then_inc(sem(f"w_loaded{s}"), 16)
                with sp.Fori(0, 2) as i:
                    for j in range(6):
                        m, kg = 2 * i + j // 3, j % 3
                        sp.wait_ge(sem("w_split"), upto(sp, "w_split", C_DOWN + 6 * i + j - 1))
                        K = DOWN_K[kg]
                        for k0 in (0, K // 2):
                            src = A["ffn_w_down"][bass.ds(l, 1), (8 * kg + k0) * P:(8 * kg + k0 + K // 2) * P, bass.ds(m * 256, 256)]
                            sp.dma_start(slot_view(w_raw, j % 2, K)[:, k0:k0 + K // 2, :],
                                         src.rearrange("a (k p) n -> p (a k) n", p=P)).then_inc(sem(f"w_loaded{j % 2}"), 16)
            end_layer("sp")
            layer[sp] = 2
            for c, (K, parts) in enumerate(second):
                if c == C2_QK:
                    sp.wait_ge(sem("stat"), upto(sp, "stat", 2))
                    sp.dma_start(win_in[:], A["c_win"]).then_inc(sem("win_loaded"), 16)
                    sp.dma_start(a_cos[:], A["c_arope"][:, 0]).then_inc(sem("win_loaded"), 16)
                    sp.dma_start(a_sin[:], A["c_arope"][:, 1]).then_inc(sem("win_loaded"), 16)
                if c == C2_MA:
                    sp.wait_ge(sem("pv"), upto(sp, "pv", 32))
                    sp.dma_start(late[:], A["c_late"]).then_inc(sem("late_loaded"), 16)
                if c == C2_GB:
                    sp.wait_ge(sem("h_lo"), upto(sp, "h_lo", 12))
                    sp.dma_start(mem_in[:], A["mem_2"][0].rearrange("(t p) d -> p t d", p=P)).then_inc(sem("mem_loaded"), 16)
                load(c, c % 2, parts, K)
            for r in range(RES):
                sp.wait_ge(sem("out_copied"), upto(sp, "out_copied", 2 * r + 2))
                sp.dma_start(out[0].rearrange("(n r) d -> r n d", r=RES)[r], out_sb[:, r]).then_inc(sem(f"out_stored{r % 2}"), 16)
            for r in range(2):
                sp.wait_ge(sem(f"out_stored{r}"), 16 * RES // 2)
            end_layer("sp")

        @block.gpsimd
        def _(pool):
            pool.memset(slot_view(w_raw, 0, KD)[:, :, P + ROPE + GATE_RANK:256], 0.0).then_inc(sem("w_split"), 1)
            pool.memset(ones[:], 1.0).then_inc(sem("w_split"), 1)
            pool.wait_ge(sem("w_split"), 2)
            with nc.allow_non_contiguous_dma("gains go one to a partition"):
                pool.dma_start(wg_all[64:64 + GATE_RANK], A["gla_w_gate"].rearrange("l r n -> r l n")).then_inc(sem("init_g"), 16)
                for c0, k, src in ((0, 8, A["final_norm"]), (8, 8, A["g_pre_2"][0]), (16, 8, A["g_mem_2"][0]),
                                   (24, 8, A["g_post_2"][0]), (32, 24, A["b_merge_2"][0])):
                    pool.dma_start(g2[:, c0:c0 + k], src.rearrange("(k p) -> p k", p=P)).then_inc(sem("init_g"), 16)
                for c, name in ((56, "q_norm_2"), (57, "k_norm_2")):
                    for half in range(2):
                        pool.dma_start(g2[64 * half:64 * half + 64, c:c + 1],
                                       A[name][0].rearrange("(p k) -> p k", k=1)).then_inc(sem("init_g"), 16)

            def split(c, slot, K):
                n = K * 256
                pool.wait_ge(sem("w_high"), upto(pool, "w_high", c + 1))
                pool.tensor_tensor(w_lo[:, slot, 0:n], w_raw[:, slot, 0:n], w_hi[:, slot, 0:n].bitcast(F32),
                                   ALU.subtract).then_inc(sem("w_split"), 1)

            with pool.Fori(0, DEPTH) as l:
                layer[pool] = l
                for c, (K, _) in enumerate(layer_chunks(0)):
                    split(c, c % 2, K)
                with pool.Fori(0, KF // 2) as i:
                    for q in range(2):
                        split(C_UP + 2 * i + q, q, KD)
                with pool.Fori(0, 2) as i:
                    for j in range(6):
                        split(C_DOWN + 6 * i + j, j % 2, DOWN_K[j % 3])
            layer[pool] = 2
            for c, (K, _) in enumerate(second):
                split(c, c % 2, K)
                if c == 1:
                    for k in range(KD):
                        pool.wait_ge(sem("x1_full"), upto(pool, "x1_full", k + 1))
                        pool.tensor_copy(x_t[:, k], x1[k]).then_inc(sem("x1"), tick("x1"))

        @block.tensor
        def _(pe):
            def split_ready(c):
                pe.wait_ge(sem("w_split"), upto(pe, "w_split", c + 1))

            def bank_free(t):
                if not isinstance(t, int) or t > 3:
                    pe.wait_ge(sem("tile_copied"), upto(pe, "tile_copied", t - 3))

            def tile(t, K, hi, lo, kind="f", width=P, **kw):
                c, half = t // 2, t % 2
                if half == 0:
                    split_ready(c)
                bank_free(t)
                if kind == "f":
                    ins = features(pe, c % 2, half, K, hi, lo, t % 4, width, **kw)
                else:
                    ins = tokens(pe, c % 2, half, K, hi, lo, t % 4, (2 * half, 2 * half + 1))
                ins.then_inc(sem("tile_done"), tick("tile_done"))

            pe.wait_ge(sem("init_i"), 16)
            pe.wait_ge(sem("init_x"), 16 * NT)
            pe.wait_ge(sem("w_split"), 2)
            for k in range(KD):
                if k > 3:
                    pe.wait_ge(sem("init_xt"), k - 3)
                for t in range(NT):
                    ins = pe.transpose(ps[:, MAIN + k % 4, t * P:t * P + P], x_in[:, t, k * P:k * P + P], ident)
                ins.then_inc(sem("init_turn"), 1)
            pe.wait_ge(sem("init_gain"), 16 * (len(GAINS) + 1))
            for l in range(DEPTH):
                pe.transpose(ps[:, l, 0:G_N], gains_in[0:G_N, l, :], ident[0:G_N, 0:G_N]).then_inc(sem("gains_turned"), 1)
            pe.matmul(ps[0:1, 2, 0:1], ones[:, 0:1], ones[:, 0:1], start=True, stop=True).then_inc(sem("tile_done"), 1)

            with pe.Fori(0, DEPTH) as l:
                layer[pe] = l
                att_base.update(pe=0, pe_o=0)
                sum_stat(pe, 0)

                def pairs(q, k, banks, heads=range(4)):
                    for t in range(NT):
                        c = slice(t * P, t * P + P)
                        for h, b in zip(heads, banks):
                            r = slice(LIN_DK * h, LIN_DK * h + LIN_DK)
                            ins = pe.matmul(ps[:, b, c], k[r, c], q[r, c], start=True, stop=True,
                                            tile_position=(LIN_DK * h, 0))
                    ins.then_inc(sem("lvl_a"), tick("lvl_a"))

                def lin_turn(no, k, bank):
                    pe.wait_ge(sem("lin_qk"), upto(pe, "lin_qk", 2 * no + 2))
                    for t in range(NT):
                        ins = pe.transpose(ps[:, bank, t * P:t * P + P], k[:, t * P:t * P + P], ident)
                    ins.then_inc(sem("kd_turned"), tick("kd_turned"))

                def lin_update(no, kd, v, banks):
                    pe.wait_ge(sem("kd_t"), upto(pe, "kd_t", no + 1))
                    for t in range(NT):
                        ins = pe.matmul(ps[:, banks[t // 2], t % 2 * 256:t % 2 * 256 + 256], kd[:, t, :], tm[:, t, v:v + 256],
                                        start=True, stop=True)
                    ins.then_inc(sem("u_sum"), tick("u_sum"))

                def lin_out(no, q, a, u, v, banks, tiles):
                    pe.wait_ge(sem("state"), upto(pe, "state", 2 * no + 2))
                    pe.wait_ge(sem("lvl_kept"), upto(pe, "lvl_kept", 8 + no))
                    for t in tiles:
                        b, c0 = banks[t // 2], t % 2 * 256
                        if t:
                            pe.matmul(ps[:, b, c0:c0 + 256], q[:, t * P:t * P + P], u[:, t - 1, :],
                                      start=True, stop=False, skip_group_check=True)
                        for h in range(4):
                            ins = pe.matmul(ps[:, b, c0 + h * 64:c0 + h * 64 + 64], a[:, h, t, :],
                                            tm[:, t, v + h * 64:v + h * 64 + 64],
                                            start=(t == 0), stop=(t == 0 or h == 3), skip_group_check=True)
                    ins.then_inc(sem("o_lin"), tick("o_lin"))

                for t in range(2 * CH_Z):
                    kind = "t" if Z_KIND[t // 2] == "t" else "f"
                    if t == 0:
                        split_ready(0)
                        bank_free(0)
                        bank_free(1)
                        two_tiles(pe, 0, KD, h_hi, h_lo, (0, 1), (P, ROPE + GATE_RANK), PART["x"])
                    elif t > 1:
                        tile(t, KD, h_hi, h_lo, kind)
                    if t == 2:
                        pe.wait_ge(sem("tile_copied"), upto(pe, "tile_copied", 2))
                        pe.matmul(ps[:, 6, :], wg[64:64 + GATE_RANK, :], kg[64:64 + GATE_RANK, :], start=True,
                                  stop=True).then_inc(sem("gate"), tick("gate"))
                    if t == 4:
                        pe.wait_ge(sem("gk"), upto(pe, "gk", 1))
                        pe.wait_ge(sem("tile_copied"), upto(pe, "tile_copied", 4))
                        pairs(lin[:, 0], lin[:, 1], (4, 5, 6, 7))
                    if 6 <= t < 6 + len(LEVELS):
                        pe.wait_ge(sem("lvl_kept"), upto(pe, "lvl_kept", t - 5))
                        pe.wait_ge(sem("lvl_k"), upto(pe, "lvl_k", t - 5))
                        pairs(gl[:, 2], gl[:, 3], (4, 5, 6, 7))
                    if t == 13:
                        pe.wait_ge(sem("lvl_kept"), upto(pe, "lvl_kept", 8))
                        lin_turn(0, gl[:, 6], 4)
                        norm_stat(pe, 0, sq_c[0:3], 7)
                    if t == 14:
                        lin_update(0, kd_t, LIN["gla"]["v"], (5, 6))
                    if t == 16:
                        pe.wait_ge(sem("log_ms"), upto(pe, "log_ms", 2))
                        for half in range(2):
                            lin_out(0, gl[:, 5], amat, um, LIN["gla"]["v"], (7, 4), (2 * half, 2 * half + 1))
                norm_stat(pe, 3, sq_c[3:5], 5)
                pe.wait_ge(sem("h_lo"), upto(pe, "h_lo", PART["q"] + 3))
                for t in range(2 * C_UQ, 2 * C_UKV):
                    tile(t, 3, cq_hi, cq_lo)
                pe.wait_ge(sem("h_lo"), upto(pe, "h_lo", PART["kv"] + 2))
                kv_hi, kv_lo = h_hi[:, 3:5, :], h_lo[:, 3:5, :]
                for t in range(2 * C_UKV, 2 * C_OUT):
                    tile(t, 2, kv_hi, kv_lo, "f" if t < 2 * C_UKV + 4 else "t")
                    if t == 2 * C_UKV + 1:
                        pe.wait_ge(sem("o_copied"), upto(pe, "o_copied", 2))
                        pe.wait_ge(sem("tile_copied"), upto(pe, "tile_copied", 2 * C_UKV))
                        pe.matmul(ps[:, 4, :], dup_swap[0:64, :], kg[0:64, :], start=True, stop=True)
                        pe.matmul(ps[:, 7, :], dup[0:64, :], kg[0:64, :], start=True, stop=True).then_inc(sem("rot"), tick("rot"))
                        for j in range(2):
                            pe.matmul(ps[:, 5 + j, :], swap64, qr[:, j, :], start=True, stop=True).then_inc(sem("rot"), tick("rot"))
                pe.wait_ge(sem("tile_copied"), upto(pe, "tile_copied", 2 * C_OUT))
                pe.wait_ge(sem("roped"), upto(pe, "roped", 3))

                def ret_halves():
                    for j in range(2):
                        pe.matmul(ps[:, 3 * j, :], swap32, lin[:, 2 + j, :], start=True, stop=True).then_inc(sem("rot"), tick("rot"))

                def ret_pairs(first):
                    if first == 0:
                        pe.wait_ge(sem("roped"), upto(pe, "roped", 5))
                    else:
                        pe.wait_ge(sem("lvl_head"), upto(pe, "lvl_head", 1))
                    pairs(lin[:, 2], lin[:, 3], RET_BANKS[first:first + 2], (first, first + 1))

                def ret_turn():
                    pe.wait_ge(sem("lvl_kept"), upto(pe, "lvl_kept", 9))
                    lin_turn(1, qk_r[:, 1], 0)

                def ret_update():
                    lin_update(1, kd_t_r, LIN["ret"]["v"], (3, 7))

                def ret_out(half):
                    lin_out(1, qk_r[:, 0], amat_r, um_r, LIN["ret"]["v"], (0, 3), (2 * half, 2 * half + 1))

                att_pe(pe, mla_groups(), prob, prob_t, fill={0: ret_halves, 2: partial(ret_pairs, 0), 4: partial(ret_pairs, 2), 7: ret_turn,
                                                            9: ret_update, 11: partial(ret_out, 0), 12: partial(ret_out, 1)})

                W_OUT_BANKS = (2 * C_OUT % 4, 2 * C_OUT % 4 + 1)
                for j, k in enumerate(Y_ORDER):
                    if j == 0:
                        pe.wait_ge(sem("y_lin"), upto(pe, "y_lin", 2))
                    if k == 0:
                        pe.wait_ge(sem("ymla"), upto(pe, "ymla", 1))
                    if j > 3:
                        pe.wait_ge(sem("h_lo"), upto(pe, "h_lo", PART["y"] + j - 3))
                    for t in range(NT):
                        src = (y_mla[:, t, k * P:k * P + P] if k < 4 else
                               tm[:, t, 256 + (k - 4) * P:256 + (k - 3) * P] if k < 6 else
                               tm[:, t, 768 + (k - 6) * P:768 + (k - 5) * P])
                        ins = pe.transpose(ps[:, MAIN + j % 4, t * P:t * P + P], src, ident)
                    ins.then_inc(sem("y_turned"), tick("y_turned"))
                split_ready(C_OUT)
                two_tiles(pe, C_OUT % 2, KD, h_hi, h_lo, W_OUT_BANKS, (P, P), PART["y"], Y_ORDER)
                for t in range(2 * C_OUT + 2, 2 * C_UP):
                    tile(t, KD, h_hi, h_lo)
                sum_stat(pe, 8)
                with pe.Fori(0, KF // 2) as i:
                    for s in range(2):
                        c = C_UP + 2 * i + s
                        split_ready(c)
                        for half in range(2):
                            bank_free(2 * c + half)
                            features(pe, s, half, KD, h_hi, h_lo, 2 * s + half,
                                     ready=PART["ffn"] if s + half == 0 else None).then_inc(sem("tile_done"), 1)
                count["tile_done"] = 2 * C_DOWN
                with pe.Fori(0, 2) as i:
                    for q in range(2):
                        for part, K in enumerate(DOWN_K):
                            j = 3 * q + part
                            split_ready(C_DOWN + 6 * i + j)
                            pe.wait_ge(sem("hid_lo"), upto(pe, "hid_lo", 8 * part + K))
                            for half in range(2):
                                if part == 0:
                                    pe.wait_ge(sem("tile_copied"), upto(pe, "tile_copied", T_DOWN + 4 * i + 2 * q + half - 3))
                                features(pe, j % 2, half, K, hid_hi, hid_lo, 2 * q + half, k0=8 * part,
                                             first=part == 0, last=part == 2).then_inc(sem("tile_done"), tick("tile_done"))
                count["tile_done"] = 2 * CH_LAYER
            end_layer("pe")

            layer[pe] = 2
            att_base.update(pe=0, pe_o=0)
            sum_stat(pe, 0)
            norm_stat(pe, 0, tiles_of(sq_2), 6)

            def tile2(t, kind="f", K=KD, hi=h_hi, lo=h_lo, n=S, ready=None):
                c, half = t // 2, t % 2
                if half == 0:
                    split_ready(c)
                if before2[t] is not None:
                    pe.wait_ge(sem("tile_copied"), upto(pe, "tile_copied", before2[t] + 1))
                b = bank2[t]
                if kind == "f" or (kind == "kv" and half == 0):
                    ins = features(pe, c % 2, half, K, hi, lo, b, n=n, ready=ready)
                elif kind == "t":
                    ins = tokens(pe, c % 2, half, K, hi, lo, b, (2 * half, 2 * half + 1), ready=ready)
                else:
                    ins = tokens(pe, c % 2, half, K, hi, lo, b, range(hi.shape[-1] // P), half * P, P)
                ins.then_inc(sem("tile_done"), tick("tile_done"))

            def chunk2(c, *a, **kw):
                tile2(2 * c, *a, **kw)
                tile2(2 * c + 1, *a, **kw)

            def turn_branch(first):
                for k in range(4):
                    for r in range(RES):
                        ins = pe.transpose(ps[:, 4 + k, r * P:r * P + P], o_br[:, r, k * P:k * P + P], ident)
                    ins.then_inc(sem("o_turned"), tick("o_turned"))

            def merge_tile(c0, k, first):
                if k % 4 == 2:
                    pe.wait_ge(sem("h_lo"), upto(pe, "h_lo", first + 4))
                if k % 4 < 2:
                    tile2(2 * c0 + k)
                else:
                    tile2(2 * c0 + k, K=4, hi=gt_hi, lo=gt_lo)

            def turn_qk(n, z, bank):
                pe.matmul(ps[:, bank, :], swap64, z, start=True, stop=True).then_inc(sem("rot"), tick("rot"))

            for t in range(2 * C2_QK):
                tile2(t, "t", ready=0 if t == 0 else None)
                if t == 0:
                    pe.wait_ge(sem("h_lo"), upto(pe, "h_lo", 8))
            for gi in range(3):
                chunk2(C2_QK + gi)
            for j in range(6):
                pe.wait_ge(sem("tile_copied"), upto(pe, "tile_copied", 2 * C2_QK + j + 1))
                if j > 3:
                    pe.wait_ge(sem("roped"), upto(pe, "roped", j - 3))
                turn_qk(j, qk[:, 0, j, :], 4 + j % 4)
            for hp in range(4):
                def next_tile(j):
                    if hp < 3 and j:
                        pe.wait_ge(sem("rope_sin"), upto(pe, "rope_sin", 6 * (hp + 1) + j))
                    t = 2 * (C2_QK + 3 * hp + 3) + j
                    tile2(t, "kv" if t // 2 == C2_GA - 1 else "f")

                def next_turn(j):
                    pe.wait_ge(sem("tile_copied"), upto(pe, "tile_copied", 2 * (C2_QK + 3 * hp + 3) + j + 1))
                    turn_qk(6 * hp + 6 + j, qk[:, (hp + 1) % 2, j, :], 0)

                pe.wait_ge(sem("roped"), upto(pe, "roped", 6 * hp + 6))
                att_pe(pe, a_groups(hp), prob2, prob2_t, fill={j: partial(next_tile, j) for j in range(6)},
                       early={j + 1: partial(next_turn, j) for j in range(6)} if hp < 3 else {})
            chunk2(C2_GA)
            pe.wait_ge(sem("o_norm"), upto(pe, "o_norm", 8))
            turn_branch(8)

            def stat_b(j):
                pe.wait_ge(sem("sq"), upto(pe, "sq", 8 + j + 1))
                if j < 2:
                    pe.wait_ge(sem("h_full"), upto(pe, "h_full", 8 + j + 1))
                pe.matmul(ps[:, 4 + j % 2, :], late[:, 2 * P:3 * P], sq_b[:, j], start=True,
                          stop=True).then_inc(sem("stat"), tick("stat"))

            def turn_b(j):
                pe.wait_ge(sem("h_norm"), upto(pe, "h_norm", j + 1))
                if j < 2:
                    pe.wait_ge(sem("h_full"), upto(pe, "h_full", 8 + j + 3))
                else:
                    pe.wait_ge(sem("roped"), upto(pe, "roped", 24 + j - 1))
                pe.matmul(ps[:, 6 + j % 2, :], swap32, q_b[:, j, :], start=True, stop=True).then_inc(sem("rot"), tick("rot"))

            tile2(2 * C2_GA + 2)
            pe.wait_ge(sem("late_loaded"), 16)
            stat_b(0)
            stat_b(1)
            tile2(2 * C2_GA + 3)
            merge_tile(C2_MA, 0, 8)
            turn_b(0)
            turn_b(1)
            stat_b(2)
            stat_b(3)
            merge_tile(C2_MA, 1, 8)
            turn_b(2)
            turn_b(3)
            stat_b(4)
            merge_tile(C2_MA, 2, 8)
            turn_b(4)
            merge_tile(C2_MA, 3, 8)
            pe.wait_ge(sem("roped"), upto(pe, "roped", 29))
            for j in range(2):
                ins = pe.matmul(ps[:, 4 + j, :], late[:, j * P:j * P + P], q_b[:, 4, :], start=True, stop=True)
            ins.then_inc(sem("k_spread"), tick("k_spread"))
            pe.wait_ge(sem("k_b"), upto(pe, "k_b", 2))
            att_pe(pe, b_groups(), prob2, prob2_t,
                   fill={i: partial(merge_tile, C2_MA, k, 8) for i, k in FILL_B.items()})
            chunk2(C2_GB)
            pe.wait_ge(sem("mem_loaded"), 16)
            for k in range(KD):
                if k > 3:
                    pe.wait_ge(sem("mem_t"), upto(pe, "mem_t", k - 3))
                for t in range(2):
                    ins = pe.transpose(ps[:, 4 + k % 4, t * P:t * P + P], mem_in[:, t, k * P:k * P + P], ident)
                ins.then_inc(sem("mem_turned"), tick("mem_turned"))
            tile2(2 * C2_GB + 2)
            pe.wait_ge(sem("mem_t"), upto(pe, "mem_t", 8))
            norm_stat(pe, 13, tiles_of(mem_sq), STAT_BANK)
            tile2(2 * C2_GB + 3)
            pe.wait_ge(sem("o_norm"), upto(pe, "o_norm", 12))
            chunk2(C2_MQ)
            pe.wait_ge(sem("log_ms"), upto(pe, "log_ms", 8))
            turn_branch(20)
            chunk2(C2_MQ + 1)
            pe.wait_ge(sem("h_lo"), upto(pe, "h_lo", 20))
            for j in range(4):
                chunk2(C2_KV + j, "f" if j < 2 else "m", hi=mem_hi, lo=mem_lo, n=N_MEM)
            pe.wait_ge(sem("tile_copied"), upto(pe, "tile_copied", 2 * C2_MB))
            pe.wait_ge(sem("h_lo"), upto(pe, "h_lo", 24))
            att_pe(pe, m_groups(), prob2, prob2_t,
                   fill={i: partial(merge_tile, C2_MB, k, 20) for i, k in FILL_M.items()})
            chunk2(C2_GM)
            pe.wait_ge(sem("o_norm"), upto(pe, "o_norm", 16))
            turn_branch(24)
            chunk2(C2_GM + 1)
            for k in range(16):
                merge_tile(C2_MM, k, 24)
            split_ready(C2_OUT)
            for t in (2 * C2_OUT, 2 * C2_OUT + 1):
                pe.wait_ge(sem("tile_copied"), upto(pe, "tile_copied", before2[t] + 1))
            two_tiles(pe, C2_OUT % 2, KD, h_hi, h_lo, [bank2[2 * C2_OUT + i] for i in range(2)], (P, P), 28)
            for t in range(2 * C2_OUT + 2, 2 * C2_OUT + KD):
                tile2(t)
            sum_stat(pe, KD - 1)
            for r in range(RES):
                pe.wait_ge(sem("out_full"), upto(pe, "out_full", r + 1))
                for q in range(2):
                    if 2 * r + q > 1:
                        pe.wait_ge(sem("out_copied"), upto(pe, "out_copied", 2 * r + q - 1))
                    for k in range(4):
                        ins = pe.transpose(ps[:, 4 + q, k * P:k * P + P], out_t[:, 4 * q + k, r * P:r * P + P], ident)
                    ins.then_inc(sem("out_turned"), tick("out_turned"))
            end_layer("pe")

        @block.scalar
        def _(act):
            def copy_tile(tile, bank, dst, rows=P, func=ACT.Copy, n=S, **kw):
                act.wait_ge(sem("tile_done"), upto(act, "tile_done", tile + 1))
                src = ps[0:rows, bank, 0:n]
                if len(dst.shape) == 3:
                    src = src.rearrange("p (a n) -> p a n", a=dst.shape[1])
                act.activation(dst, src, func, **kw).then_inc(sem("tile_copied"), tick("tile_copied"))
                act.wait_ge(sem("tile_copied"), upto(act, "tile_copied"))

            def high(c, slot, K, loaded):
                n = K * 256
                act.wait_ge(sem(f"w_loaded{slot}"), upto(act, f"w_loaded{slot}", 16 * loaded))
                act.activation(w_hi[:, slot, 0:n], w_raw[:, slot, 0:n], ACT.Copy).then_inc(sem("w_high"), 1)

            act.preload_act_table_set("natural_log_exp_and_others")
            for k in range(KD):
                act.wait_ge(sem("init_turn"), k + 1)
                act.activation(x_t[:, k], ps[:, MAIN + k % 4, :], ACT.Copy).then_inc(sem("init_xt"), 1)
            for l in range(DEPTH):
                act.wait_ge(sem("gains_turned"), l + 1)
                act.activation(gains[:, l], ps[:, l, 0:G_N], ACT.Copy).then_inc(sem("init_gains"), 1)
            for slot in range(2):
                act.wait_ge(sem(f"w_loaded{slot}"), 32)
                act.activation(w_hi[:, slot], w_raw[:, slot], ACT.Copy).then_inc(sem("w_high"), 1)
            dmas = [n_dma[0::2], n_dma[1::2]]
            Ks = [K for K, _ in layer_chunks(0)]

            def next_high(c):
                high(c + 2, c % 2, Ks[c + 2] if c + 2 < C_UP else KD, sum(dmas[c % 2][:c // 2 + 2]))

            with act.Fori(0, DEPTH) as l:
                layer[act] = l
                att_base.update(act=0)
                act.preload_act_table_set("natural_log_exp_and_others")
                act.wait_ge(sem("g"), upto(act, "g", 2))
                act.wait_ge(sem("x_down"), upto(act, "x_down", 0))
                norm_factor(act, 0, STAT_BANK, D, rms_a[:])
                parts_act(act, 0, [h_hi[:, k] for k in range(KD)], fulls1)
                z_dst = [cq[:, 4], kg[0:80, :], lin[:, 0], lin[:, 1], cq[:, 0], cq[:, 1], cq[:, 2], cq[:, 3]]
                z_dst += [tm[:, 2 * a:2 * a + 2, b * 256:b * 256 + 256] for b in range(2) for a in range(2)]
                z_dst += [lin[:, 2], lin[:, 3]]
                z_dst += [tm[:, 2 * a:2 * a + 2, b * 256:b * 256 + 256] for b in (2, 3) for a in range(2)]

                def lin_gate(gate, dst):
                    act.activation(dst[:], tm[:, :, gate:gate + 256], ACT.Tanh, scale=0.5).then_inc(sem("g_tanh"), tick("g_tanh"))
                    act.wait_ge(sem("g_tanh"), upto(act, "g_tanh"))

                def lin_turned(no, dst, bank):
                    act.wait_ge(sem("kd_turned"), upto(act, "kd_turned", no + 1))
                    act.activation(dst[:], ps[:, bank, :].rearrange("p (t n) -> p t n", t=NT), ACT.Copy).then_inc(sem("kd_t"), tick("kd_t"))
                    act.wait_ge(sem("kd_t"), upto(act, "kd_t"))

                def lin_copy(no, dst, banks, halves=(0, 1)):
                    for b in halves:
                        act.wait_ge(sem("o_lin"), upto(act, "o_lin", 2 * no + b + 1))
                        act.activation(dst[:, 2 * b:2 * b + 2], ps[:, banks[b], :].rearrange("p (t n) -> p t n", t=2),
                                       ACT.Copy).then_inc(sem("o_copied"), tick("o_copied"))
                        act.wait_ge(sem("o_copied"), upto(act, "o_copied"))

                def lin_factor(no):
                    act.wait_ge(sem("o_ss"), upto(act, "o_ss", no + 1))
                    s16 = stats[:, 64 + 16 * no:80 + 16 * no]
                    act.activation(s16, s16, ACT.Ln, bias=eps[:, 0:1], scale=1.0 / LIN_DV).then_inc(sem("o_log"), tick("o_log"))
                    act.wait_ge(sem("o_log"), upto(act, "o_log"))
                    act.activation(s16, s16, ACT.Exp, scale=-0.5).then_inc(sem("o_rms"), tick("o_rms"))
                    act.wait_ge(sem("o_rms"), upto(act, "o_rms"))

                for t, d in enumerate(z_dst):
                    copy_tile(t, t % 4, d, rows=d.shape[0], scale=LIN_DK ** -0.5 if t == 2 else 1.0)
                    if t % 2:
                        next_high(t // 2)
                    if t == 2:
                        act.wait_ge(sem("gate"), upto(act, "gate", 1))
                        act.activation(gl[:, 1], ps[:, 6, :], ACT.Identity, bias=col(G_GATE, 1)).then_inc(sem("gk"), tick("gk"))
                        act.wait_ge(sem("gk"), upto(act, "gk"))
                        act.activation(gl[:, 2], gl[:, 1], ACT.Abs).then_inc(sem("gate_abs"), tick("gate_abs"))
                        act.wait_ge(sem("gate_abs"), upto(act, "gate_abs"))
                        act.activation(gl[:, 2], gl[:, 2], ACT.Exp, scale=-1.0).then_inc(sem("gate_exp"), tick("gate_exp"))
                        act.wait_ge(sem("gate_exp"), upto(act, "gate_exp"))
                        act.activation(gl[:, 2], gl[:, 2], ACT.Ln, bias=1.0).then_inc(sem("gate_ln"), tick("gate_ln"))
                        act.wait_ge(sem("gate_ln"), upto(act, "gate_ln"))
                    if t == 3:
                        act.wait_ge(sem("decay_sum"), upto(act, "decay_sum", 1))
                        act.activation(gl[:, 4], gl[:, 0], ACT.Exp, scale=1.0 / GATE_NORM).then_inc(sem("decay_exp"), tick("decay_exp"))
                        act.wait_ge(sem("decay_exp"), upto(act, "decay_exp"))
                        act.wait_ge(sem("decay_rest"), upto(act, "decay_rest", 1))
                        act.activation(gl[:, 6], gl[:, 6], ACT.Exp, scale=1.0 / GATE_NORM).then_inc(sem("decay_exp"), tick("decay_exp"))
                        act.wait_ge(sem("decay_exp"), upto(act, "decay_exp"))
                    if 4 <= t < 4 + len(LEVELS):
                        act.wait_ge(sem("lvl_diff"), upto(act, "lvl_diff", t - 3))
                        act.activation(gl[:, 1], gl[:, 1], ACT.Abs).then_inc(sem("lvl_abs"), tick("lvl_abs"))
                        act.wait_ge(sem("lvl_abs"), upto(act, "lvl_abs"))
                        act.activation(gl[:, 1], gl[:, 1], ACT.Exp, scale=-1.0 / GATE_NORM).then_inc(sem("lvl_exp"), tick("lvl_exp"))
                        act.wait_ge(sem("lvl_exp"), upto(act, "lvl_exp"))
                    if t == 9:
                        norm_sq(act, [cq[:, k] for k in range(5)], sq_c)
                    if t == 11:
                        act.activation(spare[:, 4:5], eps[:], ACT.Copy).then_inc(sem("held_act"), tick("held_act"))
                        act.preload_act_table_set("exp_and_others")
                        lin_gate(LIN["gla"]["gate"], sig)
                        act.activation(spare[:, 4:5], eps[:], ACT.Copy).then_inc(sem("held_act"), tick("held_act"))
                        act.preload_act_table_set("natural_log_exp_and_others")
                    if t == 13:
                        lin_turned(0, kd_t, 4)
                        norm_factor(act, 1, 7, Q_RANK, rms_a[:])
                        parts_act(act, PART["q"], tiles_of(cq_hi), fulls1)
                    if t == 16:
                        lin_copy(0, o_sb, (7, 4))
                norm_factor(act, 2, 5, KV_RANK, rms_b[:])
                lin_factor(0)
                parts_act(act, PART["kv"], [h_hi[:, 3 + k] for k in range(2)], fulls1)
                for j, d in enumerate([qn[:, h] for h in range(4)] + [qr[:, i] for i in range(2)]):
                    t = 2 * C_UQ + j
                    if j == 4:
                        act.wait_ge(sem("y_lin"), upto(act, "y_lin", 1))
                    copy_tile(t, t % 4, d, scale=(NOPE + ROPE) ** -0.5)
                    if t % 2:
                        next_high(t // 2)
                for j, d in enumerate([kn[:, h] for h in range(4)] +
                                      [v_mla[:, 2 * a:2 * a + 2, b * 256:b * 256 + 256] for b in range(2) for a in range(2)]):
                    t = 2 * C_UKV + j
                    copy_tile(t, t % 4, d)
                    if t % 2:
                        next_high(t // 2)
                act.activation(spare[:, 4:5], eps[:], ACT.Copy).then_inc(sem("held_act"), tick("held_act"))
                act.preload_act_table_set("exp_and_others")
                att_act(act, mla_groups(), prob, prob_t, fill={
                    3: partial(lin_gate, LIN["ret"]["gate"], sig_r), 7: partial(lin_turned, 1, kd_t_r, 0),
                    11: partial(lin_copy, 1, o_sb_r, (0, 3), (0,)), 12: partial(lin_copy, 1, o_sb_r, (0, 3), (1,))})
                act.activation(spare[:, 4:5], eps[:], ACT.Copy).then_inc(sem("held_act"), tick("held_act"))
                act.preload_act_table_set("natural_log_exp_and_others")
                lin_factor(1)
                act.wait_ge(sem("ymla_ss"), upto(act, "ymla_ss", NT))
                s16 = stats[:, 96:112]
                act.activation(s16, s16, ACT.Ln, bias=eps[:, 0:1], scale=1.0 / VDIM).then_inc(sem("ymla_log"), tick("ymla_log"))
                act.wait_ge(sem("ymla_log"), upto(act, "ymla_log"))
                act.activation(s16, s16, ACT.Exp, scale=-0.5).then_inc(sem("ymla_rms"), tick("ymla_rms"))
                act.wait_ge(sem("ymla_rms"), upto(act, "ymla_rms"))
                for j, k in enumerate(Y_ORDER):
                    act.wait_ge(sem("y_turned"), upto(act, "y_turned", j + 1))
                    act.activation(h_hi[:, k], ps[:, MAIN + j % 4, :], ACT.Copy, scale=col(G_OUT + k, 1)).then_inc(sem("h_hi"), tick("h_hi"))
                    act.wait_ge(sem("h_hi"), upto(act, "h_hi"))
                for m in range(KD):
                    t = 2 * C_OUT + m
                    if m > 1:
                        act.wait_ge(sem("sq_sum"), upto(act, "sq_sum", m - 1))
                    copy_tile(t, t % 4, tmp[:, m % 2])
                    if t % 2:
                        next_high(t // 2)
                for k in range(KD):
                    act.wait_ge(sem("x_mix"), upto(act, "x_mix", k + 1))
                    act.activation(h_hi[:, k], x_t[:, k], ACT.Copy, scale=col(G_FFN + k, 1)).then_inc(sem("h_hi"), tick("h_hi"))
                    act.wait_ge(sem("h_hi"), upto(act, "h_hi"))
                norm_factor(act, 3, STAT_BANK, D, rms_f[:])
                act.activation(spare[:, 4:5], eps[:], ACT.Copy).then_inc(sem("held_act"), tick("held_act"))
                act.preload_act_table_set("silu_and_others")
                with act.Fori(0, KF // 2) as i:
                    for s in range(2):
                        f = 2 * i + s
                        t = T_UP + 2 * f
                        act.wait_ge(sem("tile_copied"), upto(act, "tile_copied", t + 1))
                        act.activation(conv[:], a_pad[:, s, 2:S + 2], ACT.Identity,
                                                    scale=g[:, bass.ds(G_CONVW + 2 * KF + f, 1)],
                                                    bias=g[:, bass.ds(G_CONVB + f, 1)]).then_inc(sem("conv0"), 1)
                        act.wait_ge(sem("conv0"), upto(act, "conv0", f + 1))
                        act.wait_ge(sem("conv"), upto(act, "conv", f + 1))
                        act.activation(conv[:], conv[:], ACT.Silu).then_inc(sem("silu"), 1)
                        act.wait_ge(sem("silu"), upto(act, "silu", f + 1))
                        act.wait_ge(sem("tile_done"), upto(act, "tile_done", t + 2))
                        high(C_UP + f + 2, s, KD, sum(dmas[s][:C_UP // 2]) + 2 * (i + 2))
                        act.wait_ge(sem("tile_copied"), upto(act, "tile_copied", t + 2))
                        act.activation(hid_hi[:, bass.ds(f, 1), :].rearrange("p a n -> p (a n)"), b_sb[:], ACT.Copy).then_inc(sem("hid_hi"), 1)
                        act.wait_ge(sem("hid_hi"), upto(act, "hid_hi", f + 1))
                count["tile_copied"] = T_DOWN
                for n in ("conv0", "silu", "hid_hi"):
                    count[n] = KF
                with act.Fori(0, 2) as i:
                    act.wait_ge(sem("sq_sum"), upto(act, "sq_sum", KD + 4 * i))
                    for q in range(2):
                        for j in (3 * q, 3 * q + 1):
                            act.wait_ge(sem("tile_done"), upto(act, "tile_done", 2 * (C_DOWN + 6 * i + j) + 2))
                            high(C_DOWN + 6 * i + j + 2, j % 2, DOWN_K[(j + 2) % 3],
                                 sum(dmas[j % 2][:C_DOWN // 2]) + 2 * (3 * i + j // 2 + 2))
                        for half in range(2):
                            act.wait_ge(sem("tile_done"), upto(act, "tile_done", 2 * (C_DOWN + 6 * i + 3 * q + 2) + half + 1))
                            dst = (b_sb[:], rms_f[:])[half] if q == 0 else a_pad[:, half, 0:S]
                            act.activation(dst, ps[:, 2 * q + half, :], ACT.Copy).then_inc(sem("tile_copied"), 1)
                            act.wait_ge(sem("tile_copied"), upto(act, "tile_copied", T_DOWN + 4 * i + 2 * q + half + 1))
                        j = 3 * q + 2
                        high(C_DOWN + 6 * i + j + 2, j % 2, DOWN_K[(j + 2) % 3],
                             sum(dmas[j % 2][:C_DOWN // 2]) + 2 * (3 * i + j // 2 + 2))
                count["tile_copied"] = TILES_LAYER
            end_layer("act")

            layer[act] = 2
            att_base.update(act=0)
            act.preload_act_table_set("natural_log_exp_and_others")
            act.wait_ge(sem("x_down"), upto(act, "x_down", 0))
            norm_factor(act, 0, STAT_BANK, D, rms_a[:])
            for k in range(KD):
                act.wait_ge(sem("x1_full"), upto(act, "x1_full", k + 1))
                act.activation(sq_2[:, k], x1[k], ACT.Square).then_inc(sem("sq"), tick("sq"))
                act.wait_ge(sem("sq"), upto(act, "sq"))
            norm_factor(act, 1, 6, D, rms_a[:])
            parts_act(act, 0, [h_hi[:, k] for k in range(KD)], fulls3)

            def copy2(tile, dst, **kw):
                copy_tile(tile, bank2[tile], dst, **kw)
                c = tile // 2 + 2
                if tile % 2 and c < len(second):
                    high(c, c % 2, second[c][0], sum(len(p_) for _, p_ in second[c % 2:c + 1:2]))

            def merge_copy(b, c0, k):
                half, n = k % 2, 2 * (k // 4) + k % 2
                if k % 4 < 2:
                    if k > 3:
                        act.wait_ge(sem("merged"), upto(act, "merged", 8 * b + n - 1))
                    copy2(2 * c0 + k, gate_br[:, half], func=ACT.Tanh, scale=0.5, bias=g2[:, 32 + 8 * b + n:33 + 8 * b + n])
                else:
                    copy2(2 * c0 + k, y_br[:, half], scale=0.5)

            def branch_parts(first):
                parts_act(act, first, [gt_hi[:, k] for k in range(4)], fulls2)

            for j in range(2 * C2_QK):
                copy2(j, av[:, 2 * (j % 2):2 * (j % 2) + 2, j // 2 * 256:j // 2 * 256 + 256])

            def copy_qk(hp, j):
                copy2(2 * (C2_QK + 3 * hp) + j, qk[:, hp % 2, j], scale=HD ** -0.5 if j % 2 == 0 else 1.0)

            def copy_b(j):
                copy2(2 * C2_BQ + j, q_b[:, j] if j < 5 else v_b[:])

            act.wait_ge(sem("x1"), upto(act, "x1", KD))
            for j in range(6):
                copy_qk(0, j)
            act.preload_act_table_set("exp_and_others")
            for hp in range(4):
                att_act(act, a_groups(hp), prob2, prob2_t,
                        fill={j: partial(copy_qk, hp + 1, j) if hp < 3 else partial(copy_b, j) for j in range(6)})
            act.preload_act_table_set("silu_and_others")
            act.wait_ge(sem("o_norm"), upto(act, "o_norm", 8))
            for k in range(2):
                copy2(2 * C2_GA + k, sgates[0][:, k], func=ACT.Silu)
            norm_sq(act, tiles_of(q_b), tiles_of(sq_b))
            for k in range(2, 4):
                copy2(2 * C2_GA + k, sgates[0][:, k], func=ACT.Silu)
            act.preload_act_table_set("natural_log_exp_and_others")
            branch_parts(8)
            for j in range(5):
                if j:
                    act.wait_ge(sem("h_norm"), upto(act, "h_norm", j))
                norm_factor(act, 2 + j, 4 + j % 2, HD, rms_a[:])
            act.preload_act_table_set("exp_and_others")
            for k in range(4):
                merge_copy(0, C2_MA, k)
            att_act(act, b_groups(), prob2, prob2_t, fill={i: partial(merge_copy, 0, C2_MA, k) for i, k in FILL_B.items()})
            act.preload_act_table_set("silu_and_others")
            act.wait_ge(sem("o_norm"), upto(act, "o_norm", 12))
            for k in range(2):
                copy2(2 * C2_GB + k, sgates[1][:, k], func=ACT.Silu)
            for k in range(KD):
                act.wait_ge(sem("mem_turned"), upto(act, "mem_turned", k + 1))
                if k == 0:
                    act.wait_ge(sem("merged"), upto(act, "merged", 8))
                act.activation(mem_t[:, k], ps[:, 4 + k % 4, 0:N_MEM], ACT.Copy).then_inc(sem("mem_t"), tick("mem_t"))
                act.wait_ge(sem("mem_t"), upto(act, "mem_t"))
            act.wait_ge(sem("mem_turned"), upto(act, "mem_turned", KD))
            norm_sq(act, tiles_of(mem_t), tiles_of(mem_sq))
            for k in range(2, 4):
                copy2(2 * C2_GB + k, sgates[1][:, k], func=ACT.Silu)
            act.preload_act_table_set("natural_log_exp_and_others")
            norm_factor(act, 7, STAT_BANK, D, rms_a[:, 0:N_MEM])
            parts_act(act, 12, [mem_hi[:, k] for k in range(KD)], [f[:, 0:N_MEM] for f in fulls2])
            for j in range(2):
                copy2(2 * C2_MQ + j, q_m[:, j], scale=P ** -0.5)
            branch_parts(20)
            for j in range(2, 4):
                copy2(2 * C2_MQ + j, q_m[:, j], scale=P ** -0.5)
            for j in range(4):
                copy2(2 * C2_KV + j, km[:, j], n=N_MEM)
            for j in range(4):
                copy2(2 * C2_KV + 4 + j, vm[:, :, j * P:j * P + P], n=256)
            act.preload_act_table_set("exp_and_others")
            att_act(act, m_groups(), prob2, prob2_t, fill={i: partial(merge_copy, 1, C2_MB, k) for i, k in FILL_M.items()})
            act.preload_act_table_set("silu_and_others")
            for k in range(4):
                copy2(2 * C2_GM + k, sgates[2][:, k], func=ACT.Silu)
            act.preload_act_table_set("exp_and_others")
            branch_parts(24)

            def merged_high(k):
                act.wait_ge(sem("merged"), upto(act, "merged", 16 + k + 1))
                act.activation(h_hi[:, k], merged[:, k], ACT.Copy).then_inc(sem("h_hi"), tick("h_hi"))
                act.wait_ge(sem("h_hi"), upto(act, "h_hi"))

            for k in range(16):
                merge_copy(2, C2_MM, k)
                if k == 13:
                    for m in range(KD - 2):
                        merged_high(m)
            for m in range(KD - 2, KD):
                merged_high(m)
            act.preload_act_table_set("natural_log_exp_and_others")
            for k in range(KD):
                t = 2 * C2_OUT + k
                act.wait_ge(sem("tile_done"), upto(act, "tile_done", t + 1))
                act.activation(sq_2[:, k], ps[:, bank2[t], :], ACT.Square).then_inc(sem("sq"), tick("sq"))
                act.wait_ge(sem("sq"), upto(act, "sq"))
                copy2(t, out_t[:, k], scale=g2[:, 24 + k:25 + k])
            norm_factor(act, 8, STAT_BANK, D, rms_a[:])
            for r in range(RES):
                for q in range(2):
                    act.wait_ge(sem("out_turned"), upto(act, "out_turned", 2 * r + q + 1))
                    act.activation(out_sb[:, r, q * 512:q * 512 + 512], ps[:, 4 + q, :], ACT.Copy).then_inc(sem("out_copied"), tick("out_copied"))
                    act.wait_ge(sem("out_copied"), upto(act, "out_copied"))
            end_layer("act")

        @block.vector
        def _(dve):
            dve.memset(eps[:], EPS).then_inc(sem("g_scaled"), 1)
            dve.wait_ge(sem("g_scaled"), 1)

            def add_square(x, scratch, first):
                if first:
                    dve.tensor_tensor(rms_a[:], x, x, ALU.mult).then_inc(sem("sq_sum"), tick("sq_sum"))
                else:
                    dve.tensor_tensor(scratch, x, x, ALU.mult).then_inc(sem("sq_tile"), tick("sq_tile"))
                    dve.wait_ge(sem("sq_tile"), upto(dve, "sq_tile"))
                    dve.tensor_tensor(rms_a[:], rms_a[:], scratch, ALU.add).then_inc(sem("sq_sum"), tick("sq_sum"))
                dve.wait_ge(sem("sq_sum"), upto(dve, "sq_sum"))

            for k in range(KD):
                dve.wait_ge(sem("init_xt"), k + 1)
                if k == 0:
                    dve.tensor_tensor(rms_a[:], x_t[:, k], x_t[:, k], ALU.mult).then_inc(sem("sq_sum"), 1)
                else:
                    dve.tensor_tensor(sq_in[:], x_t[:, k], x_t[:, k], ALU.mult).then_inc(sem("init_sq"), 1)
                    dve.wait_ge(sem("init_sq"), k)
                    dve.tensor_tensor(rms_a[:], rms_a[:], sq_in[:], ALU.add).then_inc(sem("sq_sum"), 1)
                dve.wait_ge(sem("sq_sum"), k + 1)
            dve.wait_ge(sem("init_g"), 16 * (1 + 5 + 4))
            dve.tensor_scalar(g2[:, 56:57], g2[:, 56:57], HD ** -0.5, None, ALU.mult).then_inc(sem("g_scaled"), 1)
            dve.tensor_scalar(g2[:, 32:56], g2[:, 32:56], 0.5, None, ALU.mult).then_inc(sem("g_scaled"), 1)
            dve.wait_ge(sem("g_scaled"), 3)
            dve.wait_ge(sem("init_gains"), DEPTH)
            dve.wait_ge(sem("init_c"), 32)
            dve.tensor_copy(levels[:], levels_in[:]).then_inc(sem("x_down"), 1)
            dve.wait_ge(sem("x_down"), 1)

            def rope(no, z, rot, cos, sin, dst, t):
                dve.wait_ge(sem("rot"), upto(dve, "rot", no + 1))
                dve.tensor_tensor(dst, z, cos, ALU.mult).then_inc(sem("rope_cos"), tick("rope_cos"))
                dve.wait_ge(sem("rope_cos"), upto(dve, "rope_cos"))
                dve.tensor_tensor(t, rot, sin, ALU.mult).then_inc(sem("rope_sin"), tick("rope_sin"))
                dve.wait_ge(sem("rope_sin"), upto(dve, "rope_sin"))
                dve.tensor_tensor(dst, dst, t, ALU.add).then_inc(sem("roped"), tick("roped"))
                dve.wait_ge(sem("roped"), upto(dve, "roped"))

            with dve.Fori(0, DEPTH) as l:
                layer[dve] = l
                att_base.update(dve=0)
                dve.tensor_copy(g[:], gains[:, bass.ds(l, 1), :].rearrange("p a n -> p (a n)")).then_inc(sem("g"), tick("g"))
                dve.wait_ge(sem("g"), upto(dve, "g"))
                dve.tensor_copy(wg[64:80, :], wg_all[64:80, bass.ds(l, 1), :].rearrange("p a n -> p (a n)")).then_inc(sem("g"), tick("g"))
                dve.wait_ge(sem("g"), upto(dve, "g"))
                hi, lo = [h_hi[:, k] for k in range(KD)], [h_lo[:, k] for k in range(KD)]
                xs = [x_t[:, k] for k in range(KD)]
                parts_dve(dve, 0, normed(dve, xs, col(G_ATTN, 8), rms_a[:], 0), hi, lo, fulls1)
                by_tile = lambda t: t.rearrange("p (t n) -> p t n", t=NT)
                dve.memset(gl[:, 4], 1.0).then_inc(sem("reset"), tick("reset"))
                dve.wait_ge(sem("reset"), upto(dve, "reset"))
                dve.memset(by_tile(gl[:, 4])[:, :, 0:1], 0.0).then_inc(sem("reset"), tick("reset"))
                dve.wait_ge(sem("reset"), upto(dve, "reset"))
                dve.memset(amat[:], 0.0).then_inc(sem("amat0"), tick("amat0"))
                dve.wait_ge(sem("amat0"), upto(dve, "amat0"))
                dve.wait_ge(sem("gk"), upto(dve, "gk", 1))
                dve.tensor_scalar(gl[:, 3], gl[:, 1], 0.0, None, ALU.min).then_inc(sem("gate_min"), tick("gate_min"))
                dve.wait_ge(sem("gate_min"), upto(dve, "gate_min"))
                dve.wait_ge(sem("gate_ln"), upto(dve, "gate_ln", 1))
                dve.tensor_tensor(gl[:, 3], gl[:, 3], gl[:, 2], ALU.subtract).then_inc(sem("gate_log"), tick("gate_log"))
                dve.wait_ge(sem("gate_log"), upto(dve, "gate_log"))
                dve.tensor_tensor_scan(gl[:, 0], gl[:, 4], gl[:, 3], 0.0, ALU.mult, ALU.add).then_inc(sem("decay_sum"), tick("decay_sum"))
                dve.wait_ge(sem("decay_sum"), upto(dve, "decay_sum"))
                b4 = by_tile(gl[:, 0])
                dve.tensor_tensor(by_tile(gl[:, 6]), b4[:, :, P - 1:P].to_broadcast([P, NT, P]), b4,
                                  ALU.subtract).then_inc(sem("decay_rest"), tick("decay_rest"))
                dve.wait_ge(sem("decay_rest"), upto(dve, "decay_rest"))

                def diff(i):
                    n = LEVELS[i]
                    v = gl[:, 0].rearrange("p (b n) -> p b n", n=2 * n)
                    dve.tensor_tensor(gl[:, 1].rearrange("p (b n) -> p b n", n=2 * n), v,
                                      v[:, :, n - 1:n].to_broadcast([P, S // (2 * n), 2 * n]),
                                      ALU.subtract).then_inc(sem("lvl_diff"), tick("lvl_diff"))
                    dve.wait_ge(sem("lvl_diff"), upto(dve, "lvl_diff"))

                def keep(i, lv):
                    dve.wait_ge(sem("lvl_a"), upto(dve, "lvl_a", i + 1))
                    dve.memset(spare[:, 2:3], 0.0).then_inc(sem("held_dve"), tick("held_dve"))
                    dve.copy_predicated(amat[:].rearrange("p h t n -> p (h t) n"),
                                        levels[:, lv:lv + 1, :].to_broadcast([P, 4 * NT, P]),
                                        ps[:, MAIN:MAIN + 4, :].rearrange("p h (t n) -> p (h t) n",
                                                                          t=NT)).then_inc(sem("lvl_kept"), tick("lvl_kept"))
                    dve.wait_ge(sem("lvl_kept"), upto(dve, "lvl_kept"))

                def lin_update(no, u, banks, decay):
                    dve.wait_ge(sem("u_sum"), upto(dve, "u_sum", no + 1))
                    for b in range(2):
                        dve.tensor_tensor(u[:, 2 * b:2 * b + 2], ps[:, banks[b], :].rearrange("p (t n) -> p t n", t=2),
                                          block_mask.unsqueeze(1).to_broadcast([P, 2, 256]), ALU.mult).then_inc(sem("um"), tick("um"))
                        dve.wait_ge(sem("um"), upto(dve, "um"))
                    for t in (1, 2):
                        dve.scalar_tensor_tensor(u[:, t], u[:, t - 1], decay(t), u[:, t], ALU.mult,
                                                 ALU.add).then_inc(sem("state"), tick("state"))
                        dve.wait_ge(sem("state"), upto(dve, "state"))

                def lin_silu(no, gate, dst):
                    dve.wait_ge(sem("g_tanh"), upto(dve, "g_tanh", no + 1))
                    dve.scalar_tensor_tensor(dst[:], dst[:], 1.0, tm[:, :, gate:gate + 256], ALU.add,
                                             ALU.mult).then_inc(sem("silu_g"), tick("silu_g"))
                    dve.wait_ge(sem("silu_g"), upto(dve, "silu_g"))

                def lin_squares(no, o_, scratch):
                    dve.wait_ge(sem("o_copied"), upto(dve, "o_copied", 2 * no + 2))
                    dve.tensor_tensor(scratch[:], o_[:], o_[:], ALU.mult).then_inc(sem("o_sq"), tick("o_sq"))
                    dve.wait_ge(sem("o_sq"), upto(dve, "o_sq"))
                    dve.tensor_reduce(stats[:, 64 + 16 * no:80 + 16 * no], heads16(scratch[:], LIN_DV), AX.X,
                                      ALU.add).then_inc(sem("o_ss"), tick("o_ss"))
                    dve.wait_ge(sem("o_ss"), upto(dve, "o_ss"))

                def lin_gated(no, o_, silu, gate):
                    dve.wait_ge(sem("o_rms"), upto(dve, "o_rms", no + 1))
                    oh = heads16(o_[:], LIN_DV)
                    factor = stats[:, 64 + 16 * no:80 + 16 * no]
                    dve.tensor_tensor(oh, oh, factor.unsqueeze(2).to_broadcast([P, 16, LIN_DV]),
                                      ALU.mult).then_inc(sem("o_scaled"), tick("o_scaled"))
                    dve.wait_ge(sem("o_scaled"), upto(dve, "o_scaled"))
                    dve.scalar_tensor_tensor(tm[:, :, gate:gate + 256], o_[:], 0.5, silu[:], ALU.mult,
                                             ALU.mult).then_inc(sem("y_lin"), tick("y_lin"))
                    dve.wait_ge(sem("y_lin"), upto(dve, "y_lin"))

                diff(0)
                keep(0, len(LEVELS))
                for i in range(len(LEVELS)):
                    dve.wait_ge(sem("lvl_exp"), upto(dve, "lvl_exp", i + 1))
                    dve.tensor_tensor(gl[:, 2], lin[:, 0], gl[:, 1], ALU.mult).then_inc(sem("lvl_q"), tick("lvl_q"))
                    dve.wait_ge(sem("lvl_q"), upto(dve, "lvl_q"))
                    dve.tensor_tensor(gl[:, 3], lin[:, 1], gl[:, 1], ALU.mult).then_inc(sem("lvl_k"), tick("lvl_k"))
                    dve.wait_ge(sem("lvl_k"), upto(dve, "lvl_k"))
                    if i + 1 < len(LEVELS):
                        diff(i + 1)
                    if i == 0:
                        dve.wait_ge(sem("decay_exp"), upto(dve, "decay_exp", 2))
                        dve.tensor_tensor(gl[:, 5], lin[:, 0], gl[:, 4], ALU.mult).then_inc(sem("lin_qk"), tick("lin_qk"))
                        dve.wait_ge(sem("lin_qk"), upto(dve, "lin_qk"))
                        dve.tensor_tensor(gl[:, 6], lin[:, 1], gl[:, 6], ALU.mult).then_inc(sem("lin_qk"), tick("lin_qk"))
                        dve.wait_ge(sem("lin_qk"), upto(dve, "lin_qk"))
                    keep(i + 1, i)
                lin_silu(0, LIN["gla"]["gate"], sig)
                parts_dve(dve, PART["q"], normed(dve, [cq[:, k] for k in range(3)], col(G_Q, 3), rms_a[:], 1),
                          tiles_of(cq_hi), tiles_of(cq_lo), fulls1)
                lin_update(0, um, (5, 6), lambda t: gl[:, 4, t * P + P - 1:t * P + P])
                lin_squares(0, o_sb, um)
                parts_dve(dve, PART["kv"], normed(dve, [cq[:, 3 + k] for k in range(2)], col(G_KV, 2), rms_b[:], 2),
                          hi[3:5], lo[3:5], fulls1)
                lin_gated(0, o_sb, sig, LIN["gla"]["gate"])
                dve.wait_ge(sem("tab_loaded"), upto(dve, "tab_loaded", 16))
                rope(0, ps[:, 7, :], ps[:, 4, :], tab[:, 0], tab[:, 1], kr[:], tmp[:, 2])
                for j in range(2):
                    rope(1 + j, qr[:, j], ps[:, 5 + j, :], tab[:, 0], tab[:, 1], qr[:, j], tmp[:, 2])

                def ret_rope():
                    for j in range(2):
                        rope(3 + j, lin[:, 2 + j], ps[:, 3 * j, :], tab[:, 2], tab[:, 3], lin[:, 2 + j], tmp[:, 2])

                def ret_decayed():
                    for j, (src, dec) in enumerate(((lin[:, 2], ret_q), (lin[:, 3], ret_k))):
                        dve.tensor_tensor(by_tile(qk_r[:, j]), by_tile(src), dec.unsqueeze(1).to_broadcast([P, NT, P]),
                                          ALU.mult).then_inc(sem("lin_qk"), tick("lin_qk"))
                        dve.wait_ge(sem("lin_qk"), upto(dve, "lin_qk"))

                def ret_weights(first):
                    dve.wait_ge(sem("lvl_a"), upto(dve, "lvl_a", 9 + first // 2))
                    for h in (first, first + 1):
                        done = "lvl_head" if h < 3 else "lvl_kept"
                        dve.tensor_tensor(amat_r[:, h], by_tile(ps[:, RET_BANKS[h], :]),
                                          ret_d[:, h:h + 1, :].to_broadcast([P, NT, P]), ALU.mult).then_inc(sem(done), tick(done))
                        dve.wait_ge(sem(done), upto(dve, done))

                def mla_squares(t):
                    ym = y_mla[:, t].rearrange("p (h d) -> p h d", d=VDIM)
                    ysq = tmp[:, 2].rearrange("p (h d) -> p h d", d=VDIM)
                    dve.tensor_tensor(ysq, ym, ym, ALU.mult).then_inc(sem("ymla_sq"), tick("ymla_sq"))
                    dve.wait_ge(sem("ymla_sq"), upto(dve, "ymla_sq"))
                    dve.tensor_reduce(stats[:, 96 + 4 * t:100 + 4 * t], ysq, AX.X, ALU.add).then_inc(sem("ymla_ss"), tick("ymla_ss"))
                    dve.wait_ge(sem("ymla_ss"), upto(dve, "ymla_ss"))

                att_dve(dve, mla_groups(), fill={
                    0: ret_rope, 1: ret_decayed, 2: partial(ret_weights, 0),
                    3: partial(lin_silu, 1, LIN["ret"]["gate"], sig_r),
                    4: lambda: (ret_weights(2), mla_squares(0)), 8: partial(mla_squares, 1),
                    9: partial(lin_update, 1, um_r, (3, 7), lambda t: ret_c),
                    12: partial(mla_squares, 2), 13: partial(lin_squares, 1, o_sb_r, um_r)})
                mla_squares(3)
                lin_gated(1, o_sb_r, sig_r, LIN["ret"]["gate"])
                dve.wait_ge(sem("ymla_rms"), upto(dve, "ymla_rms", 1))
                ym = heads16(y_mla[:], VDIM)
                dve.tensor_tensor(ym, ym, stats[:, 96:112].unsqueeze(2).to_broadcast([P, 16, VDIM]), ALU.mult).then_inc(sem("ymla"), tick("ymla"))
                dve.wait_ge(sem("ymla"), upto(dve, "ymla"))

                def low(k, src, gain):
                    dve.scalar_tensor_tensor(lo[k], src, gain, hi[k].bitcast(F32), ALU.mult,
                                             ALU.subtract).then_inc(sem("h_lo"), tick("h_lo"))
                    dve.wait_ge(sem("h_lo"), upto(dve, "h_lo"))

                for j, k in enumerate(Y_ORDER):
                    dve.wait_ge(sem("h_hi"), upto(dve, "h_hi", PART["y"] + j + 1))
                    low(k, ps[:, MAIN + j % 4, :], col(G_OUT + k, 1))
                for m in range(KD):
                    dve.wait_ge(sem("tile_copied"), upto(dve, "tile_copied", 2 * C_OUT + m + 1))
                    dve.tensor_tensor(x_t[:, m], x_t[:, m], tmp[:, m % 2], ALU.add).then_inc(sem("x_mix"), tick("x_mix"))
                    dve.wait_ge(sem("x_mix"), upto(dve, "x_mix"))
                    add_square(x_t[:, m], tmp[:, m % 2], m == 0)
                for k in range(KD):
                    dve.wait_ge(sem("h_hi"), upto(dve, "h_hi", PART["ffn"] + k + 1))
                    low(k, x_t[:, k], col(G_FFN + k, 1))
                dve.memset(a_pad[:, :, 0:2], 0.0).then_inc(sem("pad"), tick("pad"))
                with dve.Fori(0, KF // 2) as i:
                    for s in range(2):
                        f = 2 * i + s
                        t = T_UP + 2 * f
                        dve.wait_ge(sem("tile_done"), upto(dve, "tile_done", t + 1))
                        if s == 0:
                            dve.wait_ge(sem("rms"), upto(dve, "rms", 4))
                        dve.tensor_tensor(a_pad[:, s, 2:S + 2], ps[:, 2 * s, :], rms_f[:], ALU.mult).then_inc(sem("tile_copied"), 1)
                        dve.wait_ge(sem("conv0"), upto(dve, "conv0", f + 1))
                        if s == 0:
                            dve.wait_ge(sem("pad"), upto(dve, "pad", 1))
                        for w in (1, 0):
                            dve.scalar_tensor_tensor(conv[:], a_pad[:, s, w:w + S],
                                                                  g[:, bass.ds(G_CONVW + w * KF + f, 1)], conv[:],
                                                                  ALU.mult, ALU.add).then_inc(sem("conv1" if w else "conv"), 1)
                            dve.wait_ge(sem("conv1" if w else "conv"), upto(dve, "conv1" if w else "conv", f + 1))
                        dve.wait_ge(sem("silu"), upto(dve, "silu", f + 1))
                        dve.tensor_tensor(conv[:], conv[:], rms_f[:], ALU.mult).then_inc(sem("silu_scaled"), 1)
                        dve.wait_ge(sem("silu_scaled"), upto(dve, "silu_scaled", f + 1))
                        dve.wait_ge(sem("tile_done"), upto(dve, "tile_done", t + 2))
                        dve.tensor_tensor(b_sb[:], ps[:, 2 * s + 1, :], conv[:], ALU.mult).then_inc(sem("tile_copied"), 1)
                        dve.wait_ge(sem("tile_copied"), upto(dve, "tile_copied", t + 2))
                        dve.wait_ge(sem("hid_hi"), upto(dve, "hid_hi", f + 1))
                        dve.tensor_tensor(hid_lo[:, bass.ds(f, 1), :].rearrange("p a n -> p (a n)"), b_sb[:],
                                                       hid_hi[:, bass.ds(f, 1), :].rearrange("p a n -> p (a n)").bitcast(F32),
                                                       ALU.subtract).then_inc(sem("hid_lo"), 1)
                        dve.wait_ge(sem("hid_lo"), upto(dve, "hid_lo", f + 1))
                for n in ("conv1", "conv", "silu_scaled", "hid_lo"):
                    count[n] = KF
                dve.memset(rms_a[:], 0.0).then_inc(sem("sq_reset"), tick("sq_reset"))
                with dve.Fori(0, 2) as i:
                    for q in range(2):
                        for half in range(2):
                            j = 2 * q + half
                            dve.wait_ge(sem("tile_copied"), upto(dve, "tile_copied", T_DOWN + 4 * i + j + 1))
                            src = (b_sb[:], rms_f[:])[half] if q == 0 else a_pad[:, half, 0:S]
                            x_m = x_t[:, bass.ds(4 * i + j, 1), :].rearrange("p a n -> p (a n)")
                            dve.tensor_tensor(x_m, x_m, src, ALU.add).then_inc(sem("x_down"), 1)
                            dve.wait_ge(sem("x_down"), upto(dve, "x_down", 4 * i + j + 1))
                            dve.tensor_tensor(src, x_m, x_m, ALU.mult).then_inc(sem("sq_tile"), 1)
                            dve.wait_ge(sem("sq_tile"), upto(dve, "sq_tile", KD - 1 + 4 * i + j + 1))
                            if j == 0:
                                dve.wait_ge(sem("sq_reset"), upto(dve, "sq_reset", 1))
                            dve.tensor_tensor(rms_a[:], rms_a[:], src, ALU.add).then_inc(sem("sq_sum"), 1)
                            dve.wait_ge(sem("sq_sum"), upto(dve, "sq_sum", KD + 4 * i + j + 1))
                count["x_down"] = KD
                count["sq_tile"], count["sq_sum"] = 2 * KD - 1, 2 * KD
            end_layer("dve")

            layer[dve] = 2
            att_base.update(dve=0)
            by_class = lambda t: t.rearrange("p (n r) -> p r n", r=RES)
            for k in range(KD):
                if k == 0:
                    dve.wait_ge(sem("rms"), upto(dve, "rms", 1))
                dve.scalar_tensor_tensor(x1[k].rearrange("p (r n) -> p r n", r=RES), by_class(x_t[:, k]),
                                                   g2[:, k:k + 1], by_class(rms_a[:]), ALU.mult, ALU.mult).then_inc(sem("x1_full"), tick("x1_full"))
                dve.wait_ge(sem("x1_full"), upto(dve, "x1_full"))
            parts_dve(dve, 0, normed(dve, x1, g2[:, 8:16], rms_a[:], 1), hi, lo, fulls3)

            def branch_parts(b, c0, first):
                def gated(k, dst):
                    dve.wait_ge(sem("tile_copied"), upto(dve, "tile_copied", 2 * c0 + k + 1))
                    dve.wait_ge(sem("o_turned"), upto(dve, "o_turned", 4 * b + k + 1))
                    dve.tensor_tensor(dst, ps[:, 4 + k, :], sgates[b][:, k], ALU.mult).then_inc(sem("h_full"), tick("h_full"))
                    dve.wait_ge(sem("h_full"), upto(dve, "h_full"))
                parts_dve(dve, first, gated, [gt_hi[:, k] for k in range(4)], [gt_lo[:, k] for k in range(4)], fulls2)

            def merge(b, c0, k):
                half, n = k % 2, 2 * (k // 4) + k % 2
                dve.wait_ge(sem("tile_copied"), upto(dve, "tile_copied", 2 * c0 + k + 1))
                dst = merged[:, n]
                term = dst if b == 0 else tmp2[:]
                ins = dve.scalar_tensor_tensor(term, gate_br[:, half], 1.0, y_br[:, half], ALU.add, ALU.mult)
                if b:
                    ins.then_inc(sem("merge_term"), tick("merge_term"))
                    dve.wait_ge(sem("merge_term"), upto(dve, "merge_term"))
                    ins = dve.tensor_tensor(dst, dst, tmp2[:], ALU.add)
                ins.then_inc(sem("merged"), tick("merged"))
                dve.wait_ge(sem("merged"), upto(dve, "merged"))

            dve.wait_ge(sem("win_loaded"), 48)
            dve.tensor_copy(win[:], win_in[:]).then_inc(sem("win_cast"), 1)
            dve.wait_ge(sem("win_cast"), 1)

            def rope_qk(hp, j):
                z = qk[:, hp % 2, j]
                rope(6 * hp + j, z, ps[:, 0 if hp else 4 + j % 4, :], a_cos[:], a_sin[:], z, tmp2[:])

            for j in range(6):
                rope_qk(0, j)
            for hp in range(4):
                att_dve(dve, a_groups(hp), fill={j: partial(rope_qk, hp + 1, j) for j in range(6)} if hp < 3 else {})
            branch_parts(0, C2_GA, 8)
            dve.wait_ge(sem("late_loaded"), 16)
            ax_cos, ax_sin = late[:, 3 * P:3 * P + S], late[:, 3 * P + S:3 * P + 2 * S]

            def norm_b(j):
                dve.wait_ge(sem("rms"), upto(dve, "rms", 2 + j + 1))
                z = q_b[:, j]
                dve.scalar_tensor_tensor(z, z, g2[:, 56 + j // 4:57 + j // 4], rms_a[:], ALU.mult,
                                         ALU.mult).then_inc(sem("h_norm"), tick("h_norm"))
                dve.wait_ge(sem("h_norm"), upto(dve, "h_norm"))

            def rope_b(j):
                rope(24 + j, q_b[:, j], ps[:, 6 + j % 2, :], ax_cos, ax_sin, q_b[:, j], tmp2[:])

            norm_b(0)
            norm_b(1)
            rope_b(0)
            rope_b(1)
            norm_b(2)
            norm_b(3)
            rope_b(2)
            rope_b(3)
            norm_b(4)
            rope_b(4)
            dve.wait_ge(sem("k_spread"), upto(dve, "k_spread", 1))
            for j in range(2):
                dve.tensor_copy(k_b[:, j], ps[:, 4 + j, :]).then_inc(sem("k_b"), tick("k_b"))
                dve.wait_ge(sem("k_b"), upto(dve, "k_b"))
            for k in (2, 3):
                merge(0, C2_MA, k)
            att_dve(dve, b_groups(), fill={i: partial(merge, 0, C2_MA, k) for i, k in FILL_B.items() if k % 4 > 1})
            parts_dve(dve, 12, normed(dve, [mem_t[:, k] for k in range(KD)], g2[:, 16:24], rms_a[:, 0:N_MEM], 7),
                      [mem_hi[:, k] for k in range(KD)], [mem_lo[:, k] for k in range(KD)], [f[:, 0:N_MEM] for f in fulls2])
            branch_parts(1, C2_GB, 20)
            att_dve(dve, m_groups(), fill={i: partial(merge, 1, C2_MB, k) for i, k in FILL_M.items() if k % 4 > 1})
            branch_parts(2, C2_GM, 24)

            def merged_low(k):
                dve.wait_ge(sem("h_hi"), upto(dve, "h_hi", 28 + k + 1))
                dve.tensor_tensor(h_lo[:, k], merged[:, k], h_hi[:, k].bitcast(F32), ALU.subtract).then_inc(sem("h_lo"), tick("h_lo"))
                dve.wait_ge(sem("h_lo"), upto(dve, "h_lo"))

            for k in (2, 3, 6, 7, 10, 11):
                merge(2, C2_MM, k)
            for m in range(KD - 2):
                merged_low(m)
            for k in (14, 15):
                merge(2, C2_MM, k)
            for m in range(KD - 2, KD):
                merged_low(m)
            for k in range(1, KD):
                dve.wait_ge(sem("sq"), upto(dve, "sq", 21 + k + 1))
                dve.tensor_tensor(rms_a[:], sq_2[:, 0] if k == 1 else rms_a[:], sq_2[:, k], ALU.add).then_inc(sem("sq_sum"), tick("sq_sum"))
                dve.wait_ge(sem("sq_sum"), upto(dve, "sq_sum"))
            dve.wait_ge(sem("rms"), upto(dve, "rms", 9))
            dve.wait_ge(sem("x1"), upto(dve, "x1", KD))
            for r in range(RES):
                c = slice(r * P, r * P + P)
                dve.tensor_tensor(out_t[:, :, c], out_t[:, :, c], rms_a[:, c].unsqueeze(1).to_broadcast([P, KD, P]),
                                  ALU.mult).then_inc(sem("out_scaled"), tick("out_scaled"))
                dve.wait_ge(sem("out_scaled"), upto(dve, "out_scaled"))
                dve.tensor_tensor(out_t[:, :, c], out_t[:, :, c], x_t[:, :, c], ALU.add).then_inc(sem("out_full"), tick("out_full"))
                dve.wait_ge(sem("out_full"), upto(dve, "out_full"))
            end_layer("dve")
        return total


PER_LAYER = {
    "tab_loaded": 16, "stat": 4, "tile_done": 2 * CH_LAYER, "gate": 1, "lvl_a": 10, "kd_turned": 2, "u_sum": 2,
    "o_lin": 4, "rot": 5, "score": 16, "pt_done": 16, "pv": 16, "y_turned": 8, "log_ms": 4, "rms": 4, "h_hi": 29,
    "tile_copied": TILES_LAYER, "gk": 1, "gate_abs": 1, "gate_exp": 1, "gate_ln": 1, "decay_exp": 2,
    "lvl_abs": len(LEVELS), "lvl_exp": len(LEVELS), "sq": 5, "held_act": 5, "g_tanh": 2, "kd_t": 2, "o_copied": 4,
    "o_log": 2, "o_rms": 2, "p_exp": 16, "pt_copied": 16, "ymla_log": 1, "ymla_rms": 1, "conv0": KF, "silu": KF,
    "hid_hi": KF, "g": 2, "h_full": 13, "h_lo": 29, "reset": 2, "amat0": 1, "gate_min": 1, "gate_log": 1,
    "decay_sum": 1, "decay_rest": 1, "lvl_diff": len(LEVELS), "held_dve": 8, "lvl_kept": 9, "lvl_q": len(LEVELS),
    "lvl_k": len(LEVELS), "lin_qk": 4, "silu_g": 2, "um": 4, "state": 4, "o_sq": 2, "o_ss": 2, "o_scaled": 2,
    "y_lin": 2, "rope_cos": 5, "rope_sin": 5, "roped": 5, "masked": 16, "nmax": 16, "lvl_head": 3, "rinv": 4,
    "o_norm": 4, "ymla_sq": 4, "ymla_ss": 4, "ymla": 1, "x_mix": 8, "sq_sum": 16, "sq_tile": 15, "pad": 1,
    "conv1": KF, "conv": KF, "silu_scaled": KF, "hid_lo": KF, "sq_reset": 1, "x_down": 8, "w_split": CH_LAYER,
    "w_high": CH_LAYER, "w_loaded0": 16 * 49, "w_loaded1": 16 * 51,
}


_INS = ["x", "attn_norm", "w_in", "mla_q_norm", "mla_w_uq", "mla_kv_norm", "mla_w_ukv", "mla_out_norm", "gla_w_gate",
        "gla_b_gate", "gla_out_norm", "ret_out_norm", "w_out", "ffn_norm", "ffn_w_up", "ffn_conv_w", "ffn_conv_b",
        "ffn_w_down", "final_norm", "mem_2", "g_pre_2", "w_in_2", "b_merge_2", "q_norm_2", "k_norm_2", "g_mem_2",
        "w_mem_kv_2", "w_br_a_2", "w_br_b_2", "w_br_m_2", "w_out_2", "g_post_2"]


def kernel(**inputs):
    import numpy as _np
    import concourse.bacc as _bacc
    from concourse import mybir as _mybir
    from concourse.bass_utils import run_bass_kernel_spmd as _run

    arrays = {n: _np.ascontiguousarray(inputs[n]) for n in _INS}
    arrays.update(constants())
    nc = _bacc.Bacc("TRN2", target_bir_lowering=False, num_devices=1)
    aps = {n: nc.dram_tensor(f"in_{n}_dram", a.shape, _mybir.dt.from_np(a.dtype), kind="ExternalInput").ap()
           for n, a in arrays.items()}
    out = nc.dram_tensor("out_0_dram", (1, S, D), _mybir.dt.float32, kind="ExternalOutput").ap()
    build(nc, aps, out, PER_LAYER)
    r = _run(nc, [{f"in_{n}_dram": a for n, a in arrays.items()}], core_ids=[0])
    return r.results[0]["out_0_dram"]
```
